# Optimizing a Trainium2 kernel written in Bass

```python
import jax
import jax.numpy as jnp
from jax import lax
import numpy as np

D_MODEL = 1024
BATCH = 1
SEQ = 512
DEPTH = 2

N_MIXERS = 2
MIX_WIDTH = D_MODEL
X_WIDTH = D_MODEL // 4
N_X_HEADS = 4
X_HEAD_DIM = X_WIDTH // N_X_HEADS
SEQ_MIX_WIDTH = MIX_WIDTH - X_WIDTH
LIN_HEAD_DIM = 128
N_LIN_HEADS = SEQ_MIX_WIDTH // LIN_HEAD_DIM
CONV_WIDTH = 4
CHUNK = 64
SB_HEAD_DIM = 64
N_SB_HEADS = SEQ_MIX_WIDTH // SB_HEAD_DIM
SB_BLOCK = 128
N_MEM = 256
D_FF = 4 * D_MODEL
EPS = 1e-6
N_A_LAYERS = (DEPTH + 1) // 2
N_B_LAYERS = DEPTH // 2
IN_A = 4 * SEQ_MIX_WIDTH + 2 * N_LIN_HEADS + X_WIDTH
IN_B = 3 * SEQ_MIX_WIDTH + X_WIDTH


def rms_norm(x, g):
    xf = x.astype(jnp.float32)
    y = xf * lax.rsqrt(jnp.mean(xf * xf, axis=-1, keepdims=True) + EPS)
    return (y * g.astype(jnp.float32)).astype(x.dtype)

def l2norm(x):
    return x * lax.rsqrt(jnp.sum(x * x, axis=-1, keepdims=True) + EPS)

def causal_conv(x, w):
    c = x.shape[-1]
    return lax.conv_general_dilated(
        x, w[:, None, :].astype(x.dtype), window_strides=(1,),
        padding=[(CONV_WIDTH - 1, 0)], dimension_numbers=('NWC', 'WIO', 'NWC'),
        feature_group_count=c)

def gated_deltanet(p, conv_w, a_log, dt_bias, o_gain):
    B, S, _ = p.shape
    H, Dh, C, W = N_LIN_HEADS, LIN_HEAD_DIM, CHUNK, SEQ_MIX_WIDTH
    nc = S // C
    qkv = jax.nn.silu(causal_conv(p[..., :3 * W], conv_w)).astype(jnp.float32)
    gate = p[..., 3 * W:4 * W].astype(jnp.float32)
    beta = jax.nn.sigmoid(p[..., 4 * W:4 * W + H].astype(jnp.float32))
    g = -jnp.exp(a_log.astype(jnp.float32)) * jax.nn.softplus(
        p[..., 4 * W + H:].astype(jnp.float32) + dt_bias.astype(jnp.float32))
    q = l2norm(qkv[..., :W].reshape(B, S, H, Dh)) * (Dh ** -0.5)
    k = l2norm(qkv[..., W:2 * W].reshape(B, S, H, Dh))
    v = qkv[..., 2 * W:].reshape(B, S, H, Dh)

    def chunked(t):
        t = t.reshape((B, nc, C) + t.shape[2:])
        return jnp.moveaxis(jnp.moveaxis(t, 1, 0), 3, 2)

    q, k, v, beta = chunked(q), chunked(k), chunked(v), chunked(beta)
    gc = jnp.cumsum(chunked(g), axis=-1)
    idx = jnp.arange(C)
    causal = idx[:, None] >= idx[None, :]
    strict = idx[:, None] > idx[None, :]
    decay = jnp.exp(jnp.where(causal, gc[..., :, None] - gc[..., None, :], -jnp.inf))
    kb = k * beta[..., None]
    lower = jnp.where(strict, jnp.einsum('nbhcd,nbhsd->nbhcs', kb, k) * decay, 0.0)
    eye = jnp.eye(C, dtype=jnp.float32)
    rhs = jnp.concatenate([v * beta[..., None], kb * jnp.exp(gc)[..., None]], axis=-1)
    sol = lax.linalg.triangular_solve(eye + lower, rhs, left_side=True, lower=True,
                                      unit_diagonal=True)
    u, w = sol[..., :Dh], sol[..., Dh:]
    intra = jnp.einsum('nbhcd,nbhsd->nbhcs', q, k) * decay
    q_dec = q * jnp.exp(gc)[..., None]
    k_dec = k * jnp.exp(gc[..., -1:] - gc)[..., None]
    chunk_decay = jnp.exp(gc[..., -1])

    def step(state, inp):
        u_c, w_c, q_c, k_c, a_c, d_c = inp
        v_new = u_c - jnp.einsum('bhcd,bhde->bhce', w_c, state)
        o_c = jnp.einsum('bhcd,bhde->bhce', q_c, state) + jnp.einsum('bhcs,bhse->bhce', a_c, v_new)
        state = state * d_c[..., None, None] + jnp.einsum('bhcd,bhce->bhde', k_c, v_new)
        return state, o_c

    state0 = jnp.zeros((B, H, Dh, Dh), jnp.float32)
    _, o = lax.scan(step, state0, (u, w, q_dec, k_dec, intra, chunk_decay))
    o = jnp.swapaxes(jnp.moveaxis(o, 0, 1), 2, 3).reshape(B, S, H, Dh)
    o = o * lax.rsqrt(jnp.mean(o * o, axis=-1, keepdims=True) + EPS) * o_gain.astype(jnp.float32)
    o = o * jax.nn.silu(gate.reshape(B, S, H, Dh))
    return o.reshape(B, S, W)

def stick_breaking_attention(q, k, v):
    B, S, H, Dh = q.shape
    scale = Dh ** -0.5
    outs = []
    for blk in range(S // SB_BLOCK):
        t0 = blk * SB_BLOCK
        t1 = t0 + SB_BLOCK
        kb, vb = k[:, :t1], v[:, :t1]
        z = jnp.einsum('bthd,bshd->bhts', q[:, t0:t1], kb,
                       preferred_element_type=jnp.float32) * scale
        t_idx = t0 + jnp.arange(SB_BLOCK)[:, None]
        s_idx = jnp.arange(t1)[None, :]
        before = s_idx < t_idx
        log_beta = jax.nn.log_sigmoid(z)
        log_1m_beta = jnp.where(before, jax.nn.log_sigmoid(-z), 0.0)
        tail = lax.cumsum(log_1m_beta, axis=3, reverse=True) - log_1m_beta
        a = jnp.where(before, jnp.exp(log_beta + tail), 0.0)
        outs.append(jnp.einsum('bhts,bshd->bthd', a.astype(vb.dtype), vb))
    return jnp.concatenate(outs, axis=1).reshape(B, S, H * Dh)

def memory_attention(q, mem_kv):
    B, S, _ = q.shape
    q = q.reshape(B, S, N_X_HEADS, X_HEAD_DIM)
    k = mem_kv[..., :X_WIDTH].reshape(B, N_MEM, N_X_HEADS, X_HEAD_DIM)
    v = mem_kv[..., X_WIDTH:].reshape(B, N_MEM, N_X_HEADS, X_HEAD_DIM)
    s = jnp.einsum('bshd,bmhd->bhsm', q, k, preferred_element_type=jnp.float32) * (X_HEAD_DIM ** -0.5)
    p = jax.nn.softmax(s, axis=-1).astype(v.dtype)
    return jnp.einsum('bhsm,bmhd->bshd', p, v).reshape(B, S, X_WIDTH)

def first_inputs(seed: int = 0) -> dict:
    key = jax.random.key(seed)
    ks = jax.random.split(key, 18)
    f32 = jnp.float32
    nrm = lambda k, shape, scale: jax.random.normal(k, shape, f32) * scale
    gain = lambda k, shape: 1.0 + 0.1 * jax.random.normal(k, shape, f32)
    return {
        'x': nrm(ks[0], (BATCH, SEQ, D_MODEL), 1.0),
        'mem': nrm(ks[1], (BATCH, N_MEM, D_MODEL), 1.0),
        'mem_norm': gain(ks[2], (D_MODEL,)),
        'norm_pre_mix': gain(ks[3], (DEPTH, D_MODEL)),
        'norm_post_mix': gain(ks[4], (DEPTH, D_MODEL)),
        'norm_pre_mlp': gain(ks[5], (DEPTH, D_MODEL)),
        'norm_post_mlp': gain(ks[6], (DEPTH, D_MODEL)),
        'w_in_a': nrm(ks[7], (N_A_LAYERS, D_MODEL, IN_A), D_MODEL ** -0.5),
        'conv_w_a': nrm(ks[8], (N_A_LAYERS, CONV_WIDTH, 3 * SEQ_MIX_WIDTH), CONV_WIDTH ** -0.5),
        'a_log_a': jnp.log(jax.random.uniform(ks[9], (N_A_LAYERS, N_LIN_HEADS), f32, 0.01, 1.0)),
        'dt_bias_a': nrm(ks[10], (N_A_LAYERS, N_LIN_HEADS), 0.1),
        'onorm_a': gain(ks[11], (N_A_LAYERS, LIN_HEAD_DIM)),
        'w_in_b': nrm(ks[12], (N_B_LAYERS, D_MODEL, IN_B), D_MODEL ** -0.5),
        'w_mem_kv': nrm(ks[13], (DEPTH, D_MODEL, 2 * X_WIDTH), D_MODEL ** -0.5),
        'w_out': nrm(ks[14], (DEPTH, MIX_WIDTH, D_MODEL), MIX_WIDTH ** -0.5),
        'w_up': nrm(ks[15], (DEPTH, D_MODEL, D_FF), D_MODEL ** -0.5),
        'w_down': nrm(ks[16], (DEPTH, D_FF, D_MODEL), D_FF ** -0.5),
    }

def first_block(x, mem, mem_norm, norm_pre_mix, norm_post_mix, norm_pre_mlp, norm_post_mlp,
              w_in_a, conv_w_a, a_log_a, dt_bias_a, onorm_a, w_in_b, w_mem_kv, w_out,
              w_up, w_down):
    B, S, _ = x.shape
    mem_n = rms_norm(mem, mem_norm)
    for i in range(DEPTH):
        j = i // N_MIXERS
        h = rms_norm(x, norm_pre_mix[i])
        if i % N_MIXERS == 0:
            proj = h @ w_in_a[j]
            mix = gated_deltanet(proj[..., :IN_A - X_WIDTH], conv_w_a[j], a_log_a[j],
                                 dt_bias_a[j], onorm_a[j])
            mem_q = proj[..., IN_A - X_WIDTH:]
        else:
            proj = h @ w_in_b[j]
            W = SEQ_MIX_WIDTH
            q = proj[..., :W].reshape(B, S, N_SB_HEADS, SB_HEAD_DIM)
            k = proj[..., W:2 * W].reshape(B, S, N_SB_HEADS, SB_HEAD_DIM)
            v = proj[..., 2 * W:3 * W].reshape(B, S, N_SB_HEADS, SB_HEAD_DIM)
            mix = stick_breaking_attention(q, k, v)
            mem_q = proj[..., 3 * W:]
        cross = memory_attention(mem_q, mem_n @ w_mem_kv[i])
        y = jnp.concatenate([mix.astype(x.dtype), cross.astype(x.dtype)], axis=-1) @ w_out[i]
        x = x + rms_norm(y, norm_post_mix[i])
        h = rms_norm(x, norm_pre_mlp[i])
        y = jnp.square(jax.nn.relu(h @ w_up[i])) @ w_down[i]
        x = x + rms_norm(y, norm_post_mlp[i])
    return x


DEPTH_2 = 1

HG_HEADS = 8
HG_DK = 128
HG_DV = D_MODEL // HG_HEADS
HG_KW = HG_HEADS * HG_DK
HG_VW = HG_HEADS * HG_DV
HG_CHUNK = 32
CONV_WIDTH_2 = D_MODEL
CONV_K = 31
IN_SIZES = (HG_KW, HG_KW, HG_VW, HG_VW, CONV_WIDTH_2, CONV_WIDTH_2, D_MODEL, D_MODEL)
IN_SPLITS = tuple(int(s) for s in np.cumsum(IN_SIZES)[:-1])
N_IN = sum(IN_SIZES)
PEER_HEADS = 8
PEER_NKEYS = 128
PEER_EXPERTS = PEER_NKEYS * PEER_NKEYS
PEER_DQ = 256
PEER_TOPK = 16
PEER_BLOCK = 128


def rms_norm_2(x, g):
    xf = x.astype(jnp.float32)
    y = xf * lax.rsqrt(jnp.mean(xf * xf, axis=-1, keepdims=True) + EPS)
    return (y * g.astype(jnp.float32)).astype(x.dtype)

def layer_norm(x, g, b):
    xf = x.astype(jnp.float32)
    mu = jnp.mean(xf, axis=-1, keepdims=True)
    xc = xf - mu
    y = xc * lax.rsqrt(jnp.mean(xc * xc, axis=-1, keepdims=True) + EPS)
    return (y * g.astype(jnp.float32) + b.astype(jnp.float32)).astype(x.dtype)

def hgrn2_chunkwise(q, k, v, logf):
    B, S, H, dk = q.shape
    dv = v.shape[-1]
    n = S // HG_CHUNK

    def to_chunks(t):
        return t.reshape(B, n, HG_CHUNK, H, t.shape[-1]).transpose(1, 0, 3, 2, 4)

    causal = jnp.tril(jnp.ones((HG_CHUNK, HG_CHUNK), dtype=bool))

    def step(state, inp):
        qt, kt, vt, lt = inp
        bcum = jnp.cumsum(lt, axis=2)
        rel = bcum[:, :, :, None, :] - bcum[:, :, None, :, :]
        decay = jnp.exp(jnp.where(causal[:, :, None], rel, -jnp.inf))
        scores = jnp.einsum('bhtk,bhsk,bhtsk->bhts', qt, kt, decay)
        o = jnp.einsum('bhts,bhsv->bhtv', scores, vt)
        o = o + jnp.einsum('bhtk,bhkv->bhtv', qt * jnp.exp(bcum), state)
        blast = bcum[:, :, -1:, :]
        state = (jnp.exp(blast[:, :, 0, :])[..., None] * state
                 + jnp.einsum('bhsk,bhsv->bhkv', kt * jnp.exp(blast - bcum), vt))
        return state, o

    s0 = jnp.zeros((B, H, dk, dv), jnp.float32)
    _, o = lax.scan(step, s0, (to_chunks(q), to_chunks(k), to_chunks(v), to_chunks(logf)))
    return o.transpose(1, 0, 3, 2, 4).reshape(B, S, H, dv)

def causal_depthwise_conv(u, w, b):
    y = lax.conv_general_dilated(
        u, w[:, None, :].astype(u.dtype), window_strides=(1,),
        padding=((CONV_K - 1, 0),), dimension_numbers=('NWC', 'WIO', 'NWC'),
        feature_group_count=u.shape[-1])
    return y + b

def peer_layer(h, w_q, sub_keys, u_tab, v_tab):
    B, S, D = h.shape
    T = B * S
    hf = h.reshape(T, D)
    q = (hf @ w_q).reshape(T, PEER_HEADS, 2, PEER_DQ // 2)
    s = jnp.einsum('thpd,hpnd->thpn', q, sub_keys)
    sc, idx = lax.top_k(s, PEER_TOPK)
    cand = (sc[:, :, 0, :, None] + sc[:, :, 1, None, :]).reshape(T, PEER_HEADS, PEER_TOPK * PEER_TOPK)
    cidx = (idx[:, :, 0, :, None] * PEER_NKEYS + idx[:, :, 1, None, :]).reshape(T, PEER_HEADS, PEER_TOPK * PEER_TOPK)
    top_sc, pos = lax.top_k(cand, PEER_TOPK)
    eidx = jnp.take_along_axis(cidx, pos, axis=-1)
    gate = jax.nn.softmax(top_sc.astype(jnp.float32), axis=-1).astype(h.dtype)
    nb = T // PEER_BLOCK

    def block(args):
        hb, eb, gb = args
        act = jax.nn.gelu(jnp.einsum('thkd,td->thk', u_tab[eb], hb), approximate=False)
        return jnp.einsum('thk,thkd->td', gb * act, v_tab[eb])

    y = lax.map(block, (hf.reshape(nb, PEER_BLOCK, D),
                        eidx.reshape(nb, PEER_BLOCK, PEER_HEADS, PEER_TOPK),
                        gate.reshape(nb, PEER_BLOCK, PEER_HEADS, PEER_TOPK)))
    return y.reshape(B, S, D)

def second_inputs(seed: int = 0) -> dict:
    key = jax.random.key(seed)
    ks = jax.random.split(key, 24)
    L = DEPTH_2

    def nrm(k, shape, scale):
        return jax.random.normal(k, shape, jnp.float32) * scale

    return {
        'x': nrm(ks[0], (BATCH, SEQ, D_MODEL), 1.0),
        'c': nrm(ks[1], (BATCH, D_MODEL), 1.0),
        'ada_w': nrm(ks[2], (L, D_MODEL, 6 * D_MODEL), 0.5 * D_MODEL ** -0.5),
        'ada_b': nrm(ks[3], (L, 6 * D_MODEL), 0.02),
        'norm1_g': 1.0 + nrm(ks[4], (L, D_MODEL), 0.02),
        'w_in': nrm(ks[5], (L, D_MODEL, N_IN), D_MODEL ** -0.5),
        'lb_logits': nrm(ks[6], (L + 1, HG_KW), 0.5),
        'hg_norm_g': 1.0 + nrm(ks[7], (L, HG_VW), 0.02),
        'w_a': nrm(ks[8], (L, HG_VW, D_MODEL), HG_VW ** -0.5),
        'conv_w': nrm(ks[9], (L, CONV_K, CONV_WIDTH_2), CONV_K ** -0.5),
        'conv_b': nrm(ks[10], (L, CONV_WIDTH_2), 0.02),
        'conv_ln_g': 1.0 + nrm(ks[11], (L, CONV_WIDTH_2), 0.02),
        'conv_ln_b': nrm(ks[12], (L, CONV_WIDTH_2), 0.02),
        'w_b': nrm(ks[13], (L, CONV_WIDTH_2, D_MODEL), CONV_WIDTH_2 ** -0.5),
        'w_out': nrm(ks[14], (L, D_MODEL, D_MODEL), D_MODEL ** -0.5),
        'norm2_g': 1.0 + nrm(ks[15], (L, D_MODEL), 0.02),
        'peer_wq': nrm(ks[16], (L, D_MODEL, PEER_HEADS * PEER_DQ), D_MODEL ** -0.5),
        'peer_keys': nrm(ks[17], (L, PEER_HEADS, 2, PEER_NKEYS, PEER_DQ // 2), (PEER_DQ // 2) ** -0.5),
        'peer_u': nrm(ks[18], (L, PEER_EXPERTS, D_MODEL), D_MODEL ** -0.5),
        'peer_v': nrm(ks[19], (L, PEER_EXPERTS, D_MODEL), PEER_HEADS ** -0.5),
        'final_g': 1.0 + nrm(ks[20], (D_MODEL,), 0.02),
    }

def second_block(x, c, ada_w, ada_b, norm1_g, w_in, lb_logits, hg_norm_g, w_a, conv_w, conv_b,
              conv_ln_g, conv_ln_b, w_b, w_out, norm2_g, peer_wq, peer_keys, peer_u, peer_v,
              final_g):
    B, S, D = x.shape
    lower_bounds = jnp.cumsum(jax.nn.softmax(lb_logits.astype(jnp.float32), axis=0), axis=0)

    def heads(t):
        return t.reshape(B, S, HG_HEADS, -1)

    h = x
    for l in range(DEPTH_2):
        ada = (jax.nn.silu(c) @ ada_w[l] + ada_b[l])[:, None, :]
        sh1, sc1, g1, sh2, sc2, g2 = jnp.split(ada, 6, axis=-1)

        u = rms_norm_2(h, norm1_g[l]) * (1 + sc1) + sh1
        z = u @ w_in[l]
        zq, zf, zi, zg, zca, zcb, zga, zgb = jnp.split(z, IN_SPLITS, axis=-1)

        lb = lower_bounds[l]
        f = lb + (1.0 - lb) * jax.nn.sigmoid(zf.astype(jnp.float32))
        o = hgrn2_chunkwise(heads(zq.astype(jnp.float32)), heads(1.0 - f),
                            heads(zi.astype(jnp.float32)), heads(jnp.log(f)))
        o = rms_norm_2(o, hg_norm_g[l].reshape(HG_HEADS, HG_DV)).reshape(B, S, HG_VW).astype(x.dtype)
        y_a = (o * jax.nn.silu(zg)) @ w_a[l]

        glu = zca * jax.nn.sigmoid(zcb)
        cv = causal_depthwise_conv(glu, conv_w[l], conv_b[l])
        cv = jax.nn.silu(layer_norm(cv, conv_ln_g[l], conv_ln_b[l]))
        y_b = cv @ w_b[l]

        merged = jax.nn.sigmoid(zga) * y_a + jax.nn.sigmoid(zgb) * y_b
        h = h + g1 * (merged @ w_out[l])

        u2 = rms_norm_2(h, norm2_g[l]) * (1 + sc2) + sh2
        h = h + g2 * peer_layer(u2, peer_wq[l], peer_keys[l], peer_u[l], peer_v[l])

    return rms_norm_2(h, final_g)


def setup_inputs(seed=0):
    out = dict(first_inputs(seed))
    for name, value in second_inputs(seed + 1).items():
        if name != "x":
            out[name + "_2"] = value
    return out


def reference(
    x, mem, mem_norm, norm_pre_mix, norm_post_mix, norm_pre_mlp, norm_post_mlp, w_in_a,
    conv_w_a, a_log_a, dt_bias_a, onorm_a, w_in_b, w_mem_kv, w_out, w_up, w_down, c_2, ada_w_2,
    ada_b_2, norm1_g_2, w_in_2, lb_logits_2, hg_norm_g_2, w_a_2, conv_w_2, conv_b_2,
    conv_ln_g_2, conv_ln_b_2, w_b_2, w_out_2, norm2_g_2, peer_wq_2, peer_keys_2, peer_u_2,
    peer_v_2, final_g_2,
):
    x = first_block(
        x, mem, mem_norm, norm_pre_mix, norm_post_mix, norm_pre_mlp, norm_post_mlp, w_in_a,
        conv_w_a, a_log_a, dt_bias_a, onorm_a, w_in_b, w_mem_kv, w_out, w_up, w_down,
    )
    return second_block(
        x, c_2, ada_w_2, ada_b_2, norm1_g_2, w_in_2, lb_logits_2, hg_norm_g_2, w_a_2, conv_w_2,
        conv_b_2, conv_ln_g_2, conv_ln_b_2, w_b_2, w_out_2, norm2_g_2, peer_wq_2, peer_keys_2,
        peer_u_2, peer_v_2, final_g_2,
    )


_drawn_inputs = setup_inputs


def setup_inputs(seed=0):
    import zlib

    import numpy as np

    out = dict(_drawn_inputs(seed))
    spreads = {}
    factors = {'mem_norm': 3.521,
     'dt_bias_a': 8.0,
     'ada_b_2': 7.698,
     'norm1_g_2': 8.0,
     'lb_logits_2': 3.765,
     'hg_norm_g_2': 8.0,
     'conv_b_2': 64.0,
     'conv_ln_g_2': 64.0,
     'conv_ln_b_2': 64.0,
     'norm2_g_2': 40.023,
     'final_g_2': 7.812}
    for name, (base, spread) in spreads.items():
        noise = np.random.default_rng([zlib.crc32(name.encode()), seed]).standard_normal(out[name].shape)
        drawn = base * np.exp(spread * noise) if base else spread * noise
        out[name] = jnp.asarray(drawn.astype(out[name].dtype))
    for name, factor in factors.items():
        out[name] = (out[name] * factor).astype(out[name].dtype)
    return out
```

```python
from contextlib import ExitStack

import concourse.bass as bass
from concourse import mybir

F32 = mybir.dt.float32
U32 = mybir.dt.uint32
ALU = mybir.AluOpType
ACT = mybir.ActivationFunctionType
AX_X = mybir.AxisListType.X

P = 128
SEQ = 512
D = 1024
DT = D // P
TT = SEQ // P
DEPTH = 2
XW = D // 4
XT = XW // P
XH = 4
XD = XW // XH
MW = D - XW
MT = MW // P
LH = MW // P
SH = MW // 64
SD = 64
CONV_A = 4
NMEM = 256
FF = 4 * D
FT = FF // P
EPS = 1e-6
LEVELS = 7
HH = 8
CONV_B = 31
PH = 8
NKEY = 128
TOPK = 16
HP = 2 * PH
RING = 4
UNIT_K = 8
UNIT_N = 256
GATHER = 16


class Tile:

    def __init__(self, sem, n, bank, use):
        self.sem, self.n, self.bank, self.use = sem, n, bank, use


class Unit:

    def __init__(self, u, src, cols):
        self.u, self.slot, self.load = u, u % RING, u // RING + 1
        self.src, self.cols = src, cols


def build(nc, a, out):
    ctx = ExitStack()
    with ctx:
        def sb(name, shape, dt=F32):
            return ctx.enter_context(nc.sbuf_tensor(name, shape, dt))

        def sem(name):
            return ctx.enter_context(nc.semaphore(name))

        ring = sb("weight_ring", [P, RING, UNIT_K * UNIT_N])
        X = sb("residual", [P, DT, SEQ])
        H = sb("normed", [P, DT, SEQ])
        Y = sb("branch", [P, DT, SEQ])
        ARENA = 24960
        arena = sb("arena", [P, ARENA])
        ident = sb("ident", [P, P])
        ones = sb("ones", [P, P])
        neg_ones = sb("neg_ones", [P, P])
        neg_tri = sb("neg_tri", [P, P])
        causal = sb("causal", [P, P])
        strict = sb("strict", [P, P])
        not_before = sb("not_before", [P, P])
        zeros = sb("zeros", [P, P])
        level_mask = sb("level_mask", [P, LEVELS, P])
        VROWS = [("mem_norm", 8), ("norm_pre_mix", 16), ("norm_post_mix", 16), ("norm_pre_mlp", 16),
                 ("norm_post_mlp", 16), ("norm1_g_2", 8), ("hg_norm_g_2", 8), ("conv_b_2", 8),
                 ("conv_ln_g_2", 8), ("conv_ln_b_2", 8), ("norm2_g_2", 8), ("final_g_2", 8),
                 ("lb_logits_2", 16), ("ada_b_2", 48), ("c_2", 8), ("onorm_a", 1),
                 ("conv_w_a", 72), ("conv_w_2", 248)]
        VT = (sum(n for _, n in VROWS) + P - 1) // P
        vec = sb("vector_columns", [P, VT * P])
        ada = sb("ada", [P, 6, DT])
        c_col = sb("silu_c", [P, DT])
        lb = sb("lower_bound", [P, 2, DT])
        eps = sb("eps", [P, 1])
        tok = sb("token_scalars", [P, 6, TT * LH])
        memk = sb("mem_keys", [P, DEPTH, XT, NMEM])
        memv = sb("mem_values", [P, DEPTH, 2, XW])
        sqb = sb("squares", [P, 2, SEQ])
        rstd = sb("rstd", [P, 2, SEQ])
        small6 = sb("head_scalars", [LH, 2])
        psum = [ctx.enter_context(nc.psum_tensor(f"bank{i}", [P, 512], F32)) for i in range(8)]

        voff = {}
        at = 0
        for name, n in VROWS:
            voff[name] = at
            at += n
        VN = at

        def vcol(name, i):
            return vec[:, voff[name] + i:voff[name] + i + 1]

        def region(off, tiles, width=SEQ):
            return arena[:, off:off + tiles * width].rearrange("p (t n) -> p t n", n=width)

        landed = [sem(f"weights_landed{i}") for i in range(RING)]
        half_done = sem("half_unit_done")
        psum_full = sem("psum_full")
        bank_out = [sem(f"bank_read{i}") for i in range(8)]
        s_x = sem("x_landed")
        s_mem = sem("mem_landed")
        s_vec = sem("vectors_landed")
        s_const = sem("constants_built")
        act_chain = sem("act_step")
        dve_chain = sem("dve_step")
        pool_chain = sem("pool_step")

        count = {"aux": 0, "unit": 0}
        uses = [0] * 8
        units = []

        def aux(bank):
            count["aux"] += 1
            uses[bank] += 1
            return Tile(psum_full, count["aux"], bank, uses[bank])

        def unit(src, cols=UNIT_N):
            u = Unit(len(units), src, cols)
            units.append(u)
            return u

        def half_tile(u, half, bank):
            uses[bank] += 1
            return Tile(half_done, 2 * u.u + half + 1, bank, uses[bank])

        def k_major(w):
            return w.rearrange("(k p) n -> p k n", p=P)

        def column_units(w, first, n):
            us = [unit(k_major(w)[:, :, first + UNIT_N * j:first + UNIT_N * (j + 1)]) for j in range(n)]
            return us, [half_tile(u, h, (2 * j + h) % 4) for j, u in enumerate(us) for h in range(2)]

        x_turn = [aux(k % 4) for k in range(DT)]
        vec_turn = [aux(4 + j % 4) for j in range(VT)]
        mem_turn = [aux(k % 4) for k in range(DT)]
        norms = [aux(4)]

        kv_units, key_tiles, value_tiles = [], [], []
        for l in range(DEPTH):
            uk = unit(k_major(a["w_mem_kv"][l])[:, :, 0:XW])
            uv = unit(k_major(a["w_mem_kv"][l])[:, :, XW:2 * XW])
            kv_units.append((uk, uv))
            key_tiles.append([half_tile(uk, h, h) for h in range(2)])
            value_tiles.append([half_tile(uv, h, 2 + h) for h in range(2)])

        ADA_N = 6 * D // P
        ada_units = [unit(k_major(a["ada_w_2"][0])[:, :, UNIT_N * j:UNIT_N * (j + 1)]) for j in range(ADA_N // 2)]
        ada_tile = half_tile(ada_units[-1], 1, 5)

        def plan_cross():
            c = {"sc": [[aux(4), aux(5)]], "turn": [], "out": []}
            for x in range(XH):
                c["turn"].append([aux(6), aux(7)])
                if x + 1 < XH:
                    c["sc"].append([aux(4), aux(5)])
                c["out"].append(aux(x % 2))
            return c

        def plan_mlp(l):
            m = {"norm": aux(4)}
            up = a["w_up"][l]
            first = len(units)
            for j in range(FF // UNIT_N):
                unit(k_major(up)[:, :, UNIT_N * j:UNIT_N * (j + 1)])
            m["up"] = units[first:]
            m["up_tiles"] = [half_tile(u, h, (2 * j + h) % 4) for j, u in enumerate(m["up"]) for h in range(2)]
            down = k_major(a["w_down"][l])
            first = len(units)
            for n in range(DT):
                for kh in range(2):
                    unit(down[:, kh * 16:(kh + 1) * 16, n * P:(n + 1) * P], P)
            m["down"] = units[first:]
            m["down_tiles"] = [half_tile(m["down"][2 * n + 1], 1, n % 4) for n in range(DT)]
            m["post"] = aux(4)
            return m

        norms.append(aux(4))
        wa = a["w_in_a"][0]
        qkv_units, qkv_tiles = column_units(wa, 0, 3 * MW // UNIT_N)
        gate_units, gate_tiles = column_units(wa, 3 * MW, MW // UNIT_N)
        head_unit = unit(k_major(wa)[:, :, 4 * MW:4 * MW + 2 * LH], 2 * LH)
        head_tiles = [half_tile(head_unit, h, h) for h in range(2)]
        uses_q = unit(k_major(wa)[:, :, 4 * MW + 2 * LH:4 * MW + 2 * LH + XW])
        memq_units = [[uses_q]]
        memq_tiles = [[half_tile(uses_q, h, 2 + h) for h in range(2)]]
        l2_sums = [aux(4 + i % 4) for i in range(2 * LH)]
        tok_turn = aux(6)
        cross = [plan_cross()]
        GH = 3
        delta = []
        for g in range(LH // GH):
            d = {"prep": [[aux(4 * (j % 2) + b) for b in range(4)] for j in range(GH)], "X": [], "TX": [], "UX": []}
            for lv in range(LEVELS):
                d["X"].append([aux(2 * j) for j in range(GH)])
                tx, ux = [], []
                for j in range(GH):
                    if lv:
                        if lv < LEVELS - 1:
                            tx.append(aux(2 * j))
                        ux.append(aux(2 * j + 1))
                d["TX"].append(tx)
                d["UX"].append(ux)
            d["kturn"], d["vturn"], d["u"], d["w"] = [], [], [], []
            for j in range(GH):
                d["kturn"].append(aux(2 * j))
                d["vturn"].append(aux(2 * j + 1))
            for j in range(GH):
                d["u"].append(aux(2 * j))
                d["w"].append(aux(2 * j + 1))
            delta.append(d)
        scan = []
        for n in range(TT):
            st = {"ws": [], "o": [], "sd": []}
            if n:
                st["ws"] = [aux(g) for g in range(2)]
            for g in range(2):
                st["o"].append(aux(2 + g))
                if n < TT - 1:
                    st["sd"].append(aux(4 + g))
            scan.append(st)
        o_sums = [aux(4 + h % 4) for h in range(LH)]
        out_units, out_tiles, post = [], [], []

        def plan_out(w):
            u, t = column_units(w, 0, D // UNIT_N)
            out_units.append(u)
            out_tiles.append(t)
            post.append(aux(4))

        plan_out(a["w_out"][0])
        mlps = [plan_mlp(0)]

        norms.append(aux(4))
        wb = a["w_in_b"][0]
        sq_units, sq_tiles = column_units(wb, 0, 2 * MW // UNIT_N)
        sv_units = [unit(k_major(wb)[:, :, 2 * MW + UNIT_N * j:2 * MW + UNIT_N * (j + 1)]) for j in range(MW // UNIT_N)]
        sv_tiles = [half_tile(u, h, (2 * j + h) % 4) for j, u in enumerate(sv_units) for h in range(2)]
        ub = unit(k_major(wb)[:, :, 3 * MW:3 * MW + XW])
        memq_units.append([ub])
        memq_tiles.append([half_tile(ub, h, 2 + h) for h in range(2)])
        cross.append(plan_cross())
        stick = []
        stick.append({"z": [aux(j) for j in range(TT)]})
        for h in range(SH):
            if h + 1 < SH:
                stick.append({"z": [aux(4 * ((h + 1) % 2) + j) for j in range(TT)]})
            b = 4 * (h % 2)
            stick[h]["sum"] = [aux(b + j) for j in range(TT)]
            stick[h]["out"] = aux(b + 3)
        plan_out(a["w_out"][1])
        mlps.append(plan_mlp(1))

        norms.append(aux(4))
        w2 = a["w_in_2"][0]
        Z_Q, Z_F, Z_I, Z_G, Z_CA, Z_CB, Z_GA, Z_GB = [D * i for i in range(8)]
        glu_units, glu_tiles = [], []
        for j in range(D // UNIT_N):
            for first, b in ((Z_CA, 0), (Z_CB, 2)):
                u = unit(k_major(w2)[:, :, first + UNIT_N * j:first + UNIT_N * (j + 1)])
                glu_units.append(u)
                glu_tiles += [half_tile(u, h, b + h) for h in range(2)]
        zf_units, zf_tiles = column_units(w2, Z_F, D // UNIT_N)
        zq_units, zq_tiles = column_units(w2, Z_Q, D // UNIT_N)
        zi_units, zi_tiles = column_units(w2, Z_I, D // UNIT_N)
        zgb_units, zgb_tiles = column_units(w2, Z_GB, D // UNIT_N)
        ln_mean, ln_var = aux(5), aux(4)
        yb_units, yb_tiles = column_units(a["w_b_2"][0], 0, D // UNIT_N)
        zg_units, zg_tiles = [], []
        hg = []
        for h in range(HH):
            if h % 2 == 0:
                zg_units.append(unit(k_major(w2)[:, :, Z_G + P * h:Z_G + P * (h + 2)]))
            zg_tiles.append(half_tile(zg_units[-1], h % 2, h % 4))
            e = {"diag": aux(6)}
            if h:
                hg[h - 1]["kv"] = aux(6)
            e["lv"] = [aux(4 + lv % 2) for lv in range(LEVELS)]
            if h:
                hg[h - 1]["o"] = aux(7)
            e["kturn"], e["vturn"] = aux(6), aux(7)
            hg.append(e)
        hg[HH - 1]["kv"], hg[HH - 1]["o"] = aux(6), aux(7)
        zga_units, zga_tiles = column_units(w2, Z_GA, D // UNIT_N)
        hg_sums = [aux(4 + h % 4) for h in range(HH)]
        ya_units, ya_tiles = column_units(a["w_a_2"][0], 0, D // UNIT_N)
        wo_units, wo_tiles = column_units(a["w_out_2"][0], 0, D // UNIT_N)
        norms.append(aux(4))
        pq_units, pq_tiles = column_units(a["peer_wq_2"][0], 0, HP * P // UNIT_N)
        key_turn = [aux(4 + i) for i in range(HP // 4)]
        tok_turns = [[aux(2 * (n % 2) + i) for i in range(2)] for n in range(TT)]
        peer_scores = [[aux(4 + i) for i in range(HP // 4)] for n in range(2)]
        peer_back = []
        for n in range(TT):
            peer_back.append([aux(2 * (n % 2) + i) for i in range(2)])
            if n + 2 < TT:
                peer_scores.append([aux(4 + i) for i in range(HP // 4)])
        norms.append(aux(4))
        out_turn = [[aux(2 * (n % 2) + i) for i in range(2)] for n in range(TT)]

        q_f = region(0, LH)
        k_f = region(LH * SEQ, LH)
        v_f = region(2 * LH * SEQ, LH)
        gate_f = region(3 * LH * SEQ, LH)
        intra_f = region(4 * LH * SEQ, LH)
        kdec_f = region(5 * LH * SEQ, LH)
        memq_f = region(6 * LH * SEQ, XT)
        A_SMALL = (6 * LH + XT) * SEQ
        beta6 = arena[0:LH, A_SMALL:A_SMALL + SEQ]
        gc6 = arena[0:LH, A_SMALL + SEQ:A_SMALL + 2 * SEQ]
        spare = region(A_SMALL + 2 * SEQ, 8)
        pool512 = [Y[:, i, :] for i in range(8)] + [spare[:, i, :] for i in range(8)]
        L_t, B_t, T_t, U_t, X_t = [[pool512[5 * j + i] for j in range(GH)] for i in range(5)]
        state = Y[:, 0:2, :].rearrange("p a (h e) -> p (a h) e", e=P)
        conv_pad = Y[:, :, :].rearrange("p a n -> p (a n)")[:, 0:4 * (SEQ + CONV_A - 1)].rearrange(
            "p (i n) -> p i n", i=4)
        gtmp = [Y[0:LH, 6, :], Y[0:LH, 7, :], spare[0:LH, 4, :], spare[0:LH, 5, :]]
        prob = spare[:, 0:2, :].rearrange("p a (b m) -> p (a b) m", m=NMEM)
        prob_t = spare[:, 2:4, :]
        beta_tok = tok[:, 0, :].rearrange("p (n h) -> p n h", h=LH)
        gc_tok = tok[:, 1, :].rearrange("p (n h) -> p n h", h=LH)
        bg_tok = tok[:, 2, :].rearrange("p (n h) -> p n h", h=LH)
        kdec_tok = tok[:, 3, :].rearrange("p (h n) -> p h n", n=TT)
        chunk_decay = tok[:, 4, :].rearrange("p (h n) -> p h n", n=TT)
        soft = sb("softmax_rows", [P, 4, TT])
        mlp_f = region(0, FT)
        branch_sq = region(FT * SEQ, DT)
        sq_f = region(0, MT)
        sk_f = region(MT * SEQ, MT)
        sv_tok = arena[:, 2 * MT * SEQ:(2 * MT + LH) * SEQ].rearrange("p (t w) -> p t w", w=MW)
        S_OFF = 3 * LH * SEQ
        soft_f = region(S_OFF, 2 * TT)
        attn_f = region(S_OFF + 2 * TT * SEQ, 2 * TT)
        stick_tmp = Y[:, 0:TT, :]
        memq_of = [memq_f, memq_f]
        vec_rows = arena[:, 0:VT * P].rearrange("p (j c) -> p j c", c=P)
        mem_rows = arena[:, 1024:1024 + 2 * D].rearrange("p (t d) -> p t d", d=D)
        mem_f = region(4096, DT, NMEM)
        mem_n = H[:, :, 0:NMEM]
        x_rows = Y[:, :, :].rearrange("p a n -> p (a n)").rearrange("p (t d) -> p t d", d=D)

        PAD = CONV_B - 1
        glu = arena[:, 0:DT * (SEQ + PAD)].rearrange("p (t n) -> p t n", n=SEQ + PAD)
        yb_f = region(0, DT)
        A2 = DT * (SEQ + PAD)
        hq_f, hk_f, hb_f, hv_f = [region(A2 + i * DT * SEQ, DT) for i in range(4)]
        F2 = A2 + 4 * DT * SEQ
        hs_f = region(F2, 8)
        h_dif, h_pair, h_score = [hs_f[:, 2 * i:2 * i + 2, :] for i in range(3)]
        h_kdec, h_eb = hs_f[:, 6, :], hs_f[:, 7, :]
        h_kdt, h_state = rstd[:, 0, :], rstd[:, 1, :]
        zga_f = hb_f
        merged_f = hk_f
        mod_gain = sb("modulated_gain", [P, 2, DT])
        pq_f = region(0, HP)
        key_rows = arena[:, F2:F2 + HP * P].rearrange("p (i d) -> p i d", d=P)
        rows = arena[:, HP * SEQ:HP * SEQ + GATHER * D].rearrange("p (s d) -> p s d", d=D)
        keys_t, score_s, work_a, work_b = [ring[:, i, :] for i in range(4)]
        h_tok = Y[:, :, :].rearrange("p a n -> p (a n)").rearrange("p (t d) -> p t d", d=D)
        y_acc = H[:, :, :].rearrange("p a n -> p (a n)").rearrange("p (t d) -> p t d", d=D)
        tk = sqb[:, :, :].rearrange("p a n -> p (a n)")
        top_v = tk[:, 0:HP * TOPK].rearrange("p (i k) -> p i k", k=TOPK)
        top_i = tk[:, HP * TOPK:2 * HP * TOPK].bitcast(U32).rearrange("p (i k) -> p i k", k=TOPK)
        top_f = tk[:, 2 * HP * TOPK:3 * HP * TOPK].rearrange("p (i k) -> p i k", k=TOPK)
        NE = PH * TOPK
        best = tk[:, 3 * HP * TOPK:3 * HP * TOPK + NE].rearrange("p (h k) -> p h k", k=TOPK)
        pos_u = tk[:, 3 * HP * TOPK + NE:3 * HP * TOPK + 2 * NE].bitcast(U32).rearrange("p (h k) -> p h k", k=TOPK)
        rs = rstd[:, :, :].rearrange("p a n -> p (a n)")
        part_u, part_f = rs[:, 0:NE].bitcast(U32), rs[:, NE:2 * NE]
        e_first, e_second = rs[:, 2 * NE:3 * NE], rs[:, 3 * NE:4 * NE]
        gates = [rs[:, (4 + i) * NE:(5 + i) * NE] for i in range(2)]
        experts = [rs[:, (6 + i) * NE:(7 + i) * NE].bitcast(U32) for i in range(2)]
        expert_w = sb("expert_weight", [P, NE])
        iota16 = sb("iota16", [P, TOPK])
        iota_i = sb("iota16_int", [P, TOPK], mybir.dt.int32)
        row_ids = sb("row_ids", [P, 2, TOPK], U32)
        dots = sb("dots", [P, 2, TOPK])
        gate_pass = sb("gate_pass", [P, 1])
        gate_sum = sb("gate_sum", [P, 2, PH])

        sq_ready = sem("square_ready")
        sq_used = sem("square_summed")
        rstd_ready = sem("rstd_ready")
        norm_out = sem("normed_ready")
        x_ready = sem("residual_ready")
        conv_ready = sem("conv_ready")
        silu_ready = sem("silu_ready")
        s_small = sem("head_scalars_landed")
        gates_ready = sem("gates_ready")
        hs_ready = sem("head_square_ready")
        hr_ready = sem("head_rstd_ready")
        hn_out = sem("head_norm_ready")
        neg_max = sem("score_max_ready")
        prob_exp = sem("score_exp_ready")
        prob_ready = sem("score_prob_ready")
        cross_out = sem("cross_ready")
        eg_ready = sem("decay_row_ready")
        dexp_ready = sem("decay_ready")
        qdec_ready = sem("decayed_query_ready")
        lvl_ready = sem("level_block_ready")
        unit_ready = sem("first_inverse_ready")
        up_ready = sem("mlp_hidden_ready")
        soft_ready = sem("softplus_ready")
        attn_ready = sem("attention_ready")
        zabs_ready = sem("score_log_ready")
        mix_ready = sem("mix_ready")
        stored = sem("output_stored")
        ada_ready = sem("ada_ready")
        lb_exp = sem("bound_exp_ready")
        sig_ready = sem("conv_gate_ready")
        conv2_ready = sem("wide_conv_ready")
        mean_ready = sem("mean_ready")
        centered = sem("centered_ready")
        scaled = sem("conv_normed_ready")
        ln_out = sem("conv_branch_ready")
        forget_ready = sem("forget_ready")
        log_ready = sem("log_forget_ready")
        cum_ready = sem("cumulated_ready")
        h_sub = sem("level_difference_ready")
        h_exp = sem("level_decay_ready")
        h_pairs = sem("level_pair_ready")
        h_tail = sem("chunk_decay_ready")
        h_kd = sem("decayed_key_ready")
        h_qd = sem("hgrn_query_ready")
        merged = sem("merged_ready")
        gate2_ready = sem("output_gate_ready")
        s_keys = sem("keys_landed")
        id_ready = sem("expert_ids_ready")
        soft_in = sem("gate_logits_ready")
        soft_out = sem("gate_exp_ready")
        row_landed = [sem(f"row_landed{i}") for i in range(GATHER)]
        ids_copied = sem("row_ids_copied")
        pass_done = sem("slots_passed")
        row_free = sem("row_free")
        dots_taken = sem("dots_kept")
        w_copied = sem("expert_weights_copied")
        act_in = sem("expert_dots_ready")
        act_out = sem("expert_gelu_ready")
        y_ready = sem("expert_sum_ready")
        y_taken = sem("expert_sum_taken")
        gates_act = sem("gate_logs_ready")
        tok_exp = sem("token_decay_ready")

        def full(eng, t):
            eng.wait_ge(t.sem, t.n)

        def have(eng, t):
            eng.wait_ge(bank_out[t.bank], t.use)

        def free(pe, t):
            if t.use > 1:
                pe.wait_ge(bank_out[t.bank], t.use - 1)

        class Chain:

            def __init__(self, eng, s):
                self.eng, self.s, self.n = eng, s, 0

            def mark(self, ins):
                self.n += 1
                ins.then_inc(self.s, 1)
                return self.n

            def link(self, ins):
                self.eng.wait_ge(self.s, self.mark(ins))

            def wait(self, n):
                self.eng.wait_ge(self.s, n)

        def bc_mid(ap, n):
            return ap.unsqueeze(1).to_broadcast([ap.shape[0], n, ap.shape[1]])

        def bc_last(ap, n):
            return ap.unsqueeze(2).to_broadcast([ap.shape[0], ap.shape[1], n])

        def chunks(ap):
            return ap.rearrange("p (n c) -> p n c", c=P)

        def blk(ap, n):
            return ap[:, n * P:(n + 1) * P]

        row_src = {
            "mem_norm": a["mem_norm"].rearrange("(k p) -> k p", p=P),
            "c_2": a["c_2"].rearrange("o (k p) -> (o k) p", p=P),
            "onorm_a": a["onorm_a"], "final_g_2": a["final_g_2"].rearrange("(k p) -> k p", p=P),
            "conv_w_a": a["conv_w_a"].rearrange("o j (k p) -> (o j k) p", p=P),
            "conv_w_2": a["conv_w_2"].rearrange("o j (k p) -> (o j k) p", p=P),
        }
        for name, _ in VROWS:
            if name not in row_src:
                row_src[name] = a[name].rearrange("l (k p) -> (l k) p", p=P)
        row_parts = []
        for name, n in VROWS:
            r = 0
            while r < n:
                j, p0 = divmod(voff[name] + r, P)
                m = min(n - r, P - p0)
                row_parts.append((vec_rows[p0:p0 + m, j, :], row_src[name][r:r + m, :]))
                r += m

        block = ctx.enter_context(nc.Block())

        @block.sync
        def _(sp):
            sp.dma_start(x_rows, a["x"].rearrange("o (t p) d -> p (o t) d", p=P)).then_inc(s_x, 16)
            sp.dma_start(mem_rows, a["mem"].rearrange("o (t p) d -> p (o t) d", p=P)).then_inc(s_mem, 16)

            def load(u):
                if u.u >= RING:
                    sp.wait_ge(half_done, 2 * (u.u - RING + 1))
                sp.dma_start(ring[:, u.slot, 0:u.src.shape[1] * u.cols].rearrange("p (k n) -> p k n", n=u.cols),
                             u.src).then_inc(landed[u.slot], 16)

            def load_loop(us, per, cols, src):
                with sp.Fori(0, len(us) // per) as i:
                    for j in range(per):
                        u = us[j]
                        sp.wait_ge(half_done, i * (2 * per) + 2 * (u.u - RING + 1))
                        sp.dma_start(ring[:, u.slot, :].rearrange("p (k n) -> p k n", n=cols),
                                     src(i, j)).then_inc(landed[u.slot], 16)

            def load_mlp(l):
                up, down = k_major(a["w_up"][l]), k_major(a["w_down"][l])
                load_loop(mlps[l]["up"], 4, UNIT_N,
                          lambda i, j: up[:, :, bass.ds(i * (4 * UNIT_N) + j * UNIT_N, UNIT_N)])
                load_loop(mlps[l]["down"], 8, P,
                          lambda i, j: down[:, (j % 2) * 16:(j % 2 + 1) * 16, bass.ds(i * (4 * P) + j // 2 * P, P)])

            for u in units[:mlps[0]["up"][0].u]:
                load(u)
            load_mlp(0)
            for u in units[mlps[0]["down"][-1].u + 1:mlps[1]["up"][0].u]:
                load(u)
            load_mlp(1)
            for u in units[mlps[1]["down"][-1].u + 1:]:
                load(u)
            for t in ya_tiles:
                have(sp, t)
            sp.dma_start(key_rows, a["peer_keys_2"].rearrange("o h s n d -> n (o h s) d")).then_inc(s_keys, 16)
            for n in range(TT):
                have(sp, out_turn[n][0])
                have(sp, out_turn[n][1])
                sp.dma_start(out[0, n * P:(n + 1) * P, :], h_tok[:, n, :]).then_inc(stored, 16)
            sp.wait_ge(stored, 16 * TT)

        @block.gpsimd
        def _(pool):
            ch = Chain(pool, pool_chain)
            for t, v in ((ident, 0.0), (ones, 1.0), (neg_ones, -1.0), (neg_tri, -1.0), (causal, 1.0), (strict, 1.0),
                         (not_before, 1.0), (zeros, 0.0), (eps, EPS)):
                pool.memset(t[:], v)
            ch.link(pool.memset(level_mask[:], 0.0))

            def select(t, pattern, op, base, cm, fill):
                return pool.affine_select(out=t, in_=t, pattern=pattern, compare_op=op, fill=fill, base=base,
                                          channel_multiplier=cm)

            select(ident[:], [[-1, P]], ALU.not_equal, 0, 1, 1.0)
            select(neg_tri[:], [[-1, P]], ALU.is_ge, 0, 1, 0.0)
            select(causal[:], [[1, P]], ALU.is_ge, 0, -1, 0.0)
            select(strict[:], [[1, P]], ALU.is_gt, 0, -1, 0.0)
            ch.link(select(not_before[:], [[-1, P]], ALU.is_ge, 0, 1, 0.0))
            for lv in range(LEVELS):
                h = 1 << lv
                v = level_mask[:, lv, :].rearrange("p (b two h) -> p b two h", two=2, h=h)[:, :, 1, :]
                ch.link(pool.memset(v, 1.0))
                ch.link(select(v, [[-2 * h, P // (2 * h)], [0, h]], ALU.is_ge, 0, 1, 0.0))
                ch.link(select(v, [[2 * h, P // (2 * h)], [0, h]], ALU.is_ge, h - 1, -1, 0.0))
            ch.link(pool.iota(iota_i[:], [[1, TOPK]], base=0, channel_multiplier=0))
            pool.tensor_copy(iota16[:], iota_i[:]).then_inc(s_const, 1)
            for g, d in enumerate(delta):
                for lv in range(LEVELS):
                    for j in range(GH):
                        if lv == 0:
                            have(pool, d["prep"][j][3])
                        else:
                            full(pool, d["X"][lv - 1][j])
                            if lv == 1:
                                pool.wait_ge(unit_ready, g * GH + j + 1)
                        pool.tensor_tensor(chunks(B_t[j]), chunks(L_t[j]), bc_mid(level_mask[:, lv, :], TT),
                                           ALU.mult).then_inc(lvl_ready, 1)

            pool.wait_ge(cum_ready, 1)
            for h in range(HH):
                for lv in range(LEVELS):
                    half = 1 << lv
                    b = hb_f[:, h, :].rearrange("p (n w) -> p n w", w=2 * half)
                    dif = h_dif[:, lv % 2, :].rearrange("p (n w) -> p n w", w=2 * half)
                    r = h * LEVELS + lv
                    if lv >= 2 or h:
                        pool.wait_ge(h_pairs, r - 1 if lv >= 2 else h * LEVELS)
                    mid = b[:, :, half - 1:half].to_broadcast([P, SEQ // (2 * half), half])
                    pool.tensor_tensor(dif[:, :, 0:half], mid, b[:, :, 0:half], ALU.subtract)
                    pool.tensor_tensor(dif[:, :, half:], b[:, :, half:], mid, ALU.subtract).then_inc(h_sub, 1)
                if h:
                    full(pool, hg[h - 1]["kturn"])
                pool.tensor_tensor(chunks(h_kdec), chunks(hb_f[:, h, :])[:, :, P - 1:P].to_broadcast([P, TT, P]),
                                   chunks(hb_f[:, h, :]), ALU.subtract).then_inc(h_sub, 1)

            pool.memset(gate_pass[:], 0.0).then_inc(pass_done, 1)
            phase = 0
            for n in range(TT):
                for table in (a["peer_u_2"][0], a["peer_v_2"][0]):
                    pool.wait_ge(id_ready, n + 1)
                    with pool.Fori(0, PH // 2) as i:
                        for half in range(2):
                            ch2 = pool.tensor_copy(row_ids[:, half, :],
                                                   experts[n % 2][:, bass.ds(i * (2 * TOPK) + half * TOPK, TOPK)])
                            ch2.then_inc(ids_copied, 1)
                            for k in range(TOPK):
                                if k % 4 == 0:
                                    if k == 0:
                                        pool.wait_ge(ids_copied, i * 2 + (phase * PH + half + 1))
                                    pool.wait_ge(row_free, i * (2 * TOPK) + (phase * NE + half * TOPK + k + 4))
                                    pool.wait_ge(pass_done, i * 8 + (phase * 4 * PH + half * 4 + k // 4 + 1))
                                    pool.tensor_tensor(gate_pass[:], zeros[:, 0:1], zeros[:, 0:1], ALU.add).then_inc(
                                        pass_done, 1)
                                pool.indirect_dma_start(rows[:, k, :], None, table,
                                                        bass.IndirectOffsetOnAxis(ap=row_ids[:, half, k:k + 1], axis=0)
                                                        ).then_inc(row_landed[k], 16)
                    phase += 1

        @block.tensor
        def _(pe):
            nrm = [0]

            def norm_sum(t, width=SEQ, sq=None):
                i = nrm[0]
                nrm[0] += 1
                free(pe, t)
                for k in range(DT):
                    pe.wait_ge(sq_ready, DT * i + k + 1)
                    m = pe.matmul(psum[t.bank][:, 0:width], ones[:], sq[:, k, :] if sq is not None else
                                  sqb[:, k % 2, 0:width], start=k == 0, stop=k == DT - 1)
                    if k < DT - 1:
                        m.then_inc(sq_used, 1)
                    else:
                        m.then_inc(psum_full, 1)

            def block_of(u, k, c, n=P):
                return ring[:, u.slot, k * u.cols + c:k * u.cols + c + n]

            def project(us, tiles, rhs, width=SEQ, ready=None):
                for j, u in enumerate(us):
                    pe.wait_ge(landed[u.slot], 16 * u.load)
                    for h in range(2):
                        t = tiles[2 * j + h]
                        free(pe, t)
                        for k in range(DT):
                            if ready and j == 0 and h == 0:
                                ready(k)
                            m = pe.matmul(psum[t.bank][:, 0:width], block_of(u, k, h * P), rhs[:, k, :],
                                          start=k == 0, stop=k == DT - 1)
                        m.then_inc(half_done, 1)

            pre = [0]

            def normed(k):
                pe.wait_ge(norm_out, DT * pre[0] + k + 1)

            def turn(t, parts):
                free(pe, t)
                at = 0
                for src in parts:
                    r, c = src.shape
                    m = pe.transpose(psum[t.bank][0:c, at:at + r], src, ident[0:r, 0:r])
                    at += r
                m.then_inc(psum_full, 1)

            def cross_attention(l):
                c = cross[l]
                q, kk, vv = memq_of[l], memk[:, l], memv[:, l]

                def scores(x):
                    r = slice((x % 2) * XD, (x % 2) * XD + XD)
                    for b in range(2):
                        t = c["sc"][x][b]
                        free(pe, t)
                        for n in range(2):
                            m = pe.matmul(psum[t.bank][:, n * NMEM:(n + 1) * NMEM],
                                          q[r, x // 2, (2 * b + n) * P:(2 * b + n + 1) * P], kk[r, x // 2, :],
                                          start=True, stop=True)
                        m.then_inc(psum_full, 1)

                for t in memq_tiles[l]:
                    have(pe, t)
                scores(0)
                for x in range(XH):
                    pe.wait_ge(prob_ready, XH * l + x + 1)
                    for mt in range(2):
                        turn(c["turn"][x][mt], [prob[:, n, mt * P:(mt + 1) * P] for n in range(TT)])
                    if x + 1 < XH:
                        scores(x + 1)
                    t = c["out"][x]
                    free(pe, t)
                    r0 = (x % 2) * XD
                    for mt in range(2):
                        have(pe, c["turn"][x][mt])
                        m = pe.matmul(psum[t.bank][r0:r0 + XD, :], vv[:, mt, x * XD:(x + 1) * XD], prob_t[:, mt, :],
                                      start=mt == 0, stop=mt == 1)
                    m.then_inc(psum_full, 1)

            def head_sums(tiles, base):
                for i, t in enumerate(tiles):
                    free(pe, t)
                    pe.wait_ge(hs_ready, base + i + 1)
                    pe.matmul(psum[t.bank][:], ones[:], sqb[:, i % 2, :], start=True, stop=True).then_inc(psum_full, 1)

            def mlp(l):
                m = mlps[l]
                with pe.Fori(0, len(m["up"]) // 4) as i:
                    for j in range(4):
                        u = m["up"][j]
                        pe.wait_ge(landed[u.slot], i * 16 + 16 * u.load)
                        for h in range(2):
                            t = m["up_tiles"][2 * j + h]
                            pe.wait_ge(bank_out[t.bank], i * 2 + (t.use - 1))
                            for k in range(DT):
                                if j == 0 and h == 0:
                                    normed(k)
                                mm = pe.matmul(psum[t.bank][:], block_of(u, k, h * P), H[:, k, :], start=k == 0,
                                               stop=k == DT - 1)
                            mm.then_inc(half_done, 1)
                with pe.Fori(0, 2) as i:
                    for j in range(8):
                        u = m["down"][j]
                        t = m["down_tiles"][j // 2]
                        pe.wait_ge(landed[u.slot], i * 32 + 16 * u.load)
                        if j % 2 == 0:
                            pe.wait_ge(bank_out[t.bank], i + (t.use - 1))
                        pe.wait_ge(up_ready, FT * l + 16 * (j % 2 + 1))
                        for k in range(16):
                            mm = pe.matmul(psum[t.bank][:], block_of(u, k, 0), mlp_f[:, 16 * (j % 2) + k, :],
                                           start=j % 2 == 0 and k == 0, stop=j % 2 == 1 and k == 15)
                            if k % 8 == 7:
                                mm.then_inc(half_done, 1)
                pre[0] += 1
                norm_sum(m["post"], sq=branch_sq)

            pe.wait_ge(s_const, 1)
            pe.wait_ge(s_x, 16)
            for k in range(DT):
                turn(x_turn[k], [x_rows[:, n, k * P:(k + 1) * P] for n in range(TT)])
            pe.wait_ge(s_vec, 16 * len(row_parts))
            for j in range(VT):
                r = min(P, VN - j * P)
                turn(vec_turn[j], [vec_rows[0:r, j, :]])
            pe.wait_ge(s_mem, 16)
            for k in range(DT):
                turn(mem_turn[k], [mem_rows[:, n, k * P:(k + 1) * P] for n in range(2)])
            norm_sum(norms[0], NMEM)
            for l in range(DEPTH):
                uk, uv = kv_units[l]
                project([uk], key_tiles[l], mem_n, NMEM, normed if l == 0 else None)
                pe.wait_ge(landed[uv.slot], 16 * uv.load)
                for n in range(2):
                    t = value_tiles[l][n]
                    free(pe, t)
                    for k in range(DT):
                        m = pe.matmul(psum[t.bank][:, 0:XW], mem_n[:, k, n * P:(n + 1) * P], block_of(uv, k, 0, XW),
                                      start=k == 0, stop=k == DT - 1)
                    m.then_inc(half_done, 1)
            pre[0] += 1
            pe.wait_ge(ada_ready, 1)
            free(pe, ada_tile)
            for j, u in enumerate(ada_units):
                pe.wait_ge(landed[u.slot], 16 * u.load)
                for h in range(2):
                    for k in range(DT):
                        m = pe.matmul(psum[ada_tile.bank][:, 2 * j + h:2 * j + h + 1], block_of(u, k, h * P),
                                      c_col[:, k:k + 1], start=k == 0, stop=k == DT - 1)
                    m.then_inc(half_done, 1)

            norm_sum(norms[1])
            project(qkv_units, qkv_tiles, H, ready=normed)
            project(gate_units, gate_tiles, H)
            pe.wait_ge(landed[head_unit.slot], 16 * head_unit.load)
            for h, t in enumerate(head_tiles):
                free(pe, t)
                for k in range(DT):
                    m = pe.matmul(psum[t.bank][0:LH, :], block_of(head_unit, k, h * LH, LH), H[:, k, :], start=k == 0,
                                  stop=k == DT - 1)
                m.then_inc(half_done, 1)
            project(memq_units[0], memq_tiles[0], H)
            pre[0] += 1
            head_sums(l2_sums, 0)
            pe.wait_ge(gates_ready, 1)
            turn(tok_turn, [blk(beta6, n) for n in range(TT)] + [blk(gc6, n) for n in range(TT)])
            cross_attention(0)
            for g, d in enumerate(delta):
                heads = range(g * GH, (g + 1) * GH)
                for j, h in enumerate(heads):
                    gb, kk, qk, bb = d["prep"][j]
                    free(pe, gb)
                    pe.matmul(psum[gb.bank][:], ident[0:LH, h:h + 1].to_broadcast([LH, P]), gc6, start=True,
                              stop=True).then_inc(psum_full, 1)
                    if j == 0 and g == 0:
                        pe.wait_ge(hn_out, 2 * LH)
                    for t, rhs in ((kk, k_f), (qk, q_f)):
                        free(pe, t)
                        for n in range(TT):
                            m = pe.matmul(blk(psum[t.bank], n), blk(k_f[:, h, :], n), blk(rhs[:, h, :], n), start=True,
                                          stop=True)
                        m.then_inc(psum_full, 1)
                    free(pe, bb)
                    pe.matmul(psum[bb.bank][:], ident[0:LH, h:h + 1].to_broadcast([LH, P]), beta6, start=True,
                              stop=True).then_inc(psum_full, 1)
                for lv in range(LEVELS):
                    for j in range(GH):
                        t = d["X"][lv][j]
                        free(pe, t)
                        pe.wait_ge(lvl_ready, (g * LEVELS + lv) * GH + j + 1)
                        for n in range(TT):
                            m = pe.matmul(blk(psum[t.bank], n), blk(B_t[j], n), blk(T_t[j], n) if lv else ident[:],
                                          start=True, stop=True)
                        m.then_inc(psum_full, 1)
                    if not lv:
                        continue
                    for j in range(GH):
                        t = d["UX"][lv][j]
                        if lv == 1:
                            pe.wait_ge(unit_ready, g * GH + j + 1)
                        free(pe, t)
                        have(pe, d["X"][lv][j])
                        if lv < LEVELS - 1:
                            tx = d["TX"][lv][j]
                            for n in range(TT):
                                m = pe.matmul(blk(psum[tx.bank], n), blk(U_t[j], n), blk(X_t[j], n), start=True, stop=True)
                            m.then_inc(psum_full, 1)
                        for n in range(TT):
                            m = pe.matmul(blk(psum[t.bank], n), blk(X_t[j], n), blk(U_t[j], n), start=True, stop=True)
                        m.then_inc(psum_full, 1)
                for j, h in enumerate(heads):
                    turn(d["kturn"][j], [blk(k_f[:, h, :], n) for n in range(TT)])
                    turn(d["vturn"][j], [blk(v_f[:, h, :], n) for n in range(TT)])
                for j, h in enumerate(heads):
                    t = d["u"][j]
                    free(pe, t)
                    have(pe, d["UX"][LEVELS - 1][j])
                    have(pe, d["vturn"][j])
                    for n in range(TT):
                        m = pe.matmul(blk(psum[t.bank], n), blk(U_t[j], n), blk(L_t[j], n), start=True, stop=True)
                    m.then_inc(psum_full, 1)
                    t = d["w"][j]
                    free(pe, t)
                    have(pe, d["kturn"][j])
                    for n in range(TT):
                        m = pe.matmul(blk(psum[t.bank], n), blk(B_t[j], n), blk(U_t[j], n), start=True, stop=True)
                    m.then_inc(psum_full, 1)
            for t in delta[0]["u"] + delta[0]["w"] + delta[1]["u"] + delta[1]["w"]:
                have(pe, t)
            pe.wait_ge(qdec_ready, LH)
            for n, st in enumerate(scan):
                for g in range(2):
                    if n:
                        t = st["ws"][g]
                        have(pe, scan[n - 1]["sd"][g])
                        free(pe, t)
                        for j in range(GH):
                            h = g * GH + j
                            m = pe.matmul(blk(psum[t.bank], j), blk(k_f[:, h, :], n), state[:, h, :], start=True, stop=True)
                        m.then_inc(psum_full, 1)
                for g in range(2):
                    if n:
                        have(pe, st["ws"][g])
                    t = st["o"][g]
                    free(pe, t)
                    for j in range(GH):
                        h = g * GH + j
                        if n:
                            pe.matmul(blk(psum[t.bank], j), state[:, h, :], blk(q_f[:, h, :], n), start=True, stop=False)
                        m = pe.matmul(blk(psum[t.bank], j), blk(v_f[:, h, :], n), blk(intra_f[:, h, :], n), start=n == 0,
                                      stop=True)
                    m.then_inc(psum_full, 1)
                    if n < TT - 1:
                        t = st["sd"][g]
                        free(pe, t)
                        for j in range(GH):
                            h = g * GH + j
                            m = pe.matmul(blk(psum[t.bank], j), blk(kdec_f[:, h, :], n), blk(v_f[:, h, :], n), start=True,
                                          stop=True)
                        m.then_inc(psum_full, 1)
            head_sums(o_sums, 2 * LH)

            def mixed(l):
                def ready(k):
                    if k < MT:
                        if l == 0:
                            pe.wait_ge(mix_ready, k + 1)
                        else:
                            for h in (2 * k, 2 * k + 1):
                                have(pe, stick[h]["out"])
                    else:
                        for x in (2 * (k - MT), 2 * (k - MT) + 1):
                            have(pe, cross[l]["out"][x])
                return ready

            project(out_units[0], out_tiles[0], H, ready=mixed(0))
            norm_sum(post[0], sq=branch_sq)
            norm_sum(mlps[0]["norm"])
            mlp(0)

            norm_sum(norms[2])
            project(sq_units, sq_tiles, H, ready=normed)
            for j, u in enumerate(sv_units):
                pe.wait_ge(landed[u.slot], 16 * u.load)
                for h in range(2):
                    t = sv_tiles[2 * j + h]
                    free(pe, t)
                    for n in range(2):
                        for k in range(DT):
                            m = pe.matmul(psum[t.bank][:, n * UNIT_N:(n + 1) * UNIT_N], blk(H[:, k, :], 2 * h + n),
                                          block_of(u, k, 0, UNIT_N), start=k == 0, stop=k == DT - 1)
                    m.then_inc(half_done, 1)
            project(memq_units[1], memq_tiles[1], H)
            pre[0] += 1
            cross_attention(1)

            def stick_scores(h):
                r = slice((h % 2) * SD, (h % 2) * SD + SD)
                for j, t in enumerate(stick[h]["z"]):
                    free(pe, t)
                    pe.matmul(psum[t.bank][:, j * P:], blk(sk_f[r, h // 2, :], j), sq_f[r, h // 2, j * P:], start=True,
                              stop=True, skip_group_check=True).then_inc(psum_full, 1)

            for t in sq_tiles + sv_tiles:
                have(pe, t)
            stick_scores(0)
            for h in range(SH):
                if h + 1 < SH:
                    stick_scores(h + 1)
                sp_h, at_h = soft_f[:, TT * (h % 2):TT * (h % 2) + TT, :], attn_f[:, TT * (h % 2):TT * (h % 2) + TT, :]
                for j, t in enumerate(stick[h]["sum"]):
                    pe.wait_ge(soft_ready, TT * (h + 1))
                    free(pe, t)
                    for i in range(j, TT):
                        m = pe.matmul(psum[t.bank][:, i * P:], neg_tri[:] if i == j else neg_ones[:], sp_h[:, i, i * P:],
                                      start=False, stop=i == TT - 1, skip_group_check=True)
                    m.then_inc(psum_full, 1)
                t = stick[h]["out"]
                free(pe, t)
                pe.wait_ge(attn_ready, TT * (h + 1))
                r0 = (h % 2) * SD
                for j in range(TT):
                    m = pe.matmul(psum[t.bank][r0:r0 + SD, j * P:], sv_tok[:, j, h * SD:(h + 1) * SD], at_h[:, j, j * P:],
                                  start=j == 0, stop=j == TT - 1, skip_group_check=True)
                m.then_inc(psum_full, 1)
            project(out_units[1], out_tiles[1], H, ready=mixed(1))
            norm_sum(post[1], sq=branch_sq)
            norm_sum(mlps[1]["norm"])
            mlp(1)

            norm_sum(norms[3])
            project(glu_units, glu_tiles, H, ready=normed)
            project(zf_units, zf_tiles, H)
            project(zq_units, zq_tiles, H)
            project(zi_units, zi_tiles, H)
            project(zgb_units, zgb_tiles, H)
            free(pe, ln_mean)
            for k in range(DT):
                pe.wait_ge(conv2_ready, k + 1)
                m = pe.matmul(psum[ln_mean.bank][:], ones[:], Y[:, k, :], start=k == 0, stop=k == DT - 1)
            m.then_inc(psum_full, 1)
            norm_sum(ln_var)
            project(yb_units, yb_tiles, Y, ready=lambda k: pe.wait_ge(ln_out, k + 1))

            def hgrn_kv(h):
                t = hg[h]["kv"]
                free(pe, t)
                have(pe, hg[h]["kturn"])
                have(pe, hg[h]["vturn"])
                for n in range(TT - 1):
                    m = pe.matmul(blk(psum[t.bank], n), blk(h_kdt, n), blk(hv_f[:, h, :], n), start=True, stop=True)
                m.then_inc(psum_full, 1)

            def hgrn_out(h):
                t = hg[h]["o"]
                free(pe, t)
                pe.wait_ge(h_qd, h + 1)
                have(pe, hg[h]["kv"])
                have(pe, hg[h]["lv"][LEVELS - 1])
                for n in range(TT):
                    if n:
                        pe.matmul(blk(psum[t.bank], n), blk(h_state, n - 1), blk(hq_f[:, h, :], n), start=True, stop=False)
                    m = pe.matmul(blk(psum[t.bank], n), blk(hv_f[:, h, :], n), blk(h_score[:, h % 2, :], n), start=n == 0,
                                  stop=True)
                m.then_inc(psum_full, 1)

            for t in zq_tiles + zi_tiles:
                have(pe, t)
            pe.wait_ge(cum_ready, 1)
            for h in range(HH):
                u, t = zg_units[h // 2], zg_tiles[h]
                pe.wait_ge(landed[u.slot], 16 * u.load)
                free(pe, t)
                for k in range(DT):
                    m = pe.matmul(psum[t.bank][:], block_of(u, k, (h % 2) * P), H[:, k, :], start=k == 0, stop=k == DT - 1)
                m.then_inc(half_done, 1)
                t = hg[h]["diag"]
                free(pe, t)
                for n in range(TT):
                    m = pe.matmul(blk(psum[t.bank], n), blk(hk_f[:, h, :], n), blk(hq_f[:, h, :], n), start=True, stop=True)
                m.then_inc(psum_full, 1)
                if h:
                    hgrn_kv(h - 1)
                for lv in range(LEVELS):
                    t = hg[h]["lv"][lv]
                    free(pe, t)
                    pe.wait_ge(h_pairs, h * LEVELS + lv + 1)
                    for n in range(TT):
                        p = blk(h_pair[:, lv % 2, :], n)
                        m = pe.matmul(blk(psum[t.bank], n), p, p, start=True, stop=True)
                    m.then_inc(psum_full, 1)
                if h:
                    hgrn_out(h - 1)
                pe.wait_ge(h_kd, h + 1)
                turn(hg[h]["kturn"], [blk(h_kdec, n) for n in range(TT)])
                turn(hg[h]["vturn"], [blk(hv_f[:, h, :], n) for n in range(TT)])
            hgrn_kv(HH - 1)
            hgrn_out(HH - 1)
            project(zga_units, zga_tiles, H)
            pre[0] += 1
            head_sums(hg_sums, 3 * LH)
            project(ya_units, ya_tiles, hq_f, ready=lambda k: pe.wait_ge(mix_ready, LH + k + 1))
            project(wo_units, wo_tiles, merged_f, ready=lambda k: pe.wait_ge(merged, k + 1))

            norm_sum(norms[4])
            project(pq_units, pq_tiles, H, ready=normed)
            pre[0] += 1
            pe.wait_ge(s_keys, 16)
            for i, t in enumerate(key_turn):
                turn(t, [key_rows[:, 4 * i + j, :] for j in range(4)])
            for n in range(TT):
                for i in range(2):
                    turn(tok_turns[n][i], [blk(H[:, 4 * i + j, :], n) for j in range(4)])
            for t in key_turn + pq_tiles:
                have(pe, t)

            def key_scores(n):
                for i, t in enumerate(peer_scores[n]):
                    free(pe, t)
                    for j in range(4):
                        m = pe.matmul(blk(psum[t.bank], j), blk(pq_f[:, 4 * i + j, :], n), blk(keys_t, 4 * i + j), start=True,
                                      stop=True)
                    m.then_inc(psum_full, 1)

            for n in range(2):
                key_scores(n)
            for n in range(TT):
                pe.wait_ge(y_ready, n + 1)
                for i in range(2):
                    turn(peer_back[n][i], [y_acc[:, 0, (4 * i + j) * P:(4 * i + j + 1) * P] for j in range(4)])
                if n + 2 < TT:
                    key_scores(n + 2)
            norm_sum(norms[5])
            for n in range(TT):
                for i in range(2):
                    for j in range(4):
                        if n == 0:
                            normed(4 * i + j)
                    turn(out_turn[n][i], [blk(H[:, 4 * i + j, :], n) for j in range(4)])

        @block.scalar
        def _(act):
            ch = Chain(act, act_chain)
            for dst, src in row_parts:
                act.dma_start(dst, src).then_inc(s_vec, 16)
            act.dma_start(small6[:, 0:1], a["dt_bias_a"].rearrange("o h -> h o")).then_inc(s_small, 16)
            act.dma_start(small6[:, 1:2], a["a_log_a"].rearrange("o h -> h o")).then_inc(s_small, 16)
            nrm = [0]

            def log_exp_table():
                act.preload_act_table_set("natural_log_exp_and_others")

            def norm_scale(t, src, ready, width=SEQ, scale=1.0 / D, sq=None):
                i = nrm[0]
                nrm[0] += 1
                for k in range(DT):
                    ready(act, k)
                    if k >= 2 and sq is None:
                        act.wait_ge(sq_used, (DT - 1) * i + k - 1)
                    act.activation(sqb[:, k % 2, 0:width] if sq is None else sq[:, k, :], src[:, k, :],
                                   ACT.Square).then_inc(sq_ready, 1)
                full(act, t)
                act.activation(rstd[:, 0, 0:width], psum[t.bank][:, 0:width], ACT.Ln, bias=eps[:, 0:1],
                               scale=scale).then_inc(bank_out[t.bank], 1)
                have(act, t)
                act.activation(rstd[:, 0, 0:width], rstd[:, 0, 0:width], ACT.Exp, scale=-0.5).then_inc(rstd_ready, 1)

            def head_scale(tiles, base, src, scale, ready=None, tail=None):
                def finish(i):
                    t = tiles[i]
                    full(act, t)
                    if i >= 2:
                        act.wait_ge(hn_out, base + i - 1)
                    act.activation(rstd[:, i % 2, :], psum[t.bank][:], ACT.Ln, bias=eps[:, 0:1],
                                   scale=scale).then_inc(bank_out[t.bank], 1)
                    have(act, t)
                    act.activation(rstd[:, i % 2, :], rstd[:, i % 2, :], ACT.Exp, scale=-0.5).then_inc(hr_ready, 1)

                for i in range(len(tiles)):
                    if ready:
                        ready(i)
                    act.activation(sqb[:, i % 2, :], src[:, i, :], ACT.Square).then_inc(hs_ready, 1)
                    if i:
                        finish(i - 1)
                finish(len(tiles) - 1)

            def take(t, dst, func=ACT.Copy, width=SEQ, rows=slice(0, P)):
                full(act, t)
                act.activation(dst, psum[t.bank][rows, 0:width], func).then_inc(bank_out[t.bank], 1)

            def cross_attention(l):
                c = cross[l]
                log_exp_table()
                for x in range(XH):
                    for b in range(2):
                        t = c["sc"][x][b]
                        act.wait_ge(neg_max, 2 * (XH * l + x) + b + 1)
                        for n in range(2):
                            m = act.activation(prob[:, 2 * b + n, :], psum[t.bank][:, n * NMEM:(n + 1) * NMEM], ACT.Exp,
                                               bias=soft[:, 0, 2 * b + n:2 * b + n + 1], scale=XD ** -0.5,
                                               accum_out=soft[:, 1, 2 * b + n:2 * b + n + 1])
                        m.then_inc(bank_out[t.bank], 1)
                    take(c["turn"][x][0], prob_t[:, 0, :])

            def branch_out(tiles, t):
                def ready(eng, k):
                    take(tiles[k], Y[:, k, :])
                    have(act, tiles[k])
                norm_scale(t, Y, ready, sq=branch_sq)

            def mlp(l):
                m = mlps[l]
                for j, t in enumerate(m["up_tiles"]):
                    take(t, mlp_f[:, j, :], ACT.Relu)
                    have(act, t)
                    act.activation(mlp_f[:, j, :], mlp_f[:, j, :], ACT.Square).then_inc(up_ready, 1)
                branch_out(m["down_tiles"], m["post"])

            upd = [0]

            def residual(eng, k):
                eng.wait_ge(x_ready, DT * (upd[0] - 1) + k + 1)

            act.wait_ge(s_const, 1)
            log_exp_table()
            norm_scale(norms[0], mem_f, lambda eng, k: have(eng, mem_turn[k]), NMEM)
            have(act, vec_turn[VT - 1])
            for t in vec_turn:
                have(act, t)
            c0 = voff["c_2"]
            act.activation(c_col[:], vec[:, c0:c0 + DT], ACT.Silu).then_inc(ada_ready, 1)
            for l in range(DEPTH):
                for h in range(2):
                    take(key_tiles[l][h], memk[:, l, h, :], width=NMEM)
                for h in range(2):
                    take(value_tiles[l][h], memv[:, l, h, :], width=XW)

            log_exp_table()
            norm_scale(norms[1], X, lambda eng, k: have(eng, x_turn[k]))
            qkv = [q_f[:, i, :] for i in range(LH)] + [k_f[:, i, :] for i in range(LH)] + [v_f[:, i, :] for i in range(LH)]

            def silu(i):
                act.wait_ge(conv_ready, i + 1)
                act.activation(qkv[i], qkv[i], ACT.Silu).then_inc(silu_ready, 1)

            for i, t in enumerate(qkv_tiles):
                if i >= 4:
                    act.wait_ge(conv_ready, i - 3)
                take(t, conv_pad[:, i % 4, CONV_A - 1:])
                if i:
                    silu(i - 1)
            silu(3 * LH - 1)
            for h, t in enumerate(gate_tiles):
                take(t, gate_f[:, h, :], ACT.Silu)
            tb, tg = head_tiles
            take(tb, beta6, ACT.Sigmoid, rows=slice(0, LH))
            act.wait_ge(s_small, 32)
            full(act, tg)
            ch.link(act.activation(gtmp[0], psum[tg.bank][0:LH, :], ACT.Abs, bias=small6[:, 0:1]))
            log_exp_table()
            ch.link(act.activation(small6[:, 1:2], small6[:, 1:2], ACT.Exp))
            ch.link(act.activation(gtmp[0], gtmp[0], ACT.Exp, scale=-1.0))
            act.activation(gtmp[0], gtmp[0], ACT.Ln, bias=1.0).then_inc(gates_act, 1)
            for t, dst in zip(memq_tiles[0], (memq_f[:, 0, :], memq_f[:, 1, :])):
                take(t, dst)
            act.wait_ge(silu_ready, 2 * LH)
            head_scale(l2_sums, 0, arena[:, 0:2 * LH * SEQ].rearrange("p (t n) -> p t n", n=SEQ), 1.0)
            have(act, tok_turn)
            act.activation(tok[:, 2, :], tok[:, 1, :], ACT.Exp).then_inc(tok_exp, 1)
            cross_attention(0)
            have(act, cross[0]["out"][XH - 1])
            for g, d in enumerate(delta):
                for j in range(GH):
                    gb = d["prep"][j][0]
                    full(act, gb)
                    act.activation(T_t[j], psum[gb.bank][:], ACT.Exp).then_inc(eg_ready, 1)
                    have(act, gb)
                    act.activation(kdec_tok[:, g * GH + j, :], kdec_tok[:, g * GH + j, :], ACT.Exp)
                    act.activation(U_t[j], U_t[j], ACT.Exp).then_inc(dexp_ready, 1)
                for lv in range(1, LEVELS):
                    for j in range(GH):
                        take(d["X"][lv][j], X_t[j])
                for j in range(GH):
                    take(d["u"][j], v_f[:, g * GH + j, :])
            for n, st in enumerate(scan):
                for g in range(2):
                    t = st["o"][g]
                    full(act, t)
                    act.activation(q_f[:, g * GH:(g + 1) * GH, n * P:(n + 1) * P], psum[t.bank][:, 0:GH * P].rearrange(
                        "p (h c) -> p h c", c=P), ACT.Copy).then_inc(bank_out[t.bank], 1)
            head_scale(o_sums, 2 * LH, q_f, 1.0 / P, lambda i: have(act, scan[TT - 1]["o"][i // GH]))
            branch_out(out_tiles[0], post[0])
            upd[0] += 1
            norm_scale(mlps[0]["norm"], X, residual)
            mlp(0)
            upd[0] += 1

            norm_scale(norms[2], X, residual)
            for i, t in enumerate(sq_tiles):
                full(act, t)
                dst, s = (sq_f[:, i, :], SD ** -0.5) if i < MT else (sk_f[:, i - MT, :], 1.0)
                act.activation(dst, psum[t.bank][:], ACT.Copy, scale=s).then_inc(bank_out[t.bank], 1)
            for i, t in enumerate(sv_tiles):
                full(act, t)
                j, h = divmod(i, 2)
                act.activation(sv_tok[:, 2 * h:2 * h + 2, j * UNIT_N:(j + 1) * UNIT_N],
                               psum[t.bank][:].rearrange("p (t w) -> p t w", w=UNIT_N), ACT.Copy).then_inc(bank_out[t.bank], 1)
            for t, dst in zip(memq_tiles[1], (memq_f[:, 0, :], memq_f[:, 1, :])):
                take(t, dst)
            cross_attention(1)

            def logs(h):
                for j, t in enumerate(stick[h]["z"]):
                    full(act, t)
                    if h:
                        act.wait_ge(soft_ready, TT * (h - 1) + j + 1)
                    w = stick_tmp[:, j, j * P:]
                    ch.mark(act.activation(w, psum[t.bank][:, j * P:], ACT.Abs))
                m = ch.n
                for j in range(TT):
                    w = stick_tmp[:, j, j * P:]
                    ch.wait(m - TT + 1 + j)
                    ch.mark(act.activation(w, w, ACT.Exp, scale=-1.0))
                m = ch.n
                for j in range(TT):
                    w = stick_tmp[:, j, j * P:]
                    ch.wait(m - TT + 1 + j)
                    act.activation(w, w, ACT.Ln, bias=1.0).then_inc(zabs_ready, 1)

            logs(0)
            for h in range(SH):
                if h + 1 < SH:
                    logs(h + 1)
                for j, t in enumerate(stick[h]["sum"]):
                    full(act, t)
                    if h >= 2:
                        full(act, stick[h - 2]["out"])
                    act.activation(attn_f[:, TT * (h % 2) + j, j * P:], psum[t.bank][:, j * P:],
                                   ACT.Exp).then_inc(bank_out[t.bank], 1)
            branch_out(out_tiles[1], post[1])
            upd[0] += 1
            norm_scale(mlps[1]["norm"], X, residual)
            mlp(1)
            upd[0] += 1

            log_exp_table()
            act.wait_ge(lb_exp, 1)
            act.activation(lb[:], lb[:], ACT.Exp).then_inc(lb_exp, 1)
            norm_scale(norms[3], X, residual)
            for j in range(DT // 2):
                for h in range(2):
                    t = glu_tiles[4 * j + 2 + h]
                    if j:
                        have(act, glu_tiles[4 * (j - 1) + h])
                    full(act, t)
                    act.activation(sqb[:, h, :], psum[t.bank][:], ACT.Sigmoid).then_inc(bank_out[t.bank], 1)
            for k, t in enumerate(zf_tiles):
                take(t, hb_f[:, k, :], ACT.Sigmoid)
            for k, t in enumerate(zq_tiles):
                take(t, hq_f[:, k, :])
            for k, t in enumerate(zi_tiles):
                take(t, hv_f[:, k, :])
            act.wait_ge(conv2_ready, DT)
            for k, t in enumerate(zgb_tiles):
                take(t, yb_f[:, k, :], ACT.Sigmoid)
            full(act, ln_mean)
            act.activation(rstd[:, 1, :], psum[ln_mean.bank][:], ACT.Copy, scale=1.0 / D).then_inc(bank_out[ln_mean.bank], 1)
            log_exp_table()
            norm_scale(ln_var, Y, lambda eng, k: eng.wait_ge(centered, k + 1))
            act.wait_ge(forget_ready, DT)
            act.activation(hb_f, hb_f, ACT.Ln).then_inc(log_ready, 1)
            for k in range(DT):
                act.wait_ge(scaled, k + 1)
                act.activation(Y[:, k, :], Y[:, k, :], ACT.Silu, scale=vcol("conv_ln_g_2", k),
                               bias=vcol("conv_ln_b_2", k)).then_inc(ln_out, 1)
            log_exp_table()
            act.wait_ge(cum_ready, 1)
            for t in yb_tiles:
                full(act, t)
            for h in range(HH):
                e = hg[h]
                for lv in range(LEVELS):
                    act.wait_ge(h_sub, h * (LEVELS + 1) + lv + 1)
                    act.activation(h_dif[:, lv % 2, :], h_dif[:, lv % 2, :], ACT.Exp).then_inc(h_exp, 1)
                if h:
                    take(hg[h - 1]["o"], hq_f[:, h - 1, :])
                act.wait_ge(h_sub, (h + 1) * (LEVELS + 1))
                act.activation(h_kdec, h_kdec, ACT.Exp)
                if h:
                    have(act, hg[h - 1]["kv"])
                act.activation(h_eb, hb_f[:, h, :], ACT.Exp).then_inc(h_tail, 1)
                if h:
                    full(act, hg[h - 1]["kv"])
                take(e["kturn"], h_kdt)
                take(e["vturn"], hv_f[:, h, :])
                take(zg_tiles[h], Y[:, h, :])
            take(hg[HH - 1]["o"], hq_f[:, HH - 1, :])
            for t in zg_tiles:
                have(act, t)
            act.activation(Y[:, :, :], Y[:, :, :], ACT.Silu).then_inc(gate2_ready, 1)
            for k, t in enumerate(zga_tiles):
                take(t, zga_f[:, k, :], ACT.Sigmoid)
            log_exp_table()
            head_scale(hg_sums, 3 * LH, hq_f, 1.0 / P, lambda i: have(act, hg[i]["o"]))

            norm_scale(norms[4], X, lambda eng, k: have(eng, wo_tiles[k]))
            for i, t in enumerate(pq_tiles):
                take(t, pq_f[:, i, :])
            for i, t in enumerate(key_turn):
                take(t, keys_t[:, 512 * i:512 * (i + 1)])
            for n in range(TT):
                for i in range(2):
                    take(tok_turns[n][i], h_tok[:, n, 512 * i:512 * (i + 1)])
            for n in range(TT):
                if n:
                    act.wait_ge(id_ready, n)
                for i, t in enumerate(peer_scores[n]):
                    take(t, score_s[:, 512 * i:512 * (i + 1)])
                act.wait_ge(soft_in, n + 1)
                act.activation(gates[n % 2], gates[n % 2], ACT.Exp).then_inc(soft_out, 1)
                act.wait_ge(act_in, n + 1)
                act.activation(expert_w[:], expert_w[:], ACT.Gelu).then_inc(act_out, 1)
            log_exp_table()
            norm_scale(norms[5], X, lambda eng, k: eng.wait_ge(x_ready, 4 * DT + 1))
            for n in range(TT):
                take(out_turn[n][0], h_tok[:, n, 0:512])

        @block.vector
        def _(dve):
            ch = Chain(dve, dve_chain)
            nrm = [0]
            upd = [0]

            def take(t, dst, width=SEQ, rows=slice(0, P)):
                full(dve, t)
                dve.tensor_copy(dst, psum[t.bank][rows, 0:width]).then_inc(bank_out[t.bank], 1)

            def normalize(src, dst, gain, width=SEQ):
                nrm[0] += 1
                dve.wait_ge(rstd_ready, nrm[0])
                for k in range(DT):
                    dve.scalar_tensor_tensor(dst[:, k, :], src[:, k, :], gain(k), rstd[:, 0, 0:width], ALU.mult,
                                             ALU.mult).then_inc(norm_out, 1)

            def add_branch(gain):
                nrm[0] += 1
                dve.wait_ge(rstd_ready, nrm[0])
                marks = []
                for k in range(DT + 1):
                    if k < DT:
                        marks.append(ch.mark(dve.scalar_tensor_tensor(Y[:, k, :], Y[:, k, :], gain(k), rstd[:, 0, :],
                                                                      ALU.mult, ALU.mult)))
                    if k:
                        ch.wait(marks[k - 1])
                        dve.tensor_tensor(X[:, k - 1, :], X[:, k - 1, :], Y[:, k - 1, :], ALU.add).then_inc(x_ready, 1)

            def cross_attention(l):
                c = cross[l]
                for x in range(XH):
                    for b in range(2):
                        t = c["sc"][x][b]
                        full(dve, t)
                        ch.link(dve.tensor_reduce(soft[:, 2, 2 * b:2 * b + 2],
                                                  psum[t.bank][:].rearrange("p (n m) -> p n m", m=NMEM), AX_X, ALU.max))
                        dve.tensor_scalar(soft[:, 0, 2 * b:2 * b + 2], soft[:, 2, 2 * b:2 * b + 2], -XD ** -0.5, None,
                                          ALU.mult).then_inc(neg_max, 1)
                    for t in c["sc"][x]:
                        have(dve, t)
                    ch.link(dve.reciprocal(soft[:, 3, :], soft[:, 1, :]))
                    dve.tensor_tensor(prob, prob, bc_last(soft[:, 3, :], NMEM), ALU.mult).then_inc(prob_ready, 1)
                    take(c["turn"][x][1], prob_t[:, 1, :])
                    r = slice((x % 2) * XD, (x % 2) * XD + XD)
                    take(c["out"][x], H[r, MT + x // 2, :], rows=r)

            dve.wait_ge(s_const, 1)
            for k in range(DT):
                take(x_turn[k], X[:, k, :])
            for j, t in enumerate(vec_turn):
                r = min(P, VN - j * P)
                take(t, vec[:, j * P:j * P + r], width=r)
            for k in range(DT):
                take(mem_turn[k], mem_f[:, k, :], width=NMEM)
            normalize(mem_f, mem_n, lambda k: vcol("mem_norm", k), NMEM)
            full(dve, ada_tile)
            dve.tensor_tensor(ada[:].rearrange("p a k -> p (a k)"), psum[ada_tile.bank][:, 0:ADA_N],
                              vec[:, voff["ada_b_2"]:voff["ada_b_2"] + ADA_N], ALU.add).then_inc(bank_out[ada_tile.bank], 1)

            dve.memset(conv_pad[:, :, 0:CONV_A - 1], 0.0)
            normalize(X, H, lambda k: vcol("norm_pre_mix", k))
            qkv = [q_f[:, i, :] for i in range(LH)] + [k_f[:, i, :] for i in range(LH)] + [v_f[:, i, :] for i in range(LH)]
            for i, t in enumerate(qkv_tiles):
                have(dve, t)
                src = conv_pad[:, i % 4, :]
                ch.link(dve.tensor_scalar(qkv[i], src[:, 0:SEQ], vcol("conv_w_a", i), None, ALU.mult))
                for j in range(1, CONV_A):
                    m = dve.scalar_tensor_tensor(qkv[i], src[:, j:j + SEQ], vcol("conv_w_a", j * 3 * LH + i), qkv[i],
                                                 ALU.mult, ALU.add)
                    if j < CONV_A - 1:
                        ch.link(m)
                    else:
                        m.then_inc(conv_ready, 1)
            tb, tg = head_tiles
            have(dve, tb)
            full(dve, tg)
            dve.wait_ge(gates_act, 1)
            ch.link(dve.tensor_scalar(gtmp[1], psum[tg.bank][0:LH, :], small6[:, 0:1], 0.0, ALU.add, ALU.max))
            ch.link(dve.tensor_tensor(gtmp[1], gtmp[1], gtmp[0], ALU.add))
            m = dve.tensor_scalar(gtmp[1], gtmp[1], small6[:, 1:2], -1.0, ALU.mult, ALU.mult)
            m.then_inc(bank_out[tg.bank], 1)
            have(dve, tg)
            src, dst = gtmp[1], gtmp[2]
            for lv in range(LEVELS):
                h = 1 << lv
                if lv == LEVELS - 1:
                    dst = gc6
                s3, d3 = chunks(src), chunks(dst)
                ch.mark(dve.tensor_copy(d3[:, :, 0:h], s3[:, :, 0:h]))
                m = dve.tensor_tensor(d3[:, :, h:], s3[:, :, h:], s3[:, :, 0:P - h], ALU.add)
                if lv < LEVELS - 1:
                    ch.link(m)
                else:
                    m.then_inc(gates_ready, 1)
                src, dst = dst, (gtmp[3] if dst is gtmp[2] else gtmp[2])
            for i in range(2 * LH):
                dve.wait_ge(hr_ready, i + 1)
                v = arena[:, i * SEQ:(i + 1) * SEQ]
                dve.scalar_tensor_tensor(v, v, P ** -0.5 if i < LH else 1.0, rstd[:, i % 2, :], ALU.mult,
                                         ALU.mult).then_inc(hn_out, 1)
            full(dve, tok_turn)
            dve.tensor_copy(tok[:, 0:2, :].rearrange("p a c -> p (a c)"), psum[tok_turn.bank][:, 0:2 * TT * LH]).then_inc(
                bank_out[tok_turn.bank], 1)
            dve.wait_ge(tok_exp, 1)
            ch.link(dve.tensor_tensor(tok[:, 2, :], tok[:, 2, :], tok[:, 0, :], ALU.mult))
            cross_attention(0)
            for g, d in enumerate(delta):
                heads = range(g * GH, (g + 1) * GH)
                for j, h in enumerate(heads):
                    gb, kk, qk, bb = d["prep"][j]
                    dve.wait_ge(eg_ready, h + 1)
                    if j == 0 and g:
                        for t in delta[g - 1]["u"] + delta[g - 1]["w"]:
                            full(dve, t)
                    for n in range(TT):
                        dve.tensor_scalar(blk(U_t[j], n), blk(psum[gb.bank], n), gc_tok[:, n, h:h + 1], 0.0, ALU.subtract,
                                          ALU.min)
                    dve.tensor_tensor(kdec_tok[:, h, :], psum[gb.bank][:, P - 1::P], gc_tok[:, :, h],
                                      ALU.subtract).then_inc(bank_out[gb.bank], 1)
                    dve.tensor_copy(chunk_decay[:, h, :], T_t[j][:, P - 1::P])
                    full(dve, qk)
                    dve.tensor_tensor(q_f[:, h, :], q_f[:, h, :], T_t[j], ALU.mult).then_inc(qdec_ready, 1)
                    dve.wait_ge(dexp_ready, h + 1)
                    ch.link(dve.tensor_tensor(chunks(U_t[j]), chunks(U_t[j]), bc_mid(causal[:], TT), ALU.mult))
                    dve.tensor_tensor(intra_f[:, h, :], psum[qk.bank][:], U_t[j], ALU.mult).then_inc(bank_out[qk.bank], 1)
                    full(dve, kk)
                    dve.tensor_tensor(L_t[j], psum[kk.bank][:], U_t[j], ALU.mult).then_inc(bank_out[kk.bank], 1)
                    have(dve, kk)
                    full(dve, bb)
                    dve.tensor_tensor(L_t[j], L_t[j], psum[bb.bank][:], ALU.mult).then_inc(bank_out[bb.bank], 1)
                eye = bc_mid(ident[:], TT)
                for j in range(GH):
                    dve.wait_ge(lvl_ready, (g * LEVELS) * GH + j + 1)
                    dve.tensor_tensor(chunks(U_t[j]), eye, chunks(B_t[j]), ALU.subtract).then_inc(unit_ready, 1)
                    t = d["X"][0][j]
                    full(dve, t)
                    dve.tensor_tensor(chunks(T_t[j]), eye, chunks(psum[t.bank]), ALU.subtract).then_inc(bank_out[t.bank], 1)
                for lv in range(1, LEVELS):
                    for j in range(GH):
                        if lv < LEVELS - 1:
                            t = d["TX"][lv][j]
                            full(dve, d["UX"][lv][j])
                            dve.tensor_tensor(T_t[j], T_t[j], psum[t.bank][:], ALU.subtract).then_inc(bank_out[t.bank], 1)
                        t = d["UX"][lv][j]
                        full(dve, t)
                        dve.tensor_tensor(U_t[j], U_t[j], psum[t.bank][:], ALU.subtract).then_inc(bank_out[t.bank], 1)
                for j, h in enumerate(heads):
                    t = d["kturn"][j]
                    full(dve, t)
                    dve.tensor_tensor(chunks(B_t[j]), chunks(psum[t.bank]), bc_last(bg_tok[:, :, h], P), ALU.mult)
                    dve.tensor_tensor(chunks(kdec_f[:, h, :]), chunks(psum[t.bank]), bc_last(kdec_tok[:, h, :], P),
                                      ALU.mult).then_inc(bank_out[t.bank], 1)
                    t = d["vturn"][j]
                    full(dve, t)
                    dve.tensor_tensor(chunks(L_t[j]), chunks(psum[t.bank]), bc_last(beta_tok[:, :, h], P),
                                      ALU.mult).then_inc(bank_out[t.bank], 1)
                for j, h in enumerate(heads):
                    take(d["w"][j], k_f[:, h, :])
            for n, st in enumerate(scan):
                for g in range(2):
                    if n:
                        t = st["ws"][g]
                        full(dve, t)
                        v = v_f[:, g * GH:(g + 1) * GH, n * P:(n + 1) * P]
                        dve.tensor_tensor(v, v, psum[t.bank][:, 0:GH * P].rearrange("p (h e) -> p h e", e=P),
                                          ALU.subtract).then_inc(bank_out[t.bank], 1)
                if n < TT - 1:
                    for g in range(2):
                        t = st["sd"][g]
                        full(dve, t)
                        for j in range(GH):
                            h = g * GH + j
                            if n:
                                m = dve.scalar_tensor_tensor(state[:, h, :], state[:, h, :], chunk_decay[:, h, n:n + 1],
                                                             blk(psum[t.bank], j), ALU.mult, ALU.add)
                            else:
                                m = dve.tensor_copy(state[:, h, :], blk(psum[t.bank], j))
                        m.then_inc(bank_out[t.bank], 1)
            for h in range(LH):
                dve.wait_ge(hr_ready, 2 * LH + h + 1)
                dve.scalar_tensor_tensor(q_f[:, h, :], q_f[:, h, :], vcol("onorm_a", 0), rstd[:, h % 2, :], ALU.mult,
                                         ALU.mult).then_inc(hn_out, 1)
                dve.wait_ge(hn_out, 2 * LH + h + 1)
                dve.tensor_tensor(H[:, h, :], q_f[:, h, :], gate_f[:, h, :], ALU.mult).then_inc(mix_ready, 1)
            add_branch(lambda k: vcol("norm_post_mix", k))
            normalize(X, H, lambda k: vcol("norm_pre_mlp", k))
            add_branch(lambda k: vcol("norm_post_mlp", k))

            normalize(X, H, lambda k: vcol("norm_pre_mix", DT + k))
            cross_attention(1)

            def softplus(h):
                for j, t in enumerate(stick[h]["z"]):
                    dve.wait_ge(zabs_ready, TT * h + j + 1)
                    if h >= 2:
                        full(dve, stick[h - 2]["sum"][TT - 1])
                    dst = soft_f[:, TT * (h % 2) + j, j * P:]
                    dve.scalar_tensor_tensor(dst, psum[t.bank][:, j * P:], 0.0, stick_tmp[:, j, j * P:], ALU.max,
                                             ALU.add).then_inc(bank_out[t.bank], 1)
                for j, t in enumerate(stick[h]["z"]):
                    d = soft_f[:, TT * (h % 2) + j, j * P:(j + 1) * P]
                    have(dve, t)
                    dve.tensor_tensor(d, d, strict[:], ALU.mult).then_inc(soft_ready, 1)

            softplus(0)
            for h in range(SH):
                if h + 1 < SH:
                    softplus(h + 1)
                for j, t in enumerate(stick[h]["sum"]):
                    have(dve, t)
                    d = attn_f[:, TT * (h % 2) + j, j * P:(j + 1) * P]
                    dve.copy_predicated(d, not_before[:].bitcast(U32), zeros[:]).then_inc(attn_ready, 1)
                r = slice((h % 2) * SD, (h % 2) * SD + SD)
                take(stick[h]["out"], H[r, h // 2, :], rows=r)
            add_branch(lambda k: vcol("norm_post_mix", DT + k))
            normalize(X, H, lambda k: vcol("norm_pre_mlp", DT + k))
            add_branch(lambda k: vcol("norm_post_mlp", DT + k))

            l0 = voff["lb_logits_2"]
            ch.link(dve.tensor_tensor(lb[:, 0, :], vec[:, l0:l0 + DT], vec[:, l0 + DT:l0 + 2 * DT], ALU.max))
            ch.link(dve.tensor_tensor(lb[:, 1, :], vec[:, l0 + DT:l0 + 2 * DT], lb[:, 0, :], ALU.subtract))
            dve.tensor_tensor(lb[:, 0, :], vec[:, l0:l0 + DT], lb[:, 0, :], ALU.subtract).then_inc(lb_exp, 1)
            for i, name in enumerate(("norm1_g_2", "norm2_g_2")):
                c0 = voff[name]
                ch.link(dve.scalar_tensor_tensor(mod_gain[:, i, :], ada[:, 1 + 3 * i, :], 1.0, vec[:, c0:c0 + DT],
                                                 ALU.add, ALU.mult))

            def modulate(i):
                nrm[0] += 1
                dve.wait_ge(rstd_ready, nrm[0])
                marks = []
                for k in range(DT + 1):
                    if k < DT:
                        marks.append(ch.mark(dve.scalar_tensor_tensor(H[:, k, :], X[:, k, :], mod_gain[:, i, k:k + 1],
                                                                      rstd[:, 0, :], ALU.mult, ALU.mult)))
                    if k:
                        ch.wait(marks[k - 1])
                        dve.tensor_scalar(H[:, k - 1, :], H[:, k - 1, :], ada[:, 3 * i, k - 1:k], None,
                                          ALU.add).then_inc(norm_out, 1)

            modulate(0)
            dve.wait_ge(lb_exp, 2)
            ch.link(dve.tensor_tensor(lb[:, 1, :], lb[:, 0, :], lb[:, 1, :], ALU.add))
            ch.link(dve.reciprocal(lb[:, 1, :], lb[:, 1, :]))
            ch.link(dve.tensor_tensor(lb[:, 0, :], lb[:, 0, :], lb[:, 1, :], ALU.mult))
            ch.link(dve.tensor_scalar(lb[:, 1, :], lb[:, 0, :], -1.0, 1.0, ALU.mult, ALU.add))
            ch.link(dve.memset(glu[:, :, 0:PAD], 0.0))
            for j in range(DT // 2):
                for h in range(2):
                    t = glu_tiles[4 * j + h]
                    have(dve, glu_tiles[4 * j + 2 + h])
                    full(dve, t)
                    dve.tensor_tensor(glu[:, 2 * j + h, PAD:], psum[t.bank][:], sqb[:, h, :], ALU.mult).then_inc(
                        bank_out[t.bank], 1)
            for k in range(0, DT, 2):
                for kk in (k, k + 1):
                    have(dve, glu_tiles[4 * (kk // 2) + kk % 2])
                m2 = [ch.mark(dve.tensor_scalar(Y[:, kk, :], glu[:, kk, 0:SEQ], vcol("conv_w_2", kk), vcol("conv_b_2", kk),
                                                ALU.mult, ALU.add)) for kk in (k, k + 1)]
                for j in range(1, CONV_B):
                    for s_, kk in enumerate((k, k + 1)):
                        ch.wait(m2[s_])
                        m = dve.scalar_tensor_tensor(Y[:, kk, :], glu[:, kk, j:j + SEQ], vcol("conv_w_2", j * DT + kk),
                                                     Y[:, kk, :], ALU.mult, ALU.add)
                        if j < CONV_B - 1:
                            m2[s_] = ch.mark(m)
                        else:
                            m.then_inc(conv2_ready, 1)
            fm = []
            for k, t in enumerate(zf_tiles):
                have(dve, t)
                dve.tensor_scalar(hb_f[:, k, :], hb_f[:, k, :], lb[:, 1, k:k + 1], lb[:, 0, k:k + 1], ALU.mult,
                                  ALU.add).then_inc(forget_ready, 1)
            for k in range(DT):
                dve.wait_ge(forget_ready, k + 1)
                fm.append(ch.mark(dve.tensor_scalar(hk_f[:, k, :], hb_f[:, k, :], -1.0, 1.0, ALU.mult, ALU.add)))
            have(dve, ln_mean)
            for k in range(DT):
                dve.tensor_tensor(Y[:, k, :], Y[:, k, :], rstd[:, 1, :], ALU.subtract).then_inc(centered, 1)
            nrm[0] += 1
            dve.wait_ge(rstd_ready, nrm[0])
            for k in range(DT):
                dve.tensor_tensor(Y[:, k, :], Y[:, k, :], rstd[:, 0, :], ALU.mult).then_inc(scaled, 1)
            dve.wait_ge(log_ready, 1)
            b4 = hb_f.rearrange("p t (n c) -> p (t n) c", c=P)
            f4 = hs_f.rearrange("p t (n c) -> p (t n) c", c=P)
            src, dst = b4, f4
            for lv in range(LEVELS + 1):
                h = 1 << lv
                if lv == LEVELS:
                    dve.tensor_copy(dst, src).then_inc(cum_ready, 1)
                    break
                ch.mark(dve.tensor_copy(dst[:, :, 0:h], src[:, :, 0:h]))
                ch.link(dve.tensor_tensor(dst[:, :, h:], src[:, :, h:], src[:, :, 0:P - h], ALU.add))
                src, dst = dst, src
            dve.wait_ge(cum_ready, 1)
            for k, t in enumerate(yb_tiles):
                full(dve, t)
                have(dve, zgb_tiles[k])
                dve.tensor_tensor(yb_f[:, k, :], psum[t.bank][:], yb_f[:, k, :], ALU.mult).then_inc(bank_out[t.bank], 1)

            def chunk_states(h):
                t = hg[h]["kv"]
                full(dve, t)
                if h:
                    full(dve, hg[h - 1]["o"])
                ch.link(dve.tensor_copy(blk(h_state, 0), blk(psum[t.bank], 0)))
                for n in range(1, TT - 1):
                    m = dve.scalar_tensor_tensor(blk(h_state, n), blk(h_state, n - 1), h_eb[:, n * P + P - 1:n * P + P],
                                                 blk(psum[t.bank], n), ALU.mult, ALU.add)
                    if n < TT - 2:
                        ch.link(m)
                    else:
                        m.then_inc(bank_out[t.bank], 1)

            for h in range(HH):
                e = hg[h]
                t = e["diag"]
                full(dve, t)
                score = h_score[:, h % 2, :]
                if h >= 2:
                    full(dve, hg[h - 2]["o"])
                dve.tensor_tensor(chunks(score), chunks(psum[t.bank]), bc_mid(ident[:], TT), ALU.mult).then_inc(
                    bank_out[t.bank], 1)

                def pairs(lv):
                    half = 1 << lv
                    r = h * LEVELS + lv
                    if lv >= 2:
                        full(dve, e["lv"][lv - 2])
                    elif h:
                        full(dve, hg[h - 1]["lv"][LEVELS - 2 + lv])
                    dve.wait_ge(h_exp, r + 1)
                    v = [x.rearrange("p (n w) -> p n w", w=2 * half) for x in
                         (h_pair[:, lv % 2, :], h_dif[:, lv % 2, :], hk_f[:, h, :], hq_f[:, h, :])]
                    dve.tensor_tensor(v[0][:, :, 0:half], v[2][:, :, 0:half], v[1][:, :, 0:half], ALU.mult)
                    dve.tensor_tensor(v[0][:, :, half:], v[3][:, :, half:], v[1][:, :, half:], ALU.mult).then_inc(h_pairs, 1)

                pairs(0)
                for lv in range(LEVELS):
                    if lv + 1 < LEVELS:
                        pairs(lv + 1)
                    if lv == 1 and h:
                        chunk_states(h - 1)
                    tl = e["lv"][lv]
                    full(dve, tl)
                    have(dve, e["lv"][lv - 1] if lv else e["diag"])
                    dve.copy_predicated(chunks(score), bc_mid(level_mask[:, lv, :].bitcast(U32), TT),
                                        chunks(psum[tl.bank])).then_inc(bank_out[tl.bank], 1)
                dve.wait_ge(h_tail, h + 1)
                dve.tensor_tensor(h_kdec, h_kdec, hk_f[:, h, :], ALU.mult).then_inc(h_kd, 1)
                dve.tensor_tensor(hq_f[:, h, :], hq_f[:, h, :], h_eb, ALU.mult).then_inc(h_qd, 1)
            chunk_states(HH - 1)
            dve.wait_ge(gate2_ready, 1)
            for h in range(HH):
                dve.wait_ge(hr_ready, 3 * LH + h + 1)
                dve.scalar_tensor_tensor(hq_f[:, h, :], hq_f[:, h, :], vcol("hg_norm_g_2", h), rstd[:, h % 2, :], ALU.mult,
                                         ALU.mult).then_inc(hn_out, 1)
                dve.wait_ge(hn_out, 3 * LH + h + 1)
                dve.tensor_tensor(hq_f[:, h, :], hq_f[:, h, :], Y[:, h, :], ALU.mult).then_inc(mix_ready, 1)
            for k, t in enumerate(ya_tiles):
                full(dve, t)
                have(dve, zga_tiles[k])
                dve.tensor_tensor(merged_f[:, k, :], psum[t.bank][:], zga_f[:, k, :], ALU.mult).then_inc(bank_out[t.bank], 1)
                have(dve, t)
                dve.tensor_tensor(merged_f[:, k, :], merged_f[:, k, :], yb_f[:, k, :], ALU.add).then_inc(merged, 1)
            for k, t in enumerate(wo_tiles):
                full(dve, t)
                dve.scalar_tensor_tensor(X[:, k, :], psum[t.bank][:], ada[:, 2, k:k + 1], X[:, k, :], ALU.mult,
                                         ALU.add).then_inc(bank_out[t.bank], 1)

            modulate(1)

            def search(n):
                for t in peer_scores[n]:
                    have(dve, t)
                s3, w3 = [x.rearrange("p (i c) -> p i c", c=P) for x in (score_s, work_a)]

                def best16(groups, val, idx, src, left):
                    for lo in (0, 8):
                        cur = src if lo == 0 else left
                        for i in range(groups):
                            ch.mark(dve.max(val[:, i, lo:lo + 8], cur[:, i, :]))
                        m = ch.n
                        for i in range(groups):
                            ch.wait(m - groups + 1 + i)
                            ch.mark(dve.max_index(idx[:, i, lo:lo + 8], val[:, i, lo:lo + 8], cur[:, i, :]))
                            if lo == 0:
                                ch.mark(dve.match_replace(left[:, i, :], val[:, i, lo:lo + 8], cur[:, i, :], -3.0e38))
                        ch.wait(ch.n)

                best16(HP, top_v, top_i, s3, w3)
                ch.link(dve.tensor_copy(top_f, top_i))
                pair = top_v.rearrange("p (h s) k -> p h s k", s=2)
                full4 = [P, PH, TOPK, TOPK]
                sums = work_b.rearrange("p (h x y) -> p h x y", x=TOPK, y=TOPK)
                ch.link(dve.tensor_tensor(sums, pair[:, :, 0, :].unsqueeze(3).to_broadcast(full4),
                                          pair[:, :, 1, :].unsqueeze(2).to_broadcast(full4), ALU.add))
                c3, l3 = [x.rearrange("p (h c) -> p h c", c=TOPK * TOPK) for x in (work_b, work_a)]
                best16(PH, best, pos_u, c3, l3)
                pos2 = pos_u.rearrange("p h k -> p (h k)")
                ids = top_f.rearrange("p (h s) k -> p h s k", s=2)
                for side, dst in ((0, e_first), (1, e_second)):
                    ch.link(dve.tensor_scalar(part_u, pos2, 4 if side == 0 else 15, None,
                                              ALU.logical_shift_right if side == 0 else ALU.bitwise_and))
                    ch.link(dve.tensor_copy(part_f, part_u))
                    hit = work_b.rearrange("p (e x) -> p e x", x=TOPK)
                    ch.link(dve.tensor_tensor(hit, bc_mid(iota16[:], NE), bc_last(part_f, TOPK), ALU.is_equal))
                    hit4 = work_b.rearrange("p (h k x) -> p h k x", k=TOPK, x=TOPK)
                    ch.link(dve.tensor_tensor(hit4, hit4, ids[:, :, side, :].unsqueeze(2).to_broadcast(full4), ALU.mult))
                    ch.link(dve.tensor_reduce(dst, hit, AX_X, ALU.add))
                ch.link(dve.scalar_tensor_tensor(e_first, e_first, float(NKEY), e_second, ALU.mult, ALU.add))
                dve.tensor_copy(experts[n % 2], e_first).then_inc(id_ready, 1)
                g3 = gates[n % 2].rearrange("p (h k) -> p h k", k=TOPK)
                dve.tensor_tensor(g3, best, best[:, :, 0:1].to_broadcast([P, PH, TOPK]), ALU.subtract).then_inc(soft_in, 1)
                dve.wait_ge(soft_out, n + 1)
                ch.link(dve.tensor_reduce(gate_sum[:, 0, :], g3, AX_X, ALU.add))
                ch.link(dve.reciprocal(gate_sum[:, 1, :], gate_sum[:, 0, :]))
                ch.link(dve.tensor_tensor(g3, g3, bc_last(gate_sum[:, 1, :], TOPK), ALU.mult))

            for t in tok_turns[0] + tok_turns[1] + tok_turns[2] + tok_turns[3]:
                have(dve, t)
            search(0)
            dve.sem_inc(row_free, GATHER)
            phase = 0
            for n in range(TT):
                with dve.Fori(0, PH // 2) as i:
                    for half in range(2):
                        for k in range(TOPK):
                            dve.wait_ge(row_landed[k], i * 32 + 16 * (phase * PH + half + 1))
                            dve.tensor_tensor_reduce(rows[:, k, :], rows[:, k, :], h_tok[:, n, :], 1.0, 0.0, ALU.mult, ALU.add,
                                                     dots[:, half, k:k + 1]).then_inc(row_free, 1)
                        dve.wait_ge(row_free, i * (2 * TOPK) + (GATHER + phase * NE + (half + 1) * TOPK))
                        dve.tensor_scalar(expert_w[:, bass.ds(i * (2 * TOPK) + half * TOPK, TOPK)], dots[:, half, :], 1.0, None,
                                          ALU.mult).then_inc(dots_taken, 1)
                phase += 1
                dve.wait_ge(dots_taken, PH * (n + 1))
                dve.sem_inc(act_in, 1)
                if n + 1 < TT:
                    search(n + 1)
                dve.wait_ge(act_out, n + 1)
                ch.link(dve.tensor_tensor(expert_w[:], expert_w[:], gates[n % 2], ALU.mult))
                if n:
                    for t in peer_back[n - 1]:
                        have(dve, t)
                ch.link(dve.memset(y_acc[:, 0:2, :], 0.0))
                with dve.Fori(0, PH // 2) as i:
                    for half in range(2):
                        dve.tensor_scalar(dots[:, half, :], expert_w[:, bass.ds(i * (2 * TOPK) + half * TOPK, TOPK)], 1.0, None,
                                          ALU.mult).then_inc(w_copied, 1)
                        for k in range(TOPK):
                            if k == 0:
                                dve.wait_ge(w_copied, i * 2 + (n * PH + half + 1))
                            dve.wait_ge(row_free, i * (2 * TOPK) + (GATHER + phase * NE + half * TOPK + k - 1))
                            dve.wait_ge(row_landed[k], i * 32 + 16 * (phase * PH + half + 1))
                            dve.scalar_tensor_tensor(y_acc[:, k % 2, :], rows[:, k, :], dots[:, half, k:k + 1],
                                                     y_acc[:, k % 2, :], ALU.mult, ALU.add).then_inc(row_free, 1)
                phase += 1
                dve.wait_ge(row_free, GATHER + phase * NE)
                dve.tensor_tensor(y_acc[:, 0, :], y_acc[:, 0, :], y_acc[:, 1, :], ALU.add).then_inc(y_ready, 1)
                for i, t in enumerate(peer_back[n]):
                    full(dve, t)
                    for j in range(4):
                        k = 4 * i + j
                        m = dve.scalar_tensor_tensor(blk(X[:, k, :], n), blk(psum[t.bank], j), ada[:, 5, k:k + 1],
                                                     blk(X[:, k, :], n), ALU.mult, ALU.add)
                    m.then_inc(bank_out[t.bank], 1)
            for t in peer_back[TT - 1]:
                have(dve, t)
            dve.sem_inc(x_ready, 1)
            normalize(X, H, lambda k: vcol("final_g_2", k))
            for n in range(TT):
                take(out_turn[n][1], h_tok[:, n, 512:1024])


_INS = ["x", "mem", "mem_norm", "norm_pre_mix", "norm_post_mix", "norm_pre_mlp", "norm_post_mlp", "w_in_a", "conv_w_a",
        "a_log_a", "dt_bias_a", "onorm_a", "w_in_b", "w_mem_kv", "w_out", "w_up", "w_down", "c_2", "ada_w_2", "ada_b_2",
        "norm1_g_2", "w_in_2", "lb_logits_2", "hg_norm_g_2", "w_a_2", "conv_w_2", "conv_b_2", "conv_ln_g_2",
        "conv_ln_b_2", "w_b_2", "w_out_2", "norm2_g_2", "peer_wq_2", "peer_keys_2", "peer_u_2", "peer_v_2", "final_g_2"]


def kernel(**inputs):
    import numpy as np
    import concourse.bacc as bacc
    from concourse.bass_utils import run_bass_kernel_spmd as run

    nc = bacc.Bacc("TRN2", target_bir_lowering=False, num_devices=1)
    arrays, aps = {}, {}
    for name in _INS:
        arr = np.ascontiguousarray(inputs[name])
        arrays["in_" + name] = arr
        aps[name] = nc.dram_tensor("in_" + name, arr.shape, F32, kind="ExternalInput").ap()
    out = nc.dram_tensor("out", (1, SEQ, D), F32, kind="ExternalOutput").ap()
    build(nc, aps, out)
    return run(nc, [arrays], core_ids=[0]).results[0]["out"]
```

```python
from contextlib import ExitStack

import concourse.bass as bass
from concourse import mybir

F32 = mybir.dt.float32
F32R = mybir.dt.float32r
U32 = mybir.dt.uint32
ALU = mybir.AluOpType
ACT = mybir.ActivationFunctionType
AX_X = mybir.AxisListType.X

P = 128
SEQ = 512
D = 1024
DT = D // P
TT = SEQ // P
DEPTH = 2
XW = D // 4
XT = XW // P
XH = 4
XD = XW // XH
MW = D - XW
MT = MW // P
LH = MW // P
SH = MW // 64
SD = 64
CONV_A = 4
NMEM = 256
FF = 4 * D
FT = FF // P
EPS = 1e-6
LEVELS = 7
HH = 8
CONV_B = 31
PH = 8
NKEY = 128
TOPK = 16
HP = 2 * PH
RING = 4
UNIT_K = 8
UNIT_N = 256
QUARTERS = 4
QT = FF // P // QUARTERS
HALVES = 4
GATHER = 16


class Tile:

    def __init__(self, sem, n, bank, use):
        self.sem, self.n, self.bank, self.use = sem, n, bank, use


class Unit:

    def __init__(self, u, src, cols, slot, load, before):
        self.u, self.src, self.cols = u, src, cols
        self.slot, self.load, self.before = slot, load, before
        self.then = None


def build(nc, a, out):
    ctx = ExitStack()
    with ctx:
        def sb(name, shape, dt=F32):
            return ctx.enter_context(nc.sbuf_tensor(name, shape, dt))

        def sem(name):
            return ctx.enter_context(nc.semaphore(name))

        ring = sb("weight_ring", [P, RING, UNIT_K * UNIT_N])
        X = sb("residual", [P, DT, SEQ])
        with nc.sbuf_tensor("split_normed", [P, DT, SEQ], F32R) as split_H:
            pass
        H = sb("normed", [P, DT, SEQ])
        with nc.sbuf_tensor("split_branch", [P, DT, SEQ], F32R) as split_Y:
            pass
        Y = sb("branch", [P, DT, SEQ])
        ARENA = 24960
        with nc.sbuf_tensor("split_arena", [P, ARENA], F32R) as split_arena:
            pass
        arena = sb("arena", [P, ARENA])
        ident = sb("ident", [P, P])
        ones = sb("ones", [P, P])
        neg_ones = sb("neg_ones", [P, P])
        neg_tri = sb("neg_tri", [P, P])
        causal = sb("causal", [P, P])
        strict = sb("strict", [P, P])
        not_before = sb("not_before", [P, P])
        zeros = sb("zeros", [P, P])
        level_mask = sb("level_mask", [P, LEVELS, P])
        VROWS = [("mem_norm", 8), ("norm_pre_mix", 16), ("norm_post_mix", 16), ("norm_pre_mlp", 16),
                 ("norm_post_mlp", 16), ("norm1_g_2", 8), ("hg_norm_g_2", 8), ("conv_b_2", 8),
                 ("conv_ln_g_2", 8), ("conv_ln_b_2", 8), ("norm2_g_2", 8), ("final_g_2", 8),
                 ("lb_logits_2", 16), ("ada_b_2", 48), ("c_2", 8), ("onorm_a", 1),
                 ("conv_w_a", 72), ("conv_w_2", 248)]
        VT = (sum(n for _, n in VROWS) + P - 1) // P
        vec = sb("vector_columns", [P, VT * P])
        ada = sb("ada", [P, 6, DT])
        c_col = sb("silu_c", [P, DT])
        lb = sb("lower_bound", [P, 2, DT])
        eps = sb("eps", [P, 1])
        tok = sb("token_scalars", [P, 6, TT * LH])
        memk = sb("mem_keys", [P, DEPTH, XT, NMEM])
        memv = sb("mem_values", [P, DEPTH, 2, XW])
        sqb = sb("squares", [P, 2, SEQ])
        rstd = sb("rstd", [P, 2, SEQ])
        small6 = sb("head_scalars", [LH, 2])
        psum = [ctx.enter_context(nc.psum_tensor(f"bank{i}", [P, 512], F32)) for i in range(8)]

        voff = {}
        at = 0
        for name, n in VROWS:
            voff[name] = at
            at += n
        VN = at

        def vcol(name, i):
            return vec[:, voff[name] + i:voff[name] + i + 1]

        def region(off, tiles, width=SEQ):
            return arena[:, off:off + tiles * width].rearrange("p (t n) -> p t n", n=width)

        landed = [sem(f"weights_landed{i}") for i in range(RING)]
        half_done = sem("half_unit_done")
        psum_full = sem("psum_full")
        bank_out = [sem(f"bank_read{i}") for i in range(8)]
        s_x = sem("x_landed")
        s_mem = sem("mem_landed")
        s_vec = sem("vectors_landed")
        s_const = sem("constants_built")
        act_chain = sem("act_step")
        dve_chain = sem("dve_step")
        pool_chain = sem("pool_step")

        count = {"aux": 0, "unit": 0}
        uses = [0] * 8
        units = []

        def aux(bank):
            count["aux"] += 1
            uses[bank] += 1
            return Tile(psum_full, count["aux"], bank, uses[bank])

        slot_units = [[] for _ in range(RING)]

        def unit(src, cols=UNIT_N, slots=RING):
            held = slot_units[len(units) % slots]
            u = Unit(len(units), src, cols, len(units) % slots, len(held) + 1, held[-1] if held else None)
            held.append(u)
            units.append(u)
            return u

        def half_tile(u, half, bank):
            uses[bank] += 1
            return Tile(half_done, 2 * u.u + half + 1, bank, uses[bank])

        def k_major(w):
            return w.rearrange("(k p) n -> p k n", p=P)

        ADA_N = 6 * D // P
        ada_units, ada_tiles = [], []

        def follow(u):
            j = len(ada_units)
            if j < ADA_N // 2:
                u.then = unit(k_major(a["ada_w_2"][0])[:, :, UNIT_N * j:UNIT_N * (j + 1)])
                u.then.ada, u.then.layer = j, len(ada_tiles)
                ada_units.append(u.then)
            return u

        def close_ada():
            first = ada_tiles[-1].end if ada_tiles else 0
            t = half_tile(ada_units[-1], 1, 5)
            t.first, t.end = first, 2 * len(ada_units)
            ada_tiles.append(t)

        def column_units(w, first, n, ada=False):
            us = []
            for j in range(n):
                us.append(unit(k_major(w)[:, :, first + UNIT_N * j:first + UNIT_N * (j + 1)]))
                if ada:
                    follow(us[-1])
            return us, [half_tile(u, h, (2 * j + h) % 4) for j, u in enumerate(us) for h in range(2)]

        x_turn = [aux(k % 4) for k in range(DT)]
        vec_turn = [aux(4 + j % 4) for j in range(VT)]
        mem_turn = [aux(k % 4) for k in range(DT)]
        norms = [aux(4)]

        kv_units, key_tiles, value_tiles = [], [], []
        for l in range(DEPTH):
            uk = unit(k_major(a["w_mem_kv"][l])[:, :, 0:XW])
            uv = unit(k_major(a["w_mem_kv"][l])[:, :, XW:2 * XW])
            kv_units.append((uk, uv))
            key_tiles.append([half_tile(uk, h, h) for h in range(2)])
            value_tiles.append([half_tile(uv, h, 2 + h) for h in range(2)])

        def plan_cross():
            c = {"sc": [[aux(4), aux(5)]], "turn": [], "out": []}
            for x in range(XH):
                c["turn"].append([aux(6), aux(7)])
                if x + 1 < XH:
                    c["sc"].append([aux(4), aux(5)])
                c["out"].append(aux(x % 2))
            return c

        split_halves = [0]

        def split_units(us):
            for u in us:
                u.split = split_halves[0]
                split_halves[0] += 2

        IN_MLP, IN_ATTN, IN_WIDE, IN_MIXED, IN_MERGED = (0, 2 * DT), DT, 3 * DT, 4 * DT, 5 * DT

        def plan_mlp(l):
            m = {"norm": aux(4), "first": len(units)}
            up, down = k_major(a["w_up"][l]), k_major(a["w_down"][l])
            for q in range(QUARTERS):
                uu = [unit(up[:, :, UNIT_N * (4 * q + j):UNIT_N * (4 * q + j + 1)]) for j in range(4)]
                ut = [half_tile(u, h, (2 * j + h) % 4) for j, u in enumerate(uu) for h in range(2)]
                du = [unit(down[:, QT * q:QT * (q + 1), UNIT_N * j:UNIT_N * (j + 1)]) for j in range(4)]
                dt = [half_tile(u, h, (2 * j + h) % 4) for j, u in enumerate(du) for h in range(2)]
                split_units(uu + du)
                if q == 0:
                    m["units"], m["up_tiles"], m["down_tiles"] = uu + du, ut, dt
            m["post"] = aux(4)
            return m

        norms.append(aux(4))
        wa = a["w_in_a"][0]
        qkv_units, qkv_tiles = column_units(wa, 0, 3 * MW // UNIT_N, ada=True)
        gate_units, gate_tiles = column_units(wa, 3 * MW, MW // UNIT_N, ada=True)
        head_unit = follow(unit(k_major(wa)[:, :, 4 * MW:4 * MW + 2 * LH], 2 * LH))
        head_tiles = [half_tile(head_unit, h, h) for h in range(2)]
        uses_q = follow(unit(k_major(wa)[:, :, 4 * MW + 2 * LH:4 * MW + 2 * LH + XW]))
        memq_units = [[uses_q]]
        memq_tiles = [[half_tile(uses_q, h, 2 + h) for h in range(2)]]
        close_ada()
        l2_sums = [aux(4 + i % 4) for i in range(2 * LH)]
        tok_turn = aux(6)
        cross = [plan_cross()]
        GH = 3
        delta = []
        for g in range(LH // GH):
            d = {"prep": [[aux(4 * (j % 2) + b) for b in range(4)] for j in range(GH)], "X": [], "TX": [], "UX": []}
            for lv in range(LEVELS):
                d["X"].append([aux(2 * j) for j in range(GH)])
                tx, ux = [], []
                for j in range(GH):
                    if lv:
                        if lv < LEVELS - 1:
                            tx.append(aux(2 * j))
                        ux.append(aux(2 * j + 1))
                d["TX"].append(tx)
                d["UX"].append(ux)
            d["kturn"], d["vturn"], d["u"], d["w"] = [], [], [], []
            for j in range(GH):
                d["kturn"].append(aux(2 * j))
                d["vturn"].append(aux(2 * j + 1))
            for j in range(GH):
                d["u"].append(aux(2 * j))
                d["w"].append(aux(2 * j + 1))
            delta.append(d)
        scan = []
        for n in range(TT):
            st = {"ws": [], "o": [], "sd": []}
            if n:
                st["ws"] = [aux(g) for g in range(2)]
            for g in range(2):
                st["o"].append(aux(2 + g))
                if n < TT - 1:
                    st["sd"].append(aux(4 + g))
            scan.append(st)
        o_sums = [aux(4 + h % 4) for h in range(LH)]
        out_units, out_tiles, post = [], [], []

        def plan_out(w):
            u, t = column_units(w, 0, D // UNIT_N)
            out_units.append(u)
            out_tiles.append(t)
            post.append(aux(4))

        plan_out(a["w_out"][0])
        mlps = [plan_mlp(0)]

        norms.append(aux(4))
        wb = a["w_in_b"][0]
        sq_units, sq_tiles = column_units(wb, 0, 2 * MW // UNIT_N, ada=True)
        sv_units = [follow(unit(k_major(wb)[:, :, 2 * MW + UNIT_N * j:2 * MW + UNIT_N * (j + 1)])) for j in range(MW // UNIT_N)]
        sv_tiles = [half_tile(u, h, (2 * j + h) % 4) for j, u in enumerate(sv_units) for h in range(2)]
        ub = follow(unit(k_major(wb)[:, :, 3 * MW:3 * MW + XW]))
        close_ada()
        attn_units = sq_units + [ub]
        split_units(attn_units)
        memq_units.append([ub])
        memq_tiles.append([half_tile(ub, h, 2 + h) for h in range(2)])
        cross.append(plan_cross())
        stick = []
        stick.append({"z": [aux(j) for j in range(TT)]})
        for h in range(SH):
            if h + 1 < SH:
                stick.append({"z": [aux(4 * ((h + 1) % 2) + j) for j in range(TT)]})
            b = 4 * (h % 2)
            stick[h]["sum"] = [aux(b + j) for j in range(TT)]
            stick[h]["out"] = aux(b + 3)
        plan_out(a["w_out"][1])
        mlps.append(plan_mlp(1))

        norms.append(aux(4))
        w2 = a["w_in_2"][0]
        Z_Q, Z_F, Z_I, Z_G, Z_CA, Z_CB, Z_GA, Z_GB = [D * i for i in range(8)]
        glu_units, glu_tiles = [], []
        for j in range(D // UNIT_N):
            for first, b in ((Z_CA, 0), (Z_CB, 2)):
                u = unit(k_major(w2)[:, :, first + UNIT_N * j:first + UNIT_N * (j + 1)])
                glu_units.append(u)
                glu_tiles += [half_tile(u, h, b + h) for h in range(2)]
        zf_units, zf_tiles = column_units(w2, Z_F, D // UNIT_N)
        zq_units, zq_tiles = column_units(w2, Z_Q, D // UNIT_N)
        zi_units, zi_tiles = column_units(w2, Z_I, D // UNIT_N)
        zgb_units, zgb_tiles = column_units(w2, Z_GB, D // UNIT_N)
        wide_units = glu_units + zf_units + zq_units + zi_units + zgb_units
        split_units(wide_units)
        ln_mean, ln_var = aux(5), aux(4)
        yb_units, yb_tiles = column_units(a["w_b_2"][0], 0, D // UNIT_N)
        zg_units, zg_tiles = [], []
        hg = []
        for h in range(HH):
            if h % 2 == 0:
                zg_units.append(unit(k_major(w2)[:, :, Z_G + P * h:Z_G + P * (h + 2)]))
            zg_tiles.append(half_tile(zg_units[-1], h % 2, h % 4))
            e = {"diag": aux(6)}
            if h:
                hg[h - 1]["kv"] = aux(6)
            e["lv"] = [aux(4 + lv % 2) for lv in range(LEVELS)]
            if h:
                hg[h - 1]["o"] = aux(7)
            e["kturn"], e["vturn"] = aux(6), aux(7)
            hg.append(e)
        hg[HH - 1]["kv"], hg[HH - 1]["o"] = aux(6), aux(7)
        zga_units, zga_tiles = column_units(w2, Z_GA, D // UNIT_N)
        hg_sums = [aux(4 + h % 4) for h in range(HH)]
        ya_units, ya_tiles = column_units(a["w_a_2"][0], 0, D // UNIT_N)
        wo_units, wo_tiles = column_units(a["w_out_2"][0], 0, D // UNIT_N)
        split_units(ya_units + wo_units)
        norms.append(aux(4))
        key_turn = [aux(4 + i) for i in range(HP // 4)]
        SG = 2
        pq_units, pq_tiles, tok_turns, peer_scores = [], [], [], [[]]
        wq = k_major(a["peer_wq_2"][0])
        for g in range(PH // SG):
            for j in range(SG * g, SG * (g + 1)):
                pq_units.append(unit(wq[:, :, UNIT_N * j:UNIT_N * (j + 1)], slots=2))
                pq_tiles += [half_tile(pq_units[-1], h, (2 * j + h) % 4) for h in range(2)]
            if g == 0:
                tok_turns = [[aux(2 * (n % 2) + i) for i in range(2)] for n in range(TT)]
            peer_scores[0].append(aux(4 + g))
        peer_scores.append([aux(4 + i) for i in range(HP // 4)])
        peer_back = []
        row_sums = []
        for n in range(TT):
            row_sums.append([aux(i) for i in range(2)])
            peer_back.append([aux(2 + i) for i in range(2)])
            if n + 2 < TT:
                peer_scores.append([aux(4 + i) for i in range(HP // 4)])
        norms.append(aux(4))
        out_turn = [[aux(2 * (n % 2) + i) for i in range(2)] for n in range(TT)]

        q_f = region(0, LH)
        k_f = region(LH * SEQ, LH)
        v_f = region(2 * LH * SEQ, LH)
        gate_f = region(3 * LH * SEQ, LH)
        intra_f = region(4 * LH * SEQ, LH)
        kdec_f = region(5 * LH * SEQ, LH)
        memq_f = region(6 * LH * SEQ, XT)
        A_SMALL = (6 * LH + XT) * SEQ
        beta6 = arena[0:LH, A_SMALL:A_SMALL + SEQ]
        gc6 = arena[0:LH, A_SMALL + SEQ:A_SMALL + 2 * SEQ]
        spare = region(A_SMALL + 2 * SEQ, 8)
        pool512 = [Y[:, i, :] for i in range(8)] + [spare[:, i, :] for i in range(8)]
        L_t, B_t, T_t, U_t, X_t = [[pool512[5 * j + i] for j in range(GH)] for i in range(5)]
        state = Y[:, 0:2, :].rearrange("p a (h e) -> p (a h) e", e=P)
        conv_pad = Y[:, :, :].rearrange("p a n -> p (a n)")[:, 0:4 * (SEQ + CONV_A - 1)].rearrange(
            "p (i n) -> p i n", i=4)
        gtmp = [Y[0:LH, 6, :], Y[0:LH, 7, :], spare[0:LH, 4, :], spare[0:LH, 5, :]]
        prob = spare[:, 0:2, :].rearrange("p a (b m) -> p (a b) m", m=NMEM)
        prob_t = spare[:, 2:4, :]
        beta_tok = tok[:, 0, :].rearrange("p (n h) -> p n h", h=LH)
        gc_tok = tok[:, 1, :].rearrange("p (n h) -> p n h", h=LH)
        bg_tok = tok[:, 2, :].rearrange("p (n h) -> p n h", h=LH)
        kdec_tok = tok[:, 3, :].rearrange("p (h n) -> p h n", n=TT)
        chunk_decay = tok[:, 4, :].rearrange("p (h n) -> p h n", n=TT)
        soft = sb("softmax_rows", [P, 4, TT])
        def split_region(off, tiles, width=SEQ):
            return split_arena[:, off:off + tiles * width].rearrange("p (t n) -> p t n", n=width)

        mlp_w = [split_arena[:, i * HALVES * 1024:(i + 1) * HALVES * 1024].rearrange("p (s n) -> p s n", n=1024) for i in range(2)]
        M_HID = 2 * HALVES * 1024
        hid_hi, hid_lo = [split_region(M_HID + i * QT * SEQ, QT) for i in range(2)]
        in_hi, in_lo = [split_region(M_HID + (2 * QT + i * DT) * SEQ, DT) for i in range(2)]
        branch_sq = region(M_HID + 2 * QT * SEQ, DT)
        sq_f = region(0, MT)
        sk_f = region(MT * SEQ, MT)
        sv_tok = arena[:, 2 * MT * SEQ:(2 * MT + LH) * SEQ].rearrange("p (t w) -> p t w", w=MW)
        S_OFF = 3 * LH * SEQ
        attn_w = [split_arena[:, S_OFF + i * HALVES * 1024:S_OFF + (i + 1) * HALVES * 1024].rearrange(
            "p (s n) -> p s n", n=1024) for i in range(2)]
        attn_lo = in_lo
        soft_f = region(S_OFF, 2 * TT)
        attn_f = region(S_OFF + 2 * TT * SEQ, 2 * TT)
        stick_tmp = Y[:, 0:TT, :]
        memq_of = [memq_f, memq_f]
        vec_rows = arena[:, 0:VT * P].rearrange("p (j c) -> p j c", c=P)
        mem_rows = arena[:, 1024:1024 + 2 * D].rearrange("p (t d) -> p t d", d=D)
        mem_f = region(4096, DT, NMEM)
        mem_n = H[:, :, 0:NMEM]
        mod_part = [x.rearrange("p (b n) -> p b n", n=UNIT_N) for x in (Y[:, 5, :], sqb[:, 0, :])]
        x_rows = Y[:, :, :].rearrange("p a n -> p (a n)").rearrange("p (t d) -> p t d", d=D)

        PAD = CONV_B - 1
        glu = arena[:, 0:DT * (SEQ + PAD)].rearrange("p (t n) -> p t n", n=SEQ + PAD)
        yb_f = region(0, DT)
        A2 = DT * (SEQ + PAD)
        hq_f, hk_f, hb_f, hv_f = [region(A2 + i * DT * SEQ, DT) for i in range(4)]
        F2 = A2 + 4 * DT * SEQ
        hs_f = region(F2, 8)
        h_dif, h_pair, h_score = [hs_f[:, 2 * i:2 * i + 2, :] for i in range(3)]
        h_kdec, h_eb = hs_f[:, 6, :], hs_f[:, 7, :]
        h_kdt, h_state = rstd[:, 0, :], rstd[:, 1, :]
        zga_f = hb_f
        mixed_lo = split_region(A2 + 3 * DT * SEQ, DT)
        merged_hi, merged_lo = split_region(A2, DT), split_region(A2 + DT * SEQ, DT)
        wide_lo = split_region(A2 + DT * SEQ, DT)
        wide_w = [split_arena[:, F2 + i * 2048:F2 + (i + 1) * 2048].rearrange("p (s n) -> p s n", n=1024) for i in range(2)]
        mod_gain = sb("modulated_gain", [P, 2, DT])
        pq_f = region(0, HP)
        key_rows = arena[:, F2:F2 + HP * P].rearrange("p (i d) -> p i d", d=P)
        rows = arena[:, HP * SEQ:HP * SEQ + GATHER * D].rearrange("p (s d) -> p s d", d=D)
        keys_t, score_s = ring[:, 2, :], ring[:, 3, :]
        work_a, work_b = [memk[:, i, :, :].rearrange("p t n -> p (t n)") for i in range(2)]
        h_tok = Y[:, :, :].rearrange("p a n -> p (a n)").rearrange("p (t d) -> p t d", d=D)
        y_acc = H[:, :, :].rearrange("p a n -> p (a n)").rearrange("p (t d) -> p t d", d=D)
        tk = sqb[:, :, :].rearrange("p a n -> p (a n)")
        top_v = tk[:, 0:HP * TOPK].rearrange("p (i k) -> p i k", k=TOPK)
        top_i = tk[:, HP * TOPK:2 * HP * TOPK].bitcast(U32).rearrange("p (i k) -> p i k", k=TOPK)
        top_f = tk[:, 2 * HP * TOPK:3 * HP * TOPK].rearrange("p (i k) -> p i k", k=TOPK)
        NE = PH * TOPK
        best = tk[:, 3 * HP * TOPK:3 * HP * TOPK + NE].rearrange("p (h k) -> p h k", k=TOPK)
        pos_u = tk[:, 3 * HP * TOPK + NE:3 * HP * TOPK + 2 * NE].bitcast(U32).rearrange("p (h k) -> p h k", k=TOPK)
        rs = rstd[:, :, :].rearrange("p a n -> p (a n)")
        part_u, part_f = rs[:, 0:NE].bitcast(U32), rs[:, NE:2 * NE]
        e_first, e_second = rs[:, 2 * NE:3 * NE], rs[:, 3 * NE:4 * NE]
        gates = [rs[:, (4 + i) * NE:(5 + i) * NE] for i in range(2)]
        experts = [rs[:, (6 + i) * NE:(7 + i) * NE].bitcast(U32) for i in range(2)]
        expert_w = sb("expert_weight", [P, NE])
        iota16 = sb("iota16", [P, TOPK])
        iota_i = sb("iota16_int", [P, TOPK], mybir.dt.int32)
        row_ids = sb("row_ids", [P, 2, TOPK], U32)
        dots = sb("dots", [P, TOPK])
        row_w = sb("row_weights", [P, TOPK])
        y_sum = y_acc[:, 2, :]
        diag = y_acc[:, 3, :].rearrange("p (k c) -> p k c", c=P)
        gate_pass = sb("gate_pass", [P, 1])
        gate_sum = sb("gate_sum", [P, 2, PH])

        sq_ready = sem("square_ready")
        sq_used = sem("square_summed")
        rstd_ready = sem("rstd_ready")
        norm_out = sem("normed_ready")
        x_ready = sem("residual_ready")
        conv_ready = sem("conv_ready")
        silu_ready = sem("silu_ready")
        s_small = sem("head_scalars_landed")
        gates_ready = sem("gates_ready")
        hs_ready = sem("head_square_ready")
        hr_ready = sem("head_rstd_ready")
        hn_out = sem("head_norm_ready")
        neg_max = sem("score_max_ready")
        prob_exp = sem("score_exp_ready")
        prob_ready = sem("score_prob_ready")
        cross_out = sem("cross_ready")
        eg_ready = sem("decay_row_ready")
        dexp_ready = sem("decay_ready")
        qdec_ready = sem("decayed_query_ready")
        lvl_ready = sem("level_block_ready")
        unit_ready = sem("first_inverse_ready")
        up_ready = sem("mlp_hidden_ready")
        hid_high = sem("mlp_high_ready")
        relu_ready = sem("mlp_square_ready")
        split_hi = sem("weight_high_ready")
        in_joined = sem("input_joined")
        split_ready = sem("weight_split_ready")
        in_high = sem("input_high_ready")
        in_split = sem("input_split_ready")
        soft_ready = sem("softplus_ready")
        attn_ready = sem("attention_ready")
        zabs_ready = sem("score_log_ready")
        mix_ready = sem("mix_ready")
        stored = sem("output_stored")
        ada_ready = sem("ada_ready")
        mod_scaled = sem("modulation_block_scaled")
        mod_sum = sem("modulation_block_summed")
        lb_exp = sem("bound_exp_ready")
        sig_ready = sem("conv_gate_ready")
        conv2_ready = sem("wide_conv_ready")
        mean_ready = sem("mean_ready")
        centered = sem("centered_ready")
        scaled = sem("conv_normed_ready")
        ln_out = sem("conv_branch_ready")
        forget_ready = sem("forget_ready")
        log_ready = sem("log_forget_ready")
        cum_ready = sem("cumulated_ready")
        h_sub = sem("level_difference_ready")
        h_exp = sem("level_decay_ready")
        h_pairs = sem("level_pair_ready")
        h_tail = sem("chunk_decay_ready")
        h_kd = sem("decayed_key_ready")
        h_qd = sem("hgrn_query_ready")
        merged = sem("merged_ready")
        gate2_ready = sem("output_gate_ready")
        s_keys = sem("keys_landed")
        id_ready = sem("expert_ids_ready")
        soft_in = sem("gate_logits_ready")
        soft_out = sem("gate_exp_ready")
        row_landed = [sem(f"row_landed{i}") for i in range(GATHER)]
        ids_copied = sem("row_ids_copied")
        pass_done = sem("slots_passed")
        row_free = sem("row_free")
        odd_free = sem("odd_row_free")
        diag_ready = sem("diagonals_ready")
        dots_taken = sem("dots_kept")
        w_copied = sem("expert_weights_copied")
        act_in = sem("expert_dots_ready")
        act_out = sem("expert_gelu_ready")
        y_ready = sem("expert_sum_ready")
        y_taken = sem("expert_sum_taken")
        gates_act = sem("gate_logs_ready")
        tok_exp = sem("token_decay_ready")

        def full(eng, t):
            eng.wait_ge(t.sem, t.n)

        def have(eng, t):
            eng.wait_ge(bank_out[t.bank], t.use)

        def free(pe, t):
            if t.use > 1:
                pe.wait_ge(bank_out[t.bank], t.use - 1)

        pre_mlp = [2, 4]

        class Chain:

            def __init__(self, eng, s):
                self.eng, self.s, self.n = eng, s, 0

            def mark(self, ins):
                self.n += 1
                ins.then_inc(self.s, 1)
                return self.n

            def link(self, ins):
                self.eng.wait_ge(self.s, self.mark(ins))

            def wait(self, n):
                self.eng.wait_ge(self.s, n)

        def bc_mid(ap, n):
            return ap.unsqueeze(1).to_broadcast([ap.shape[0], n, ap.shape[1]])

        def bc_last(ap, n):
            return ap.unsqueeze(2).to_broadcast([ap.shape[0], ap.shape[1], n])

        def chunks(ap):
            return ap.rearrange("p (n c) -> p n c", c=P)

        def f32(ap):
            return ap.bitcast(F32)

        def blk(ap, n):
            return ap[:, n * P:(n + 1) * P]

        def raw(u):
            return ring[:, u.slot, :].rearrange("p (k n) -> p k n", n=UNIT_N)

        row_src = {
            "mem_norm": a["mem_norm"].rearrange("(k p) -> k p", p=P),
            "c_2": a["c_2"].rearrange("o (k p) -> (o k) p", p=P),
            "onorm_a": a["onorm_a"], "final_g_2": a["final_g_2"].rearrange("(k p) -> k p", p=P),
            "conv_w_a": a["conv_w_a"].rearrange("o j (k p) -> (o j k) p", p=P),
            "conv_w_2": a["conv_w_2"].rearrange("o j (k p) -> (o j k) p", p=P),
        }
        for name, _ in VROWS:
            if name not in row_src:
                row_src[name] = a[name].rearrange("l (k p) -> (l k) p", p=P)
        row_parts = []
        for name, n in VROWS:
            r = 0
            while r < n:
                j, p0 = divmod(voff[name] + r, P)
                m = min(n - r, P - p0)
                row_parts.append((vec_rows[p0:p0 + m, j, :], row_src[name][r:r + m, :]))
                r += m

        block = ctx.enter_context(nc.Block())

        @block.sync
        def _(sp):
            sp.dma_start(x_rows, a["x"].rearrange("o (t p) d -> p (o t) d", p=P)).then_inc(s_x, 16)
            sp.dma_start(mem_rows, a["mem"].rearrange("o (t p) d -> p (o t) d", p=P)).then_inc(s_mem, 16)

            def load(u):
                if u.before:
                    sp.wait_ge(half_done, 2 * (u.before.u + 1))
                sp.dma_start(ring[:, u.slot, 0:u.src.shape[1] * u.cols].rearrange("p (k n) -> p k n", n=u.cols),
                             u.src).then_inc(landed[u.slot], 16)

            def load_mlp(l):
                up, down = k_major(a["w_up"][l]), k_major(a["w_down"][l])
                with sp.Fori(0, QUARTERS) as i:
                    for j, u in enumerate(mlps[l]["units"]):
                        src = (up[:, :, bass.ds(i * (4 * UNIT_N) + j * UNIT_N, UNIT_N)] if j < 4 else
                               down[:, bass.ds(i * QT, QT), (j - 4) * UNIT_N:(j - 3) * UNIT_N])
                        sp.wait_ge(half_done, i * 16 + 2 * (u.before.u + 1))
                        sp.dma_start(ring[:, u.slot, :].rearrange("p (k n) -> p k n", n=UNIT_N),
                                     src).then_inc(landed[u.slot], 16)

            for u in units[:mlps[0]["first"]]:
                load(u)
            load_mlp(0)
            for u in units[mlps[0]["first"] + 8 * QUARTERS:mlps[1]["first"]]:
                load(u)
            load_mlp(1)
            for u in units[mlps[1]["first"] + 8 * QUARTERS:pq_units[0].u]:
                load(u)
            for t in wo_tiles:
                have(sp, t)
            sp.dma_start(key_rows, a["peer_keys_2"].rearrange("o h s n d -> n (o h s) d")).then_inc(s_keys, 16)
            for u in pq_units:
                load(u)
            for n in range(TT):
                have(sp, out_turn[n][0])
                have(sp, out_turn[n][1])
                sp.dma_start(out[0, n * P:(n + 1) * P, :], h_tok[:, n, :]).then_inc(stored, 16)
            sp.wait_ge(stored, 16 * TT)

        @block.gpsimd
        def _(pool):
            ch = Chain(pool, pool_chain)
            for t, v in ((ident, 0.0), (ones, 1.0), (neg_ones, -1.0), (neg_tri, -1.0), (causal, 1.0), (strict, 1.0),
                         (not_before, 1.0), (zeros, 0.0), (eps, EPS)):
                pool.memset(t[:], v)
            ch.link(pool.memset(level_mask[:], 0.0))

            def select(t, pattern, op, base, cm, fill):
                return pool.affine_select(out=t, in_=t, pattern=pattern, compare_op=op, fill=fill, base=base,
                                          channel_multiplier=cm)

            select(ident[:], [[-1, P]], ALU.not_equal, 0, 1, 1.0)
            select(neg_tri[:], [[-1, P]], ALU.is_ge, 0, 1, 0.0)
            select(causal[:], [[1, P]], ALU.is_ge, 0, -1, 0.0)
            select(strict[:], [[1, P]], ALU.is_gt, 0, -1, 0.0)
            ch.link(select(not_before[:], [[-1, P]], ALU.is_ge, 0, 1, 0.0))
            for lv in range(LEVELS):
                h = 1 << lv
                v = level_mask[:, lv, :].rearrange("p (b two h) -> p b two h", two=2, h=h)[:, :, 1, :]
                ch.link(pool.memset(v, 1.0))
                ch.link(select(v, [[-2 * h, P // (2 * h)], [0, h]], ALU.is_ge, 0, 1, 0.0))
                ch.link(select(v, [[2 * h, P // (2 * h)], [0, h]], ALU.is_ge, h - 1, -1, 0.0))
            ch.link(pool.iota(iota_i[:], [[1, TOPK]], base=0, channel_multiplier=0))
            pool.tensor_copy(iota16[:], iota_i[:]).then_inc(s_const, 1)
            pool.wait_ge(ada_ready, 1)
            for u in ada_units:
                if u.layer == 0:
                    pool.wait_ge(landed[u.slot], 16 * u.load)
                    pool.tensor_tensor(raw(u), raw(u), bc_last(c_col[:], UNIT_N), ALU.mult).then_inc(mod_scaled, 1)
            for g, d in enumerate(delta):
                for lv in range(LEVELS):
                    for j in range(GH):
                        if lv == 0:
                            have(pool, d["prep"][j][3])
                        else:
                            full(pool, d["X"][lv - 1][j])
                            if lv == 1:
                                pool.wait_ge(unit_ready, g * GH + j + 1)
                        pool.tensor_tensor(chunks(B_t[j]), chunks(L_t[j]), bc_mid(level_mask[:, lv, :], TT),
                                           ALU.mult).then_inc(lvl_ready, 1)

            def split_half(u, h, w, waits, at):
                part = raw(u)[:, :, h * P:(h + 1) * P]
                hi, lo = [x[:, (u.split + h) % w[0].shape[1], :].rearrange("p (k n) -> p k n", n=P) for x in w]
                for s_, v in waits:
                    pool.wait_ge(s_, v)
                pool.tensor_tensor(hi, part, bc_mid(ones[:], DT), ALU.mult).then_inc(split_hi, 1)
                pool.wait_ge(split_hi, at)
                pool.tensor_tensor(lo, part, f32(hi), ALU.subtract).then_inc(split_ready, 1)

            for l in range(DEPTH):
                if l:
                    done = [2 * u.u + h + 1 for u in attn_units for h in range(2)]
                    for i, (u, h) in enumerate((u, h) for u in attn_units for h in range(2)):
                        place = (half_done, done[i - HALVES]) if i >= HALVES else (psum_full, mlps[0]["post"].n)
                        split_half(u, h, attn_w, ((landed[u.slot], 16 * u.load), place), u.split + h + 1)
                with pool.Fori(0, QUARTERS) as i:
                    for u in mlps[l]["units"]:
                        for h in range(2):
                            split_half(u, h, mlp_w, ((landed[u.slot], i * 32 + 16 * u.load),
                                                     (half_done, i * 16 + 2 * u.u + h + 1 - HALVES)),
                                       i * 16 + u.split + h + 1)

            for u in wide_units:
                for h in range(2):
                    split_half(u, h, wide_w, ((landed[u.slot], 16 * u.load), (half_done, 2 * u.u + h - 1)), u.split + h + 1)

            pool.wait_ge(cum_ready, 1)
            for h in range(HH):
                for lv in range(LEVELS):
                    half = 1 << lv
                    b = hb_f[:, h, :].rearrange("p (n w) -> p n w", w=2 * half)
                    dif = h_dif[:, lv % 2, :].rearrange("p (n w) -> p n w", w=2 * half)
                    r = h * LEVELS + lv
                    if lv >= 2 or h:
                        pool.wait_ge(h_pairs, r - 1 if lv >= 2 else h * LEVELS)
                    mid = b[:, :, half - 1:half].to_broadcast([P, SEQ // (2 * half), half])
                    pool.tensor_tensor(dif[:, :, 0:half], mid, b[:, :, 0:half], ALU.subtract)
                    pool.tensor_tensor(dif[:, :, half:], b[:, :, half:], mid, ALU.subtract).then_inc(h_sub, 1)
                if h:
                    full(pool, hg[h - 1]["kturn"])
                pool.tensor_tensor(chunks(h_kdec), chunks(hb_f[:, h, :])[:, :, P - 1:P].to_broadcast([P, TT, P]),
                                   chunks(hb_f[:, h, :]), ALU.subtract).then_inc(h_sub, 1)

            for i, u in enumerate(ya_units + wo_units):
                for h in range(2):
                    t = hg[HH - 1]["o"]
                    split_half(u, h, wide_w, ((landed[u.slot], 16 * u.load),
                                              (bank_out[t.bank], t.use) if i == 0 else (half_done, 2 * u.u + h - 1)),
                               u.split + h + 1)

            pool.memset(gate_pass[:], 0.0).then_inc(pass_done, 1)
            phase = 0
            for n in range(TT):
                for table in (a["peer_u_2"][0], a["peer_v_2"][0]):
                    if phase % 2 == 0 and n:
                        pool.wait_ge(odd_free, PH + n * NE // 2)
                    with pool.Fori(0, PH // 2) as i:
                        pool.wait_ge(pass_done, i * 9 + (phase * 36 + 1))
                        pool.wait_ge(id_ready, i + (n * (PH // 2) + 1))
                        pool.tensor_tensor(gate_pass[:], zeros[:, 0:1], zeros[:, 0:1], ALU.add).then_inc(pass_done, 1)
                        for half in range(2):
                            ch2 = pool.tensor_copy(row_ids[:, half, :],
                                                   experts[n % 2][:, bass.ds(i * (2 * TOPK) + half * TOPK, TOPK)])
                            ch2.then_inc(ids_copied, 1)
                            for k in range(TOPK):
                                if k % 4 == 0:
                                    if k == 0:
                                        pool.wait_ge(ids_copied, i * 2 + (phase * PH + half + 1))
                                    pool.wait_ge(row_free, i * (2 * TOPK) + (phase * NE + half * TOPK + k + 4))
                                    if phase % 2:
                                        pool.wait_ge(odd_free, i * TOPK + (n * NE // 2 + half * TOPK // 2 + k // 2 + 2))
                                    pool.wait_ge(pass_done, i * 9 + (phase * 36 + half * 4 + k // 4 + 2))
                                    pool.tensor_tensor(gate_pass[:], zeros[:, 0:1], zeros[:, 0:1], ALU.add).then_inc(
                                        pass_done, 1)
                                pool.indirect_dma_start(rows[:, k, :], None, table,
                                                        bass.IndirectOffsetOnAxis(ap=row_ids[:, half, k:k + 1], axis=0)
                                                        ).then_inc(row_landed[k], 16)
                    phase += 1

        @block.tensor
        def _(pe):
            nrm = [0]

            def norm_sum(t, width=SEQ, sq=None):
                i = nrm[0]
                nrm[0] += 1
                free(pe, t)
                for k in range(DT):
                    pe.wait_ge(sq_ready, DT * i + k + 1)
                    m = pe.matmul(psum[t.bank][:, 0:width], ones[:], sq[:, k, :] if sq is not None else
                                  sqb[:, k % 2, 0:width], start=k == 0, stop=k == DT - 1)
                    if k < DT - 1:
                        m.then_inc(sq_used, 1)
                    else:
                        m.then_inc(psum_full, 1)

            def block_of(u, k, c, n=P):
                return ring[:, u.slot, k * u.cols + c:k * u.cols + c + n]

            def project(us, tiles, rhs, width=SEQ, ready=None):
                for j, u in enumerate(us):
                    pe.wait_ge(landed[u.slot], 16 * u.load)
                    for h in range(2):
                        t = tiles[2 * j + h]
                        free(pe, t)
                        for k in range(DT):
                            if ready and j == 0 and h == 0:
                                ready(k)
                            m = pe.matmul(psum[t.bank][:, 0:width], block_of(u, k, h * P), rhs[:, k, :],
                                          start=k == 0, stop=k == DT - 1)
                        m.then_inc(half_done, 1)
                    modulation(u.then)

            def modulation(u):
                if u is None:
                    return
                t = ada_tiles[u.layer]
                c = 2 * u.ada - t.first
                if c == 0:
                    free(pe, t)
                pe.wait_ge(mod_sum, u.ada + 1)
                for h in range(2):
                    pe.matmul(psum[t.bank][:, c + h:c + h + 1], mod_part[u.layer][:, u.ada % 2, h * P:(h + 1) * P], ones[:, 0:1],
                              start=True, stop=True).then_inc(half_done, 1)

            pre = [0]

            def normed(k):
                pe.wait_ge(norm_out, DT * pre[0] + k + 1)

            def turn(t, parts):
                free(pe, t)
                at = 0
                for src in parts:
                    r, c = src.shape
                    m = pe.transpose(psum[t.bank][0:c, at:at + r], src, ident[0:r, 0:r])
                    at += r
                m.then_inc(psum_full, 1)

            def cross_attention(l):
                c = cross[l]
                q, kk, vv = memq_of[l], memk[:, l], memv[:, l]

                def scores(x):
                    r = slice((x % 2) * XD, (x % 2) * XD + XD)
                    for b in range(2):
                        t = c["sc"][x][b]
                        free(pe, t)
                        for n in range(2):
                            m = pe.matmul(psum[t.bank][:, n * NMEM:(n + 1) * NMEM],
                                          q[r, x // 2, (2 * b + n) * P:(2 * b + n + 1) * P], kk[r, x // 2, :],
                                          start=True, stop=True)
                        m.then_inc(psum_full, 1)

                for t in memq_tiles[l]:
                    have(pe, t)
                scores(0)
                for x in range(XH):
                    pe.wait_ge(prob_ready, XH * l + x + 1)
                    for mt in range(2):
                        turn(c["turn"][x][mt], [prob[:, n, mt * P:(mt + 1) * P] for n in range(TT)])
                    if x + 1 < XH:
                        scores(x + 1)
                    t = c["out"][x]
                    free(pe, t)
                    r0 = (x % 2) * XD
                    for mt in range(2):
                        have(pe, c["turn"][x][mt])
                        m = pe.matmul(psum[t.bank][r0:r0 + XD, :], vv[:, mt, x * XD:(x + 1) * XD], prob_t[:, mt, :],
                                      start=mt == 0, stop=mt == 1)
                    m.then_inc(psum_full, 1)

            def head_sums(tiles, base):
                for i, t in enumerate(tiles):
                    free(pe, t)
                    pe.wait_ge(hs_ready, base + i + 1)
                    pe.matmul(psum[t.bank][:], ones[:], sqb[:, i % 2, :], start=True, stop=True).then_inc(psum_full, 1)

            def split_product(u, h, w, t, a_hi, a_lo, ready):
                hi, lo = [x[:, (u.split + h) % w[0].shape[1], :].rearrange("p (k n) -> p k n", n=P) for x in w]
                for k in range(DT):
                    ready(k)
                    pe.matmul(psum[t.bank][:], hi[:, k, :], a_hi[:, k, :], start=k == 0, stop=False)
                    pe.matmul(psum[t.bank][:], lo[:, k, :], a_hi[:, k, :], start=False, stop=False)
                    m = pe.matmul(psum[t.bank][:], hi[:, k, :], a_lo[:, k, :], start=False, stop=k == DT - 1)
                m.then_inc(half_done, 1)

            def mlp(l):
                m = mlps[l]
                with pe.Fori(0, QUARTERS) as i:
                    for j, u in enumerate(m["units"]):
                        up = j < 4
                        a_hi, a_lo = (in_hi, in_lo) if up else (hid_hi, hid_lo)
                        for h in range(2):
                            t = (m["up_tiles"] if up else m["down_tiles"])[2 * (j % 4) + h]
                            pe.wait_ge(split_ready, i * 16 + u.split + h + 1)
                            pe.wait_ge(bank_out[t.bank], i * 4 + (t.use - 1))

                            def ready(k):
                                if j == 0 and h == 0:
                                    pe.wait_ge(in_split, IN_MLP[l] + k + 1)
                                if j == 4 and h == 0:
                                    pe.wait_ge(up_ready, i * QT + (FT * l + k + 3))

                            split_product(u, h, mlp_w, t, a_hi, a_lo, ready)
                pre[0] += 1
                norm_sum(m["post"], sq=branch_sq)

            pe.wait_ge(s_const, 1)
            pe.wait_ge(s_x, 16)
            for k in range(DT):
                turn(x_turn[k], [x_rows[:, n, k * P:(k + 1) * P] for n in range(TT)])
            pe.wait_ge(s_vec, 16 * len(row_parts))
            for j in range(VT):
                r = min(P, VN - j * P)
                turn(vec_turn[j], [vec_rows[0:r, j, :]])
            pe.wait_ge(s_mem, 16)
            for k in range(DT):
                turn(mem_turn[k], [mem_rows[:, n, k * P:(k + 1) * P] for n in range(2)])
            norm_sum(norms[0], NMEM)
            for l in range(DEPTH):
                uk, uv = kv_units[l]
                project([uk], key_tiles[l], mem_n, NMEM, normed if l == 0 else None)
                pe.wait_ge(landed[uv.slot], 16 * uv.load)
                for n in range(2):
                    t = value_tiles[l][n]
                    free(pe, t)
                    for k in range(DT):
                        m = pe.matmul(psum[t.bank][:, 0:XW], mem_n[:, k, n * P:(n + 1) * P], block_of(uv, k, 0, XW),
                                      start=k == 0, stop=k == DT - 1)
                    m.then_inc(half_done, 1)
            pre[0] += 1
            norm_sum(norms[1])
            project(qkv_units, qkv_tiles, H, ready=normed)
            project(gate_units, gate_tiles, H)
            pe.wait_ge(landed[head_unit.slot], 16 * head_unit.load)
            for h, t in enumerate(head_tiles):
                free(pe, t)
                for k in range(DT):
                    m = pe.matmul(psum[t.bank][0:LH, :], block_of(head_unit, k, h * LH, LH), H[:, k, :], start=k == 0,
                                  stop=k == DT - 1)
                m.then_inc(half_done, 1)
            modulation(head_unit.then)
            project(memq_units[0], memq_tiles[0], H)
            pre[0] += 1
            head_sums(l2_sums, 0)
            pe.wait_ge(gates_ready, 1)
            turn(tok_turn, [blk(beta6, n) for n in range(TT)] + [blk(gc6, n) for n in range(TT)])
            cross_attention(0)
            for g, d in enumerate(delta):
                heads = range(g * GH, (g + 1) * GH)
                for j, h in enumerate(heads):
                    gb, kk, qk, bb = d["prep"][j]
                    free(pe, gb)
                    pe.matmul(psum[gb.bank][:], ident[0:LH, h:h + 1].to_broadcast([LH, P]), gc6, start=True,
                              stop=True).then_inc(psum_full, 1)
                    if j == 0 and g == 0:
                        pe.wait_ge(hn_out, 2 * LH)
                    for t, rhs in ((kk, k_f), (qk, q_f)):
                        free(pe, t)
                        for n in range(TT):
                            m = pe.matmul(blk(psum[t.bank], n), blk(k_f[:, h, :], n), blk(rhs[:, h, :], n), start=True,
                                          stop=True)
                        m.then_inc(psum_full, 1)
                    free(pe, bb)
                    pe.matmul(psum[bb.bank][:], ident[0:LH, h:h + 1].to_broadcast([LH, P]), beta6, start=True,
                              stop=True).then_inc(psum_full, 1)
                for lv in range(LEVELS):
                    for j in range(GH):
                        t = d["X"][lv][j]
                        free(pe, t)
                        pe.wait_ge(lvl_ready, (g * LEVELS + lv) * GH + j + 1)
                        for n in range(TT):
                            m = pe.matmul(blk(psum[t.bank], n), blk(B_t[j], n), blk(T_t[j], n) if lv else ident[:],
                                          start=True, stop=True)
                        m.then_inc(psum_full, 1)
                    if not lv:
                        continue
                    for j in range(GH):
                        t = d["UX"][lv][j]
                        if lv == 1:
                            pe.wait_ge(unit_ready, g * GH + j + 1)
                        free(pe, t)
                        have(pe, d["X"][lv][j])
                        if lv < LEVELS - 1:
                            tx = d["TX"][lv][j]
                            for n in range(TT):
                                m = pe.matmul(blk(psum[tx.bank], n), blk(U_t[j], n), blk(X_t[j], n), start=True, stop=True)
                            m.then_inc(psum_full, 1)
                        for n in range(TT):
                            m = pe.matmul(blk(psum[t.bank], n), blk(X_t[j], n), blk(U_t[j], n), start=True, stop=True)
                        m.then_inc(psum_full, 1)
                for j, h in enumerate(heads):
                    turn(d["kturn"][j], [blk(k_f[:, h, :], n) for n in range(TT)])
                    turn(d["vturn"][j], [blk(v_f[:, h, :], n) for n in range(TT)])
                for j, h in enumerate(heads):
                    t = d["u"][j]
                    free(pe, t)
                    have(pe, d["UX"][LEVELS - 1][j])
                    have(pe, d["vturn"][j])
                    for n in range(TT):
                        m = pe.matmul(blk(psum[t.bank], n), blk(U_t[j], n), blk(L_t[j], n), start=True, stop=True)
                    m.then_inc(psum_full, 1)
                    t = d["w"][j]
                    free(pe, t)
                    have(pe, d["kturn"][j])
                    for n in range(TT):
                        m = pe.matmul(blk(psum[t.bank], n), blk(B_t[j], n), blk(U_t[j], n), start=True, stop=True)
                    m.then_inc(psum_full, 1)
            for t in delta[0]["u"] + delta[0]["w"] + delta[1]["u"] + delta[1]["w"]:
                have(pe, t)
            pe.wait_ge(qdec_ready, LH)
            for n, st in enumerate(scan):
                for g in range(2):
                    if n:
                        t = st["ws"][g]
                        have(pe, scan[n - 1]["sd"][g])
                        free(pe, t)
                        for j in range(GH):
                            h = g * GH + j
                            m = pe.matmul(blk(psum[t.bank], j), blk(k_f[:, h, :], n), state[:, h, :], start=True, stop=True)
                        m.then_inc(psum_full, 1)
                for g in range(2):
                    if n:
                        have(pe, st["ws"][g])
                    t = st["o"][g]
                    free(pe, t)
                    for j in range(GH):
                        h = g * GH + j
                        if n:
                            pe.matmul(blk(psum[t.bank], j), state[:, h, :], blk(q_f[:, h, :], n), start=True, stop=False)
                        m = pe.matmul(blk(psum[t.bank], j), blk(v_f[:, h, :], n), blk(intra_f[:, h, :], n), start=n == 0,
                                      stop=True)
                    m.then_inc(psum_full, 1)
                    if n < TT - 1:
                        t = st["sd"][g]
                        free(pe, t)
                        for j in range(GH):
                            h = g * GH + j
                            m = pe.matmul(blk(psum[t.bank], j), blk(kdec_f[:, h, :], n), blk(v_f[:, h, :], n), start=True,
                                          stop=True)
                        m.then_inc(psum_full, 1)
            head_sums(o_sums, 2 * LH)

            def mixed(l):
                def ready(k):
                    if k < MT:
                        if l == 0:
                            pe.wait_ge(mix_ready, k + 1)
                        else:
                            for h in (2 * k, 2 * k + 1):
                                have(pe, stick[h]["out"])
                    else:
                        for x in (2 * (k - MT), 2 * (k - MT) + 1):
                            have(pe, cross[l]["out"][x])
                return ready

            project(out_units[0], out_tiles[0], H, ready=mixed(0))
            norm_sum(post[0], sq=branch_sq)
            norm_sum(mlps[0]["norm"])
            mlp(0)

            norm_sum(norms[2])
            def attn_project(us, tiles):
                for j, t in enumerate(tiles):
                    u, h = us[j // 2], j % 2
                    pe.wait_ge(split_ready, u.split + h + 1)
                    free(pe, t)
                    split_product(u, h, attn_w, t, split_Y, attn_lo,
                                  lambda k: pe.wait_ge(in_split, IN_ATTN + k + 1) if u is sq_units[0] and h == 0 else None)
                    if h:
                        modulation(u.then)

            attn_project(sq_units, sq_tiles)
            for j, u in enumerate(sv_units):
                pe.wait_ge(landed[u.slot], 16 * u.load)
                for h in range(2):
                    t = sv_tiles[2 * j + h]
                    free(pe, t)
                    for n in range(2):
                        for k in range(DT):
                            m = pe.matmul(psum[t.bank][:, n * UNIT_N:(n + 1) * UNIT_N], blk(H[:, k, :], 2 * h + n),
                                          block_of(u, k, 0, UNIT_N), start=k == 0, stop=k == DT - 1)
                    m.then_inc(half_done, 1)
                modulation(u.then)
            attn_project(memq_units[1], memq_tiles[1])
            pre[0] += 1
            cross_attention(1)

            def stick_scores(h):
                r = slice((h % 2) * SD, (h % 2) * SD + SD)
                for j, t in enumerate(stick[h]["z"]):
                    free(pe, t)
                    pe.matmul(psum[t.bank][:, j * P:], blk(sk_f[r, h // 2, :], j), sq_f[r, h // 2, j * P:], start=True,
                              stop=True, skip_group_check=True).then_inc(psum_full, 1)

            for t in sq_tiles + sv_tiles:
                have(pe, t)
            stick_scores(0)
            for h in range(SH):
                if h + 1 < SH:
                    stick_scores(h + 1)
                sp_h, at_h = soft_f[:, TT * (h % 2):TT * (h % 2) + TT, :], attn_f[:, TT * (h % 2):TT * (h % 2) + TT, :]
                for j, t in enumerate(stick[h]["sum"]):
                    pe.wait_ge(soft_ready, TT * (h + 1))
                    free(pe, t)
                    for i in range(j, TT):
                        m = pe.matmul(psum[t.bank][:, i * P:], neg_tri[:] if i == j else neg_ones[:], sp_h[:, i, i * P:],
                                      start=False, stop=i == TT - 1, skip_group_check=True)
                    m.then_inc(psum_full, 1)
                t = stick[h]["out"]
                free(pe, t)
                pe.wait_ge(attn_ready, TT * (h + 1))
                r0 = (h % 2) * SD
                for j in range(TT):
                    m = pe.matmul(psum[t.bank][r0:r0 + SD, j * P:], sv_tok[:, j, h * SD:(h + 1) * SD], at_h[:, j, j * P:],
                                  start=j == 0, stop=j == TT - 1, skip_group_check=True)
                m.then_inc(psum_full, 1)
            project(out_units[1], out_tiles[1], H, ready=mixed(1))
            norm_sum(post[1], sq=branch_sq)
            norm_sum(mlps[1]["norm"])
            mlp(1)

            norm_sum(norms[3])
            for j, (u, h) in enumerate((u, h) for u in wide_units for h in range(2)):
                t = (glu_tiles + zf_tiles + zq_tiles + zi_tiles + zgb_tiles)[j]
                pe.wait_ge(split_ready, u.split + h + 1)
                free(pe, t)
                split_product(u, h, wide_w, t, split_H, wide_lo,
                              lambda k: pe.wait_ge(in_split, IN_WIDE + k + 1) if j == 0 else None)
            free(pe, ln_mean)
            for k in range(DT):
                pe.wait_ge(conv2_ready, k + 1)
                m = pe.matmul(psum[ln_mean.bank][:], ones[:], Y[:, k, :], start=k == 0, stop=k == DT - 1)
            m.then_inc(psum_full, 1)
            norm_sum(ln_var)
            project(yb_units, yb_tiles, Y, ready=lambda k: pe.wait_ge(ln_out, k + 1))

            def hgrn_kv(h):
                t = hg[h]["kv"]
                free(pe, t)
                have(pe, hg[h]["kturn"])
                have(pe, hg[h]["vturn"])
                for n in range(TT - 1):
                    m = pe.matmul(blk(psum[t.bank], n), blk(h_kdt, n), blk(hv_f[:, h, :], n), start=True, stop=True)
                m.then_inc(psum_full, 1)

            def hgrn_out(h):
                t = hg[h]["o"]
                free(pe, t)
                pe.wait_ge(h_qd, h + 1)
                have(pe, hg[h]["kv"])
                have(pe, hg[h]["lv"][LEVELS - 1])
                for n in range(TT):
                    if n:
                        pe.matmul(blk(psum[t.bank], n), blk(h_state, n - 1), blk(hq_f[:, h, :], n), start=True, stop=False)
                    m = pe.matmul(blk(psum[t.bank], n), blk(hv_f[:, h, :], n), blk(h_score[:, h % 2, :], n), start=n == 0,
                                  stop=True)
                m.then_inc(psum_full, 1)

            for t in zq_tiles + zi_tiles:
                have(pe, t)
            pe.wait_ge(in_joined, DT)
            pe.wait_ge(cum_ready, 1)
            for h in range(HH):
                def gate(k):
                    u, t = zg_units[h // 2], zg_tiles[h]
                    if k == 0:
                        pe.wait_ge(landed[u.slot], 16 * u.load)
                        free(pe, t)
                    m = pe.matmul(psum[t.bank][:], block_of(u, k, (h % 2) * P), H[:, k, :], start=k == 0, stop=k == DT - 1)
                    if k == DT - 1:
                        m.then_inc(half_done, 1)

                t = hg[h]["diag"]
                free(pe, t)
                for n in range(TT):
                    m = pe.matmul(blk(psum[t.bank], n), blk(hk_f[:, h, :], n), blk(hq_f[:, h, :], n), start=True, stop=True)
                m.then_inc(psum_full, 1)
                if h:
                    hgrn_kv(h - 1)
                for lv in range(LEVELS):
                    gate(lv)
                    t = hg[h]["lv"][lv]
                    free(pe, t)
                    pe.wait_ge(h_pairs, h * LEVELS + lv + 1)
                    for n in range(TT):
                        p = blk(h_pair[:, lv % 2, :], n)
                        m = pe.matmul(blk(psum[t.bank], n), p, p, start=True, stop=True)
                    m.then_inc(psum_full, 1)
                gate(DT - 1)
                if h:
                    hgrn_out(h - 1)
                pe.wait_ge(h_kd, h + 1)
                turn(hg[h]["kturn"], [blk(h_kdec, n) for n in range(TT)])
                turn(hg[h]["vturn"], [blk(hv_f[:, h, :], n) for n in range(TT)])
            hgrn_kv(HH - 1)
            hgrn_out(HH - 1)
            project(zga_units, zga_tiles, H)
            pre[0] += 1
            head_sums(hg_sums, 3 * LH)
            for us, tiles, hi, lo, base in ((ya_units, ya_tiles, split_H, mixed_lo, IN_MIXED),
                                            (wo_units, wo_tiles, merged_hi, merged_lo, IN_MERGED)):
                for j, t in enumerate(tiles):
                    u, h = us[j // 2], j % 2
                    pe.wait_ge(split_ready, u.split + h + 1)
                    free(pe, t)
                    split_product(u, h, wide_w, t, hi, lo, lambda k: pe.wait_ge(in_split, base + k + 1) if j == 0 else None)

            norm_sum(norms[4])
            pe.wait_ge(s_keys, 16)
            for i, t in enumerate(key_turn):
                turn(t, [key_rows[:, 4 * i + j, :] for j in range(4)])

            def key_scores(n, i):
                t = peer_scores[n][i]
                free(pe, t)
                for x in pq_tiles[4 * i:4 * i + 4]:
                    have(pe, x)
                for j in range(4):
                    m = pe.matmul(blk(psum[t.bank], j), blk(pq_f[:, 4 * i + j, :], n), blk(keys_t, 4 * i + j), start=True,
                                  stop=True)
                m.then_inc(psum_full, 1)

            for t in key_turn:
                have(pe, t)
            for g in range(PH // SG):
                project(pq_units[SG * g:SG * (g + 1)], pq_tiles[2 * SG * g:2 * SG * (g + 1)], H, ready=normed if g == 0 else None)
                if g == 0:
                    for n in range(TT):
                        for i in range(2):
                            turn(tok_turns[n][i], [blk(H[:, 4 * i + j, :], n) for j in range(4)])
                key_scores(0, g)
            pre[0] += 1
            for i in range(HP // 4):
                key_scores(1, i)
            pe.sem_inc(odd_free, PH)
            for n in range(TT):
                for t in row_sums[n]:
                    free(pe, t)
                    pe.matmul(psum[t.bank][:], zeros[:], level_mask[:, 0:TT, :].rearrange("p l c -> p (l c)"), start=True, stop=False)
                with pe.Fori(0, PH) as i:
                    for k in range(1, TOPK, 2):
                        if k == 1:
                            pe.wait_ge(diag_ready, i + (n * PH + 1))
                        pe.wait_ge(row_landed[k], i * 16 + 16 * ((2 * n + 1) * PH + 1))
                        for t, c in zip(row_sums[n], (0, 512)):
                            m = pe.matmul(psum[t.bank][:], diag[:, k // 2, :], rows[:, k, c:c + 512], start=False, stop=False)
                        m.then_inc(odd_free, 1)
                pe.wait_ge(y_ready, n + 1)
                for t, c in zip(row_sums[n], (0, 512)):
                    pe.matmul(psum[t.bank][:], ident[:], y_acc[:, 0, c:c + 512], start=False, stop=False)
                    pe.matmul(psum[t.bank][:], ident[:], y_acc[:, 1, c:c + 512], start=False, stop=True).then_inc(psum_full, 1)
                for i in range(2):
                    have(pe, row_sums[n][i])
                    turn(peer_back[n][i], [y_sum[:, (4 * i + j) * P:(4 * i + j + 1) * P] for j in range(4)])
                if n + 2 < TT:
                    for i in range(HP // 4):
                        key_scores(n + 2, i)
            norm_sum(norms[5])
            for n in range(TT):
                for i in range(2):
                    for j in range(4):
                        if n == 0:
                            normed(4 * i + j)
                    turn(out_turn[n][i], [blk(H[:, 4 * i + j, :], n) for j in range(4)])

        @block.scalar
        def _(act):
            ch = Chain(act, act_chain)
            for dst, src in row_parts:
                act.dma_start(dst, src).then_inc(s_vec, 16)
            act.dma_start(small6[:, 0:1], a["dt_bias_a"].rearrange("o h -> h o")).then_inc(s_small, 16)
            act.dma_start(small6[:, 1:2], a["a_log_a"].rearrange("o h -> h o")).then_inc(s_small, 16)
            nrm = [0]

            def log_exp_table():
                act.preload_act_table_set("natural_log_exp_and_others")

            def norm_scale(t, src, ready, width=SEQ, scale=1.0 / D, sq=None):
                i = nrm[0]
                nrm[0] += 1
                for k in range(DT):
                    ready(act, k)
                    if k >= 2 and sq is None:
                        act.wait_ge(sq_used, (DT - 1) * i + k - 1)
                    act.activation(sqb[:, k % 2, 0:width] if sq is None else sq[:, k, :], src[:, k, :],
                                   ACT.Square).then_inc(sq_ready, 1)
                full(act, t)
                act.activation(rstd[:, 0, 0:width], psum[t.bank][:, 0:width], ACT.Ln, bias=eps[:, 0:1],
                               scale=scale).then_inc(bank_out[t.bank], 1)
                have(act, t)
                act.activation(rstd[:, 0, 0:width], rstd[:, 0, 0:width], ACT.Exp, scale=-0.5).then_inc(rstd_ready, 1)

            def head_scale(tiles, base, src, scale, ready=None, tail=None):
                def finish(i):
                    t = tiles[i]
                    full(act, t)
                    if i >= 2:
                        act.wait_ge(hn_out, base + i - 1)
                    act.activation(rstd[:, i % 2, :], psum[t.bank][:], ACT.Ln, bias=eps[:, 0:1],
                                   scale=scale).then_inc(bank_out[t.bank], 1)
                    have(act, t)
                    act.activation(rstd[:, i % 2, :], rstd[:, i % 2, :], ACT.Exp, scale=-0.5).then_inc(hr_ready, 1)

                for i in range(len(tiles)):
                    if ready:
                        ready(i)
                    act.activation(sqb[:, i % 2, :], src[:, i, :], ACT.Square).then_inc(hs_ready, 1)
                    if i:
                        finish(i - 1)
                finish(len(tiles) - 1)

            def take(t, dst, func=ACT.Copy, width=SEQ, rows=slice(0, P)):
                full(act, t)
                act.activation(dst, psum[t.bank][rows, 0:width], func).then_inc(bank_out[t.bank], 1)

            def cross_attention(l):
                c = cross[l]
                log_exp_table()
                for x in range(XH):
                    for b in range(2):
                        t = c["sc"][x][b]
                        act.wait_ge(neg_max, 2 * (XH * l + x) + b + 1)
                        for n in range(2):
                            m = act.activation(prob[:, 2 * b + n, :], psum[t.bank][:, n * NMEM:(n + 1) * NMEM], ACT.Exp,
                                               bias=soft[:, 0, 2 * b + n:2 * b + n + 1], scale=XD ** -0.5,
                                               accum_out=soft[:, 1, 2 * b + n:2 * b + n + 1])
                        m.then_inc(bank_out[t.bank], 1)
                    take(c["turn"][x][0], prob_t[:, 0, :])

            def branch_out(tiles, t):
                def ready(eng, k):
                    take(tiles[k], Y[:, k, :])
                    have(act, tiles[k])
                norm_scale(t, Y, ready, sq=branch_sq)

            def mlp(l):
                m = mlps[l]
                for k in range(DT):
                    act.wait_ge(norm_out, DT * pre_mlp[l] + k + 1)
                    act.activation(in_hi[:, k, :], H[:, k, :], ACT.Copy).then_inc(in_high, 1)
                with act.Fori(0, QUARTERS) as i:
                    for j, t in enumerate(m["up_tiles"]):
                        act.wait_ge(up_ready, i * QT + (FT * l + j + 1))
                        act.wait_ge(t.sem, i * 16 + t.n)
                        act.activation(sqb[:, j % 2, :], psum[t.bank][:], ACT.Relu).then_inc(bank_out[t.bank], 1)
                        act.wait_ge(bank_out[t.bank], i * 4 + t.use)
                        act.activation(sqb[:, j % 2, :], sqb[:, j % 2, :], ACT.Square).then_inc(relu_ready, 1)

                def added(eng, k):
                    t = m["down_tiles"][k]
                    eng.wait_ge(bank_out[t.bank], t.use + 4 * (QUARTERS - 1))

                norm_scale(m["post"], Y, added, sq=branch_sq)

            upd = [0]

            def residual(eng, k):
                eng.wait_ge(x_ready, DT * (upd[0] - 1) + k + 1)

            act.wait_ge(s_const, 1)
            log_exp_table()
            norm_scale(norms[0], mem_f, lambda eng, k: have(eng, mem_turn[k]), NMEM)
            have(act, vec_turn[VT - 1])
            for t in vec_turn:
                have(act, t)
            c0 = voff["c_2"]
            act.activation(c_col[:], vec[:, c0:c0 + DT], ACT.Silu).then_inc(ada_ready, 1)
            for l in range(DEPTH):
                for h in range(2):
                    take(key_tiles[l][h], memk[:, l, h, :], width=NMEM)
                for h in range(2):
                    take(value_tiles[l][h], memv[:, l, h, :], width=XW)

            log_exp_table()
            norm_scale(norms[1], X, lambda eng, k: have(eng, x_turn[k]))
            qkv = [q_f[:, i, :] for i in range(LH)] + [k_f[:, i, :] for i in range(LH)] + [v_f[:, i, :] for i in range(LH)]

            def silu(i):
                act.wait_ge(conv_ready, i + 1)
                act.activation(qkv[i], qkv[i], ACT.Silu).then_inc(silu_ready, 1)

            for i, t in enumerate(qkv_tiles):
                if i >= 4:
                    act.wait_ge(conv_ready, i - 3)
                take(t, conv_pad[:, i % 4, CONV_A - 1:])
                if i:
                    silu(i - 1)
            silu(3 * LH - 1)
            for h, t in enumerate(gate_tiles):
                take(t, gate_f[:, h, :], ACT.Silu)
            tb, tg = head_tiles
            take(tb, beta6, ACT.Sigmoid, rows=slice(0, LH))
            act.wait_ge(s_small, 32)
            full(act, tg)
            ch.link(act.activation(gtmp[0], psum[tg.bank][0:LH, :], ACT.Abs, bias=small6[:, 0:1]))
            log_exp_table()
            ch.link(act.activation(small6[:, 1:2], small6[:, 1:2], ACT.Exp))
            ch.link(act.activation(gtmp[0], gtmp[0], ACT.Exp, scale=-1.0))
            act.activation(gtmp[0], gtmp[0], ACT.Ln, bias=1.0).then_inc(gates_act, 1)
            for t, dst in zip(memq_tiles[0], (memq_f[:, 0, :], memq_f[:, 1, :])):
                take(t, dst)
            act.wait_ge(silu_ready, 2 * LH)
            head_scale(l2_sums, 0, arena[:, 0:2 * LH * SEQ].rearrange("p (t n) -> p t n", n=SEQ), 1.0)
            have(act, tok_turn)
            act.activation(tok[:, 2, :], tok[:, 1, :], ACT.Exp).then_inc(tok_exp, 1)
            cross_attention(0)
            have(act, cross[0]["out"][XH - 1])
            for g, d in enumerate(delta):
                for j in range(GH):
                    gb = d["prep"][j][0]
                    full(act, gb)
                    act.activation(T_t[j], psum[gb.bank][:], ACT.Exp).then_inc(eg_ready, 1)
                    have(act, gb)
                    act.activation(kdec_tok[:, g * GH + j, :], kdec_tok[:, g * GH + j, :], ACT.Exp)
                    act.activation(U_t[j], U_t[j], ACT.Exp).then_inc(dexp_ready, 1)
                for lv in range(1, LEVELS):
                    for j in range(GH):
                        take(d["X"][lv][j], X_t[j])
                for j in range(GH):
                    take(d["u"][j], v_f[:, g * GH + j, :])
            for n, st in enumerate(scan):
                for g in range(2):
                    t = st["o"][g]
                    full(act, t)
                    act.activation(q_f[:, g * GH:(g + 1) * GH, n * P:(n + 1) * P], psum[t.bank][:, 0:GH * P].rearrange(
                        "p (h c) -> p h c", c=P), ACT.Copy).then_inc(bank_out[t.bank], 1)
            head_scale(o_sums, 2 * LH, q_f, 1.0 / P, lambda i: have(act, scan[TT - 1]["o"][i // GH]))
            branch_out(out_tiles[0], post[0])
            upd[0] += 1
            norm_scale(mlps[0]["norm"], X, residual)
            mlp(0)
            upd[0] += 1

            norm_scale(norms[2], X, residual)
            for k in range(DT):
                act.wait_ge(norm_out, DT * (pre_mlp[0] + 1) + k + 1)
                act.activation(split_Y[:, k, :], H[:, k, :], ACT.Copy).then_inc(in_high, 1)
            for i, t in enumerate(sq_tiles):
                full(act, t)
                dst, s = (sq_f[:, i, :], SD ** -0.5) if i < MT else (sk_f[:, i - MT, :], 1.0)
                act.activation(dst, psum[t.bank][:], ACT.Copy, scale=s).then_inc(bank_out[t.bank], 1)
            for i, t in enumerate(sv_tiles):
                full(act, t)
                j, h = divmod(i, 2)
                act.activation(sv_tok[:, 2 * h:2 * h + 2, j * UNIT_N:(j + 1) * UNIT_N],
                               psum[t.bank][:].rearrange("p (t w) -> p t w", w=UNIT_N), ACT.Copy).then_inc(bank_out[t.bank], 1)
            for t, dst in zip(memq_tiles[1], (memq_f[:, 0, :], memq_f[:, 1, :])):
                take(t, dst)
            cross_attention(1)

            def logs(h):
                for j, t in enumerate(stick[h]["z"]):
                    full(act, t)
                    if h:
                        act.wait_ge(soft_ready, TT * (h - 1) + j + 1)
                    w = stick_tmp[:, j, j * P:]
                    ch.mark(act.activation(w, psum[t.bank][:, j * P:], ACT.Abs))
                m = ch.n
                for j in range(TT):
                    w = stick_tmp[:, j, j * P:]
                    ch.wait(m - TT + 1 + j)
                    ch.mark(act.activation(w, w, ACT.Exp, scale=-1.0))
                m = ch.n
                for j in range(TT):
                    w = stick_tmp[:, j, j * P:]
                    ch.wait(m - TT + 1 + j)
                    act.activation(w, w, ACT.Ln, bias=1.0).then_inc(zabs_ready, 1)

            logs(0)
            for h in range(SH):
                if h + 1 < SH:
                    logs(h + 1)
                for j, t in enumerate(stick[h]["sum"]):
                    full(act, t)
                    if h >= 2:
                        full(act, stick[h - 2]["out"])
                    act.activation(attn_f[:, TT * (h % 2) + j, j * P:], psum[t.bank][:, j * P:],
                                   ACT.Exp).then_inc(bank_out[t.bank], 1)
            branch_out(out_tiles[1], post[1])
            upd[0] += 1
            norm_scale(mlps[1]["norm"], X, residual)
            mlp(1)
            upd[0] += 1

            log_exp_table()
            act.wait_ge(lb_exp, 1)
            act.activation(lb[:], lb[:], ACT.Exp).then_inc(lb_exp, 1)
            norm_scale(norms[3], X, residual)
            for k in range(DT):
                act.wait_ge(norm_out, DT * (DEPTH * 2 + 1) + k + 1)
                act.activation(split_H[:, k, :], sqb[:, k % 2, :], ACT.Copy).then_inc(in_high, 1)
            for j in range(DT // 2):
                for h in range(2):
                    t = glu_tiles[4 * j + 2 + h]
                    if j:
                        have(act, glu_tiles[4 * (j - 1) + h])
                    full(act, t)
                    act.activation(sqb[:, h, :], psum[t.bank][:], ACT.Sigmoid).then_inc(bank_out[t.bank], 1)
            for k, t in enumerate(zf_tiles):
                take(t, hb_f[:, k, :], ACT.Sigmoid)
            for k, t in enumerate(zq_tiles):
                take(t, hq_f[:, k, :])
            for k, t in enumerate(zi_tiles):
                take(t, hv_f[:, k, :])
            act.wait_ge(conv2_ready, DT)
            for k, t in enumerate(zgb_tiles):
                take(t, yb_f[:, k, :], ACT.Sigmoid)
            full(act, ln_mean)
            act.activation(rstd[:, 1, :], psum[ln_mean.bank][:], ACT.Copy, scale=1.0 / D).then_inc(bank_out[ln_mean.bank], 1)
            log_exp_table()
            norm_scale(ln_var, Y, lambda eng, k: eng.wait_ge(centered, k + 1))
            act.wait_ge(forget_ready, DT)
            act.activation(hb_f, hb_f, ACT.Ln).then_inc(log_ready, 1)
            for k in range(DT):
                act.wait_ge(scaled, k + 1)
                act.activation(Y[:, k, :], Y[:, k, :], ACT.Silu, scale=vcol("conv_ln_g_2", k),
                               bias=vcol("conv_ln_b_2", k)).then_inc(ln_out, 1)
            log_exp_table()
            act.wait_ge(cum_ready, 1)
            for t in yb_tiles:
                full(act, t)
            for h in range(HH):
                e = hg[h]
                for lv in range(LEVELS):
                    act.wait_ge(h_sub, h * (LEVELS + 1) + lv + 1)
                    act.activation(h_dif[:, lv % 2, :], h_dif[:, lv % 2, :], ACT.Exp).then_inc(h_exp, 1)
                if h:
                    take(hg[h - 1]["o"], hq_f[:, h - 1, :])
                act.wait_ge(h_sub, (h + 1) * (LEVELS + 1))
                act.activation(h_kdec, h_kdec, ACT.Exp)
                if h:
                    have(act, hg[h - 1]["kv"])
                act.activation(h_eb, hb_f[:, h, :], ACT.Exp).then_inc(h_tail, 1)
                if h:
                    full(act, hg[h - 1]["kv"])
                take(e["kturn"], h_kdt)
                take(e["vturn"], hv_f[:, h, :])
                take(zg_tiles[h], Y[:, h, :])
            take(hg[HH - 1]["o"], hq_f[:, HH - 1, :])
            for t in zg_tiles:
                have(act, t)
            act.activation(Y[:, :, :], Y[:, :, :], ACT.Silu).then_inc(gate2_ready, 1)
            for k, t in enumerate(zga_tiles):
                take(t, zga_f[:, k, :], ACT.Sigmoid)
            log_exp_table()
            head_scale(hg_sums, 3 * LH, hq_f, 1.0 / P, lambda i: have(act, hg[i]["o"]))
            for h in range(HH):
                act.wait_ge(mix_ready, LH + h + 1)
                act.activation(split_H[:, h, :], hq_f[:, h, :], ACT.Copy).then_inc(in_high, 1)
            for k in range(DT):
                act.wait_ge(merged, k + 1)
                act.activation(merged_hi[:, k, :], sqb[:, k % 2, :], ACT.Copy).then_inc(in_high, 1)

            norm_scale(norms[4], X, lambda eng, k: have(eng, wo_tiles[k]))
            for i, t in enumerate(key_turn):
                take(t, keys_t[:, 512 * i:512 * (i + 1)])
            for g in range(PH // SG):
                for i in range(2 * SG * g, 2 * SG * (g + 1)):
                    take(pq_tiles[i], pq_f[:, i, :])
                if g == 0:
                    for n in range(TT):
                        for i in range(2):
                            take(tok_turns[n][i], h_tok[:, n, 512 * i:512 * (i + 1)])
                take(peer_scores[0][g], score_s[:, 512 * g:512 * (g + 1)])
            for n in range(TT + 1):
                if n:
                    act.wait_ge(soft_in, 4 * n)
                    act.activation(gates[(n - 1) % 2], gates[(n - 1) % 2], ACT.Exp).then_inc(soft_out, 1)
                if 0 < n < TT:
                    act.wait_ge(id_ready, 4 * n)
                    for i, t in enumerate(peer_scores[n]):
                        take(t, score_s[:, 512 * i:512 * (i + 1)])
                if n:
                    act.wait_ge(act_in, n)
                    act.activation(expert_w[:], expert_w[:], ACT.Gelu).then_inc(act_out, 1)
                    for i, t in enumerate(row_sums[n - 1]):
                        take(t, y_sum[:, 512 * i:512 * (i + 1)])
            log_exp_table()
            norm_scale(norms[5], X, lambda eng, k: eng.wait_ge(x_ready, 4 * DT + 1))
            for n in range(TT):
                take(out_turn[n][0], h_tok[:, n, 0:512])

        @block.vector
        def _(dve):
            ch = Chain(dve, dve_chain)
            nrm = [0]
            upd = [0]

            def take(t, dst, width=SEQ, rows=slice(0, P)):
                full(dve, t)
                dve.tensor_copy(dst, psum[t.bank][rows, 0:width]).then_inc(bank_out[t.bank], 1)

            def normalize(src, dst, gain, width=SEQ):
                nrm[0] += 1
                dve.wait_ge(rstd_ready, nrm[0])
                for k in range(DT):
                    dve.scalar_tensor_tensor(dst[:, k, :], src[:, k, :], gain(k), rstd[:, 0, 0:width], ALU.mult,
                                             ALU.mult).then_inc(norm_out, 1)

            def normalize_split(gain, hi, lo, base):
                nrm[0] += 1
                dve.wait_ge(rstd_ready, nrm[0])
                for k in range(DT + 1):
                    if k < DT:
                        dve.scalar_tensor_tensor(H[:, k, :], X[:, k, :], gain(k), rstd[:, 0, :], ALU.mult,
                                                 ALU.mult).then_inc(norm_out, 1)
                    if k:
                        dve.wait_ge(in_high, base + k)
                        dve.tensor_tensor(lo[:, k - 1, :], H[:, k - 1, :], f32(hi[:, k - 1, :]), ALU.subtract).then_inc(
                            in_split, 1)

            def add_branch(gain):
                nrm[0] += 1
                dve.wait_ge(rstd_ready, nrm[0])
                marks = []
                for k in range(DT + 1):
                    if k < DT:
                        marks.append(ch.mark(dve.scalar_tensor_tensor(Y[:, k, :], Y[:, k, :], gain(k), rstd[:, 0, :],
                                                                      ALU.mult, ALU.mult)))
                    if k:
                        ch.wait(marks[k - 1])
                        dve.tensor_tensor(X[:, k - 1, :], X[:, k - 1, :], Y[:, k - 1, :], ALU.add).then_inc(x_ready, 1)

            def sum_modulation(u):
                if u.layer:
                    dve.wait_ge(landed[u.slot], 16 * u.load)
                    dve.tensor_tensor(raw(u), raw(u), bc_last(c_col[:], UNIT_N), ALU.mult).then_inc(mod_scaled, 1)
                dve.wait_ge(mod_scaled, u.ada + 1)
                if u.ada >= 2:
                    dve.wait_ge(half_done, 2 * (ada_units[u.ada - 2].u + 1))
                dve.tensor_reduce(mod_part[u.layer][:, u.ada % 2, :], raw(u).rearrange("p k n -> p n k"), AX_X,
                                  ALU.add).then_inc(mod_sum, 1)

            def keep_modulation(layer):
                t = ada_tiles[layer]
                full(dve, t)
                dve.tensor_tensor(ada[:].rearrange("p a k -> p (a k)")[:, t.first:t.end], psum[t.bank][:, 0:t.end - t.first],
                                  vec[:, voff["ada_b_2"] + t.first:voff["ada_b_2"] + t.end], ALU.add).then_inc(
                    bank_out[t.bank], 1)

            def mlp(l):
                m = mlps[l]
                ch.link(dve.memset(Y[:, :, :], 0.0))
                if l == 0:
                    dve.sem_inc(up_ready, 2)
                with dve.Fori(0, QUARTERS) as i:
                    for j in range(QT):
                        dve.wait_ge(relu_ready, i * QT + (FT * l + j + 1))
                        dve.tensor_copy(hid_hi[:, j, :], sqb[:, j % 2, :]).then_inc(hid_high, 1)
                        dve.wait_ge(hid_high, i * QT + (FT * l + j + 1))
                        dve.tensor_tensor(hid_lo[:, j, :], sqb[:, j % 2, :], f32(hid_hi[:, j, :]),
                                          ALU.subtract).then_inc(up_ready, 1)
                    for k, t in enumerate(m["down_tiles"]):
                        dve.wait_ge(t.sem, i * 16 + t.n)
                        dve.tensor_tensor(Y[:, k, :], Y[:, k, :], psum[t.bank][:], ALU.add).then_inc(bank_out[t.bank], 1)

            def cross_attention(l):
                c = cross[l]
                for x in range(XH):
                    for b in range(2):
                        t = c["sc"][x][b]
                        full(dve, t)
                        ch.link(dve.tensor_reduce(soft[:, 2, 2 * b:2 * b + 2],
                                                  psum[t.bank][:].rearrange("p (n m) -> p n m", m=NMEM), AX_X, ALU.max))
                        dve.tensor_scalar(soft[:, 0, 2 * b:2 * b + 2], soft[:, 2, 2 * b:2 * b + 2], -XD ** -0.5, None,
                                          ALU.mult).then_inc(neg_max, 1)
                    for t in c["sc"][x]:
                        have(dve, t)
                    ch.link(dve.reciprocal(soft[:, 3, :], soft[:, 1, :]))
                    dve.tensor_tensor(prob, prob, bc_last(soft[:, 3, :], NMEM), ALU.mult).then_inc(prob_ready, 1)
                    take(c["turn"][x][1], prob_t[:, 1, :])
                    r = slice((x % 2) * XD, (x % 2) * XD + XD)
                    take(c["out"][x], H[r, MT + x // 2, :], rows=r)

            dve.wait_ge(s_const, 1)
            for k in range(DT):
                take(x_turn[k], X[:, k, :])
            for j, t in enumerate(vec_turn):
                r = min(P, VN - j * P)
                take(t, vec[:, j * P:j * P + r], width=r)
            for k in range(DT):
                take(mem_turn[k], mem_f[:, k, :], width=NMEM)
            normalize(mem_f, mem_n, lambda k: vcol("mem_norm", k), NMEM)

            dve.memset(conv_pad[:, :, 0:CONV_A - 1], 0.0)
            normalize(X, H, lambda k: vcol("norm_pre_mix", k))
            qkv = [q_f[:, i, :] for i in range(LH)] + [k_f[:, i, :] for i in range(LH)] + [v_f[:, i, :] for i in range(LH)]
            for i, t in enumerate(qkv_tiles):
                if i % 2 == 0:
                    sum_modulation(qkv_units[i // 2].then)
                have(dve, t)
                src = conv_pad[:, i % 4, :]
                ch.link(dve.tensor_scalar(qkv[i], src[:, 0:SEQ], vcol("conv_w_a", i), None, ALU.mult))
                for j in range(1, CONV_A):
                    m = dve.scalar_tensor_tensor(qkv[i], src[:, j:j + SEQ], vcol("conv_w_a", j * 3 * LH + i), qkv[i],
                                                 ALU.mult, ALU.add)
                    if j < CONV_A - 1:
                        ch.link(m)
                    else:
                        m.then_inc(conv_ready, 1)
            for u in ada_units[len(qkv_units):]:
                if u.layer == 0:
                    sum_modulation(u)
            keep_modulation(0)
            tb, tg = head_tiles
            have(dve, tb)
            full(dve, tg)
            dve.wait_ge(gates_act, 1)
            ch.link(dve.tensor_scalar(gtmp[1], psum[tg.bank][0:LH, :], small6[:, 0:1], 0.0, ALU.add, ALU.max))
            ch.link(dve.tensor_tensor(gtmp[1], gtmp[1], gtmp[0], ALU.add))
            m = dve.tensor_scalar(gtmp[1], gtmp[1], small6[:, 1:2], -1.0, ALU.mult, ALU.mult)
            m.then_inc(bank_out[tg.bank], 1)
            have(dve, tg)
            src, dst = gtmp[1], gtmp[2]
            for lv in range(LEVELS):
                h = 1 << lv
                if lv == LEVELS - 1:
                    dst = gc6
                s3, d3 = chunks(src), chunks(dst)
                ch.mark(dve.tensor_copy(d3[:, :, 0:h], s3[:, :, 0:h]))
                m = dve.tensor_tensor(d3[:, :, h:], s3[:, :, h:], s3[:, :, 0:P - h], ALU.add)
                if lv < LEVELS - 1:
                    ch.link(m)
                else:
                    m.then_inc(gates_ready, 1)
                src, dst = dst, (gtmp[3] if dst is gtmp[2] else gtmp[2])
            for i in range(2 * LH):
                dve.wait_ge(hr_ready, i + 1)
                v = arena[:, i * SEQ:(i + 1) * SEQ]
                dve.scalar_tensor_tensor(v, v, P ** -0.5 if i < LH else 1.0, rstd[:, i % 2, :], ALU.mult,
                                         ALU.mult).then_inc(hn_out, 1)
            full(dve, tok_turn)
            dve.tensor_copy(tok[:, 0:2, :].rearrange("p a c -> p (a c)"), psum[tok_turn.bank][:, 0:2 * TT * LH]).then_inc(
                bank_out[tok_turn.bank], 1)
            dve.wait_ge(tok_exp, 1)
            ch.link(dve.tensor_tensor(tok[:, 2, :], tok[:, 2, :], tok[:, 0, :], ALU.mult))
            cross_attention(0)
            for g, d in enumerate(delta):
                heads = range(g * GH, (g + 1) * GH)
                for j, h in enumerate(heads):
                    gb, kk, qk, bb = d["prep"][j]
                    dve.wait_ge(eg_ready, h + 1)
                    if j == 0 and g:
                        for t in delta[g - 1]["u"] + delta[g - 1]["w"]:
                            full(dve, t)
                    for n in range(TT):
                        dve.tensor_scalar(blk(U_t[j], n), blk(psum[gb.bank], n), gc_tok[:, n, h:h + 1], 0.0, ALU.subtract,
                                          ALU.min)
                    dve.tensor_tensor(kdec_tok[:, h, :], psum[gb.bank][:, P - 1::P], gc_tok[:, :, h],
                                      ALU.subtract).then_inc(bank_out[gb.bank], 1)
                    dve.tensor_copy(chunk_decay[:, h, :], T_t[j][:, P - 1::P])
                    full(dve, qk)
                    dve.tensor_tensor(q_f[:, h, :], q_f[:, h, :], T_t[j], ALU.mult).then_inc(qdec_ready, 1)
                    dve.wait_ge(dexp_ready, h + 1)
                    ch.link(dve.tensor_tensor(chunks(U_t[j]), chunks(U_t[j]), bc_mid(causal[:], TT), ALU.mult))
                    dve.tensor_tensor(intra_f[:, h, :], psum[qk.bank][:], U_t[j], ALU.mult).then_inc(bank_out[qk.bank], 1)
                    full(dve, kk)
                    dve.tensor_tensor(L_t[j], psum[kk.bank][:], U_t[j], ALU.mult).then_inc(bank_out[kk.bank], 1)
                    have(dve, kk)
                    full(dve, bb)
                    dve.tensor_tensor(L_t[j], L_t[j], psum[bb.bank][:], ALU.mult).then_inc(bank_out[bb.bank], 1)
                eye = bc_mid(ident[:], TT)
                for j in range(GH):
                    dve.wait_ge(lvl_ready, (g * LEVELS) * GH + j + 1)
                    dve.tensor_tensor(chunks(U_t[j]), eye, chunks(B_t[j]), ALU.subtract).then_inc(unit_ready, 1)
                    t = d["X"][0][j]
                    full(dve, t)
                    dve.tensor_tensor(chunks(T_t[j]), eye, chunks(psum[t.bank]), ALU.subtract).then_inc(bank_out[t.bank], 1)
                for lv in range(1, LEVELS):
                    for j in range(GH):
                        if lv < LEVELS - 1:
                            t = d["TX"][lv][j]
                            full(dve, d["UX"][lv][j])
                            dve.tensor_tensor(T_t[j], T_t[j], psum[t.bank][:], ALU.subtract).then_inc(bank_out[t.bank], 1)
                        t = d["UX"][lv][j]
                        full(dve, t)
                        dve.tensor_tensor(U_t[j], U_t[j], psum[t.bank][:], ALU.subtract).then_inc(bank_out[t.bank], 1)
                for j, h in enumerate(heads):
                    t = d["kturn"][j]
                    full(dve, t)
                    dve.tensor_tensor(chunks(B_t[j]), chunks(psum[t.bank]), bc_last(bg_tok[:, :, h], P), ALU.mult)
                    dve.tensor_tensor(chunks(kdec_f[:, h, :]), chunks(psum[t.bank]), bc_last(kdec_tok[:, h, :], P),
                                      ALU.mult).then_inc(bank_out[t.bank], 1)
                    t = d["vturn"][j]
                    full(dve, t)
                    dve.tensor_tensor(chunks(L_t[j]), chunks(psum[t.bank]), bc_last(beta_tok[:, :, h], P),
                                      ALU.mult).then_inc(bank_out[t.bank], 1)
                for j, h in enumerate(heads):
                    take(d["w"][j], k_f[:, h, :])
            for n, st in enumerate(scan):
                for g in range(2):
                    if n:
                        t = st["ws"][g]
                        full(dve, t)
                        v = v_f[:, g * GH:(g + 1) * GH, n * P:(n + 1) * P]
                        dve.tensor_tensor(v, v, psum[t.bank][:, 0:GH * P].rearrange("p (h e) -> p h e", e=P),
                                          ALU.subtract).then_inc(bank_out[t.bank], 1)
                if n < TT - 1:
                    for g in range(2):
                        t = st["sd"][g]
                        full(dve, t)
                        for j in range(GH):
                            h = g * GH + j
                            if n:
                                m = dve.scalar_tensor_tensor(state[:, h, :], state[:, h, :], chunk_decay[:, h, n:n + 1],
                                                             blk(psum[t.bank], j), ALU.mult, ALU.add)
                            else:
                                m = dve.tensor_copy(state[:, h, :], blk(psum[t.bank], j))
                        m.then_inc(bank_out[t.bank], 1)
            for h in range(LH):
                dve.wait_ge(hr_ready, 2 * LH + h + 1)
                dve.scalar_tensor_tensor(q_f[:, h, :], q_f[:, h, :], vcol("onorm_a", 0), rstd[:, h % 2, :], ALU.mult,
                                         ALU.mult).then_inc(hn_out, 1)
                dve.wait_ge(hn_out, 2 * LH + h + 1)
                dve.tensor_tensor(H[:, h, :], q_f[:, h, :], gate_f[:, h, :], ALU.mult).then_inc(mix_ready, 1)
            add_branch(lambda k: vcol("norm_post_mix", k))
            normalize_split(lambda k: vcol("norm_pre_mlp", k), in_hi, in_lo, IN_MLP[0])
            mlp(0)
            add_branch(lambda k: vcol("norm_post_mlp", k))

            normalize_split(lambda k: vcol("norm_pre_mix", DT + k), split_Y, attn_lo, IN_ATTN)
            for u in ada_units:
                if u.layer == 1:
                    sum_modulation(u)
            keep_modulation(1)
            cross_attention(1)

            def softplus(h):
                for j, t in enumerate(stick[h]["z"]):
                    dve.wait_ge(zabs_ready, TT * h + j + 1)
                    if h >= 2:
                        full(dve, stick[h - 2]["sum"][TT - 1])
                    dst = soft_f[:, TT * (h % 2) + j, j * P:]
                    dve.scalar_tensor_tensor(dst, psum[t.bank][:, j * P:], 0.0, stick_tmp[:, j, j * P:], ALU.max,
                                             ALU.add).then_inc(bank_out[t.bank], 1)
                for j, t in enumerate(stick[h]["z"]):
                    d = soft_f[:, TT * (h % 2) + j, j * P:(j + 1) * P]
                    have(dve, t)
                    dve.tensor_tensor(d, d, strict[:], ALU.mult).then_inc(soft_ready, 1)

            softplus(0)
            for h in range(SH):
                if h + 1 < SH:
                    softplus(h + 1)
                for j, t in enumerate(stick[h]["sum"]):
                    have(dve, t)
                    d = attn_f[:, TT * (h % 2) + j, j * P:(j + 1) * P]
                    dve.copy_predicated(d, not_before[:].bitcast(U32), zeros[:]).then_inc(attn_ready, 1)
                r = slice((h % 2) * SD, (h % 2) * SD + SD)
                take(stick[h]["out"], H[r, h // 2, :], rows=r)
            add_branch(lambda k: vcol("norm_post_mix", DT + k))
            normalize_split(lambda k: vcol("norm_pre_mlp", DT + k), in_hi, in_lo, IN_MLP[1])
            mlp(1)
            add_branch(lambda k: vcol("norm_post_mlp", DT + k))

            l0 = voff["lb_logits_2"]
            ch.link(dve.tensor_tensor(lb[:, 0, :], vec[:, l0:l0 + DT], vec[:, l0 + DT:l0 + 2 * DT], ALU.max))
            ch.link(dve.tensor_tensor(lb[:, 1, :], vec[:, l0 + DT:l0 + 2 * DT], lb[:, 0, :], ALU.subtract))
            dve.tensor_tensor(lb[:, 0, :], vec[:, l0:l0 + DT], lb[:, 0, :], ALU.subtract).then_inc(lb_exp, 1)
            for i, name in enumerate(("norm1_g_2", "norm2_g_2")):
                c0 = voff[name]
                ch.link(dve.scalar_tensor_tensor(mod_gain[:, i, :], ada[:, 1 + 3 * i, :], 1.0, vec[:, c0:c0 + DT],
                                                 ALU.add, ALU.mult))

            def modulate(i):
                nrm[0] += 1
                dve.wait_ge(rstd_ready, nrm[0])
                marks = []
                for k in range(DT + 1):
                    if k < DT:
                        marks.append(ch.mark(dve.scalar_tensor_tensor(H[:, k, :], X[:, k, :], mod_gain[:, i, k:k + 1],
                                                                      rstd[:, 0, :], ALU.mult, ALU.mult)))
                    if k:
                        ch.wait(marks[k - 1])
                        dve.tensor_scalar(H[:, k - 1, :], H[:, k - 1, :], ada[:, 3 * i, k - 1:k], None,
                                          ALU.add).then_inc(norm_out, 1)

            nrm[0] += 1
            dve.wait_ge(rstd_ready, nrm[0])
            for k in range(DT + 1):
                if k < DT:
                    if k >= 2:
                        dve.wait_ge(in_split, IN_WIDE + k - 1)
                    m = ch.mark(dve.scalar_tensor_tensor(sqb[:, k % 2, :], X[:, k, :], mod_gain[:, 0, k:k + 1], rstd[:, 0, :],
                                                         ALU.mult, ALU.mult))
                if k:
                    dve.wait_ge(in_high, IN_WIDE + k)
                    dve.tensor_tensor(wide_lo[:, k - 1, :], sqb[:, (k - 1) % 2, :], f32(split_H[:, k - 1, :]),
                                      ALU.subtract).then_inc(in_split, 1)
                if k < DT:
                    ch.wait(m)
                    dve.tensor_scalar(sqb[:, k % 2, :], sqb[:, k % 2, :], ada[:, 0, k:k + 1], None, ALU.add).then_inc(norm_out, 1)
            dve.wait_ge(lb_exp, 2)
            ch.link(dve.tensor_tensor(lb[:, 1, :], lb[:, 0, :], lb[:, 1, :], ALU.add))
            ch.link(dve.reciprocal(lb[:, 1, :], lb[:, 1, :]))
            ch.link(dve.tensor_tensor(lb[:, 0, :], lb[:, 0, :], lb[:, 1, :], ALU.mult))
            ch.link(dve.tensor_scalar(lb[:, 1, :], lb[:, 0, :], -1.0, 1.0, ALU.mult, ALU.add))
            ch.link(dve.memset(glu[:, :, 0:PAD], 0.0))
            for j in range(DT // 2):
                for h in range(2):
                    t = glu_tiles[4 * j + h]
                    have(dve, glu_tiles[4 * j + 2 + h])
                    full(dve, t)
                    dve.tensor_tensor(glu[:, 2 * j + h, PAD:], psum[t.bank][:], sqb[:, h, :], ALU.mult).then_inc(
                        bank_out[t.bank], 1)
            for k in range(0, DT, 2):
                for kk in (k, k + 1):
                    have(dve, glu_tiles[4 * (kk // 2) + kk % 2])
                m2 = [ch.mark(dve.tensor_scalar(Y[:, kk, :], glu[:, kk, 0:SEQ], vcol("conv_w_2", kk), vcol("conv_b_2", kk),
                                                ALU.mult, ALU.add)) for kk in (k, k + 1)]
                for j in range(1, CONV_B):
                    for s_, kk in enumerate((k, k + 1)):
                        ch.wait(m2[s_])
                        m = dve.scalar_tensor_tensor(Y[:, kk, :], glu[:, kk, j:j + SEQ], vcol("conv_w_2", j * DT + kk),
                                                     Y[:, kk, :], ALU.mult, ALU.add)
                        if j < CONV_B - 1:
                            m2[s_] = ch.mark(m)
                        else:
                            m.then_inc(conv2_ready, 1)
            full(dve, zgb_tiles[-1])
            for k in range(DT):
                dve.tensor_tensor(H[:, k, :], f32(split_H[:, k, :]), f32(wide_lo[:, k, :]), ALU.add).then_inc(in_joined, 1)
            dve.wait_ge(in_joined, DT)
            fm = []
            for k, t in enumerate(zf_tiles):
                have(dve, t)
                dve.tensor_scalar(hb_f[:, k, :], hb_f[:, k, :], lb[:, 1, k:k + 1], lb[:, 0, k:k + 1], ALU.mult,
                                  ALU.add).then_inc(forget_ready, 1)
            for k in range(DT):
                dve.wait_ge(forget_ready, k + 1)
                fm.append(ch.mark(dve.tensor_scalar(hk_f[:, k, :], hb_f[:, k, :], -1.0, 1.0, ALU.mult, ALU.add)))
            have(dve, ln_mean)
            for k in range(DT):
                dve.tensor_tensor(Y[:, k, :], Y[:, k, :], rstd[:, 1, :], ALU.subtract).then_inc(centered, 1)
            nrm[0] += 1
            dve.wait_ge(rstd_ready, nrm[0])
            for k in range(DT):
                dve.tensor_tensor(Y[:, k, :], Y[:, k, :], rstd[:, 0, :], ALU.mult).then_inc(scaled, 1)
            dve.wait_ge(log_ready, 1)
            b4 = hb_f.rearrange("p t (n c) -> p (t n) c", c=P)
            f4 = hs_f.rearrange("p t (n c) -> p (t n) c", c=P)
            src, dst = b4, f4
            for lv in range(LEVELS + 1):
                h = 1 << lv
                if lv == LEVELS:
                    dve.tensor_copy(dst, src).then_inc(cum_ready, 1)
                    break
                ch.mark(dve.tensor_copy(dst[:, :, 0:h], src[:, :, 0:h]))
                ch.link(dve.tensor_tensor(dst[:, :, h:], src[:, :, h:], src[:, :, 0:P - h], ALU.add))
                src, dst = dst, src
            dve.wait_ge(cum_ready, 1)
            for k, t in enumerate(yb_tiles):
                full(dve, t)
                have(dve, zgb_tiles[k])
                dve.tensor_tensor(yb_f[:, k, :], psum[t.bank][:], yb_f[:, k, :], ALU.mult).then_inc(bank_out[t.bank], 1)

            def chunk_states(h):
                t = hg[h]["kv"]
                full(dve, t)
                if h:
                    full(dve, hg[h - 1]["o"])
                ch.link(dve.tensor_copy(blk(h_state, 0), blk(psum[t.bank], 0)))
                for n in range(1, TT - 1):
                    m = dve.scalar_tensor_tensor(blk(h_state, n), blk(h_state, n - 1), h_eb[:, n * P + P - 1:n * P + P],
                                                 blk(psum[t.bank], n), ALU.mult, ALU.add)
                    if n < TT - 2:
                        ch.link(m)
                    else:
                        m.then_inc(bank_out[t.bank], 1)

            for h in range(HH):
                e = hg[h]
                t = e["diag"]
                full(dve, t)
                score = h_score[:, h % 2, :]
                if h >= 2:
                    full(dve, hg[h - 2]["o"])
                dve.tensor_tensor(chunks(score), chunks(psum[t.bank]), bc_mid(ident[:], TT), ALU.mult).then_inc(
                    bank_out[t.bank], 1)

                def pairs(lv):
                    half = 1 << lv
                    r = h * LEVELS + lv
                    if lv >= 2:
                        full(dve, e["lv"][lv - 2])
                    elif h:
                        full(dve, hg[h - 1]["lv"][LEVELS - 2 + lv])
                    dve.wait_ge(h_exp, r + 1)
                    v = [x.rearrange("p (n w) -> p n w", w=2 * half) for x in
                         (h_pair[:, lv % 2, :], h_dif[:, lv % 2, :], hk_f[:, h, :], hq_f[:, h, :])]
                    dve.tensor_tensor(v[0][:, :, 0:half], v[2][:, :, 0:half], v[1][:, :, 0:half], ALU.mult)
                    dve.tensor_tensor(v[0][:, :, half:], v[3][:, :, half:], v[1][:, :, half:], ALU.mult).then_inc(h_pairs, 1)

                pairs(0)
                for lv in range(LEVELS):
                    if lv + 1 < LEVELS:
                        pairs(lv + 1)
                    if lv == 1 and h:
                        chunk_states(h - 1)
                    tl = e["lv"][lv]
                    full(dve, tl)
                    have(dve, e["lv"][lv - 1] if lv else e["diag"])
                    dve.copy_predicated(chunks(score), bc_mid(level_mask[:, lv, :].bitcast(U32), TT),
                                        chunks(psum[tl.bank])).then_inc(bank_out[tl.bank], 1)
                dve.wait_ge(h_tail, h + 1)
                dve.tensor_tensor(h_kdec, h_kdec, hk_f[:, h, :], ALU.mult).then_inc(h_kd, 1)
                dve.tensor_tensor(hq_f[:, h, :], hq_f[:, h, :], h_eb, ALU.mult).then_inc(h_qd, 1)
            chunk_states(HH - 1)
            dve.wait_ge(gate2_ready, 1)
            for h in range(HH):
                dve.wait_ge(hr_ready, 3 * LH + h + 1)
                dve.scalar_tensor_tensor(hq_f[:, h, :], hq_f[:, h, :], vcol("hg_norm_g_2", h), rstd[:, h % 2, :], ALU.mult,
                                         ALU.mult).then_inc(hn_out, 1)
                dve.wait_ge(hn_out, 3 * LH + h + 1)
                dve.tensor_tensor(hq_f[:, h, :], hq_f[:, h, :], Y[:, h, :], ALU.mult).then_inc(mix_ready, 1)
            for h in range(HH):
                dve.wait_ge(in_high, IN_MIXED + h + 1)
                dve.tensor_tensor(mixed_lo[:, h, :], hq_f[:, h, :], f32(split_H[:, h, :]), ALU.subtract).then_inc(in_split, 1)

            def merged_rest(k):
                dve.wait_ge(in_high, IN_MERGED + k + 1)
                dve.tensor_tensor(merged_lo[:, k, :], sqb[:, k % 2, :], f32(merged_hi[:, k, :]), ALU.subtract).then_inc(
                    in_split, 1)

            for k, t in enumerate(ya_tiles):
                full(dve, t)
                have(dve, zga_tiles[k])
                if k >= 2:
                    dve.wait_ge(in_split, IN_MERGED + k - 1)
                part = sqb[:, k % 2, :]
                dve.tensor_tensor(part, psum[t.bank][:], zga_f[:, k, :], ALU.mult).then_inc(bank_out[t.bank], 1)
                have(dve, t)
                dve.tensor_tensor(part, part, yb_f[:, k, :], ALU.add).then_inc(merged, 1)
                if k:
                    merged_rest(k - 1)
            merged_rest(DT - 1)
            for k, t in enumerate(wo_tiles):
                full(dve, t)
                dve.scalar_tensor_tensor(X[:, k, :], psum[t.bank][:], ada[:, 2, k:k + 1], X[:, k, :], ALU.mult,
                                         ALU.add).then_inc(bank_out[t.bank], 1)

            modulate(1)

            s3 = score_s.rearrange("p (i c) -> p i c", c=P)
            left_keys = work_a.rearrange("p (i c) -> p i c", c=P)
            left_sums = work_a.rearrange("p (h c) -> p h c", c=TOPK * TOPK)
            sums = work_b

            def best16(groups, val, idx, src, left):
                for lo in (0, 8):
                    cur = src if lo == 0 else left
                    for i in range(groups):
                        ch.mark(dve.max(val[:, i, lo:lo + 8], cur[:, i, :]))
                    m = ch.n
                    for i in range(groups):
                        ch.wait(m - groups + 1 + i)
                        ch.mark(dve.max_index(idx[:, i, lo:lo + 8], val[:, i, lo:lo + 8], cur[:, i, :]))
                        if lo == 0:
                            ch.mark(dve.match_replace(left[:, i, :], val[:, i, lo:lo + 8], cur[:, i, :], -3.0e38))
                    ch.wait(ch.n)

            def search(n, g):
                halves = slice(2 * SG * g, 2 * SG * (g + 1))
                heads = slice(SG * g, SG * (g + 1))
                es = slice(SG * g * TOPK, SG * (g + 1) * TOPK)
                ne = SG * TOPK
                best16(2 * SG, top_v[:, halves, :], top_i[:, halves, :], s3[:, halves, :], left_keys)
                ch.link(dve.tensor_copy(top_f[:, halves, :], top_i[:, halves, :]))
                pair = top_v[:, halves, :].rearrange("p (h s) k -> p h s k", s=2)
                grid = [P, SG, TOPK, TOPK]
                ch.link(dve.tensor_tensor(sums.rearrange("p (h x y) -> p h x y", x=TOPK, y=TOPK),
                                          pair[:, :, 0, :].unsqueeze(3).to_broadcast(grid),
                                          pair[:, :, 1, :].unsqueeze(2).to_broadcast(grid), ALU.add))
                best16(SG, best[:, heads, :], pos_u[:, heads, :], sums.rearrange("p (h c) -> p h c", c=TOPK * TOPK), left_sums)
                pos2 = pos_u[:, heads, :].rearrange("p h k -> p (h k)")
                ids = top_f[:, halves, :].rearrange("p (h s) k -> p h s k", s=2)
                hit = sums.rearrange("p (e x) -> p e x", x=TOPK)
                hit4 = sums.rearrange("p (h k x) -> p h k x", k=TOPK, x=TOPK)
                for side, dst in ((0, e_first), (1, e_second)):
                    ch.link(dve.tensor_scalar(part_u[:, es], pos2, 4 if side == 0 else 15, None,
                                              ALU.logical_shift_right if side == 0 else ALU.bitwise_and))
                    ch.link(dve.tensor_copy(part_f[:, es], part_u[:, es]))
                    ch.link(dve.tensor_tensor(hit, bc_mid(iota16[:], ne), bc_last(part_f[:, es], TOPK), ALU.is_equal))
                    ch.link(dve.tensor_tensor(hit4, hit4, ids[:, :, side, :].unsqueeze(2).to_broadcast(grid), ALU.mult))
                    ch.link(dve.tensor_reduce(dst[:, es], hit, AX_X, ALU.add))
                ch.link(dve.scalar_tensor_tensor(e_first[:, es], e_first[:, es], float(NKEY), e_second[:, es], ALU.mult,
                                                 ALU.add))
                dve.tensor_copy(experts[n % 2][:, es], e_first[:, es]).then_inc(id_ready, 1)
                dve.tensor_tensor(gates[n % 2][:, es].rearrange("p (h k) -> p h k", k=TOPK), best[:, heads, :],
                                  best[:, heads, 0:1].to_broadcast([P, SG, TOPK]), ALU.subtract).then_inc(soft_in, 1)

            for t in tok_turns[0] + tok_turns[1] + tok_turns[2] + tok_turns[3]:
                have(dve, t)
            dve.sem_inc(row_free, GATHER)
            have(dve, peer_scores[0][0])
            search(0, 0)

            def row_dots(n, first, count):
                phase = 2 * n
                with dve.Fori(0, count) as i:
                    dve.wait_ge(dots_taken, i + (n * PH + first + 1))
                    for k in range(TOPK):
                        dve.wait_ge(row_landed[k], i * 16 + 16 * (phase * PH + first + 1))
                        dve.tensor_tensor_reduce(rows[:, k, :], rows[:, k, :], h_tok[:, n, :], 1.0, 0.0, ALU.mult, ALU.add,
                                                 dots[:, k:k + 1]).then_inc(row_free, 1)
                    dve.wait_ge(row_free, i * TOPK + (GATHER + phase * NE + (first + 1) * TOPK))
                    dve.tensor_scalar(expert_w[:, bass.ds(i * TOPK + first * TOPK, TOPK)], dots[:], 1.0, None,
                                      ALU.mult).then_inc(dots_taken, 1)

            dve.sem_inc(dots_taken, 1)
            for n in range(TT):
                if n:
                    row_dots(n, 0, PH)
                else:
                    at = 0
                    for g in range(1, PH // SG):
                        row_dots(n, at, SG * g - 1 - at)
                        at = SG * g - 1
                        have(dve, peer_scores[0][g])
                        search(0, g)
                    row_dots(n, at, PH - at)
                dve.wait_ge(dots_taken, PH * (n + 1) + 1)
                dve.sem_inc(act_in, 1)
                g3 = gates[n % 2].rearrange("p (h k) -> p h k", k=TOPK)
                dve.wait_ge(soft_out, n + 1)
                ch.link(dve.tensor_reduce(gate_sum[:, 0, :], g3, AX_X, ALU.add))
                ch.link(dve.reciprocal(gate_sum[:, 1, :], gate_sum[:, 0, :]))
                ch.link(dve.tensor_tensor(g3, g3, bc_last(gate_sum[:, 1, :], TOPK), ALU.mult))
                if n:
                    for t in row_sums[n - 1]:
                        have(dve, t)
                ch.link(dve.memset(y_acc[:, 0:2, :], 0.0))
                dve.wait_ge(act_out, n + 1)
                ch.link(dve.tensor_tensor(expert_w[:], expert_w[:], gates[n % 2], ALU.mult))
                phase = 2 * n + 1
                for g in range(PH // SG):
                    with dve.Fori(0, SG) as i:
                        at = GATHER + phase * NE + g * SG * TOPK
                        dve.wait_ge(row_free, i * TOPK + at)
                        dve.tensor_scalar(row_w[:], expert_w[:, bass.ds(i * TOPK + g * SG * TOPK, TOPK)], 1.0, None,
                                          ALU.mult).then_inc(w_copied, 1)
                        dve.wait_ge(w_copied, i + (n * PH + g * SG + 1))
                        dve.wait_ge(odd_free, i * (TOPK // 2) + (PH + (n * PH + g * SG) * TOPK // 2))
                        dve.tensor_tensor(diag, bc_mid(ident[:], TOPK // 2),
                                          bc_last(row_w[:].rearrange("p (k two) -> p k two", two=2)[:, :, 1], P),
                                          ALU.mult).then_inc(diag_ready, 1)
                        for k in range(0, TOPK, 2):
                            dve.wait_ge(row_free, i * TOPK + (at + k - 2))
                            dve.wait_ge(row_landed[k], i * 16 + 16 * (phase * PH + g * SG + 1))
                            part = y_acc[:, k // 2 % 2, :]
                            dve.scalar_tensor_tensor(part, rows[:, k, :], row_w[:, k:k + 1], part, ALU.mult, ALU.add).then_inc(
                                row_free, 2)
                    if n + 1 < TT:
                        if g == 0:
                            for t in peer_scores[n + 1]:
                                have(dve, t)
                        search(n + 1, g)
                dve.wait_ge(row_free, GATHER + (phase + 1) * NE)
                dve.sem_inc(y_ready, 1)
                for i, t in enumerate(peer_back[n]):
                    full(dve, t)
                    for j in range(4):
                        k = 4 * i + j
                        m = dve.scalar_tensor_tensor(blk(X[:, k, :], n), blk(psum[t.bank], j), ada[:, 5, k:k + 1],
                                                     blk(X[:, k, :], n), ALU.mult, ALU.add)
                    m.then_inc(bank_out[t.bank], 1)
            for t in peer_back[TT - 1]:
                have(dve, t)
            dve.sem_inc(x_ready, 1)
            normalize(X, H, lambda k: vcol("final_g_2", k))
            for n in range(TT):
                take(out_turn[n][1], h_tok[:, n, 512:1024])


_INS = ["x", "mem", "mem_norm", "norm_pre_mix", "norm_post_mix", "norm_pre_mlp", "norm_post_mlp", "w_in_a", "conv_w_a",
        "a_log_a", "dt_bias_a", "onorm_a", "w_in_b", "w_mem_kv", "w_out", "w_up", "w_down", "c_2", "ada_w_2", "ada_b_2",
        "norm1_g_2", "w_in_2", "lb_logits_2", "hg_norm_g_2", "w_a_2", "conv_w_2", "conv_b_2", "conv_ln_g_2",
        "conv_ln_b_2", "w_b_2", "w_out_2", "norm2_g_2", "peer_wq_2", "peer_keys_2", "peer_u_2", "peer_v_2", "final_g_2"]


def kernel(**inputs):
    import numpy as np
    import concourse.bacc as bacc
    from concourse.bass_utils import run_bass_kernel_spmd as run

    nc = bacc.Bacc("TRN2", target_bir_lowering=False, num_devices=1)
    arrays, aps = {}, {}
    for name in _INS:
        arr = np.ascontiguousarray(inputs[name])
        arrays["in_" + name] = arr
        aps[name] = nc.dram_tensor("in_" + name, arr.shape, F32, kind="ExternalInput").ap()
    out = nc.dram_tensor("out", (1, SEQ, D), F32, kind="ExternalOutput").ap()
    build(nc, aps, out)
    return run(nc, [arrays], core_ids=[0]).results[0]["out"]
```
